# Optimizing a Trainium2 kernel written in Bass

```python
import jax, jax.numpy as jnp
from jax import lax
import numpy as np

D_MODEL = 1024
BATCH = 1
SEQ = 1024
DEPTH = 1

ATTN_HEAD_DIM = 64
ATTN_WIDTH = D_MODEL // 2
ATTN_HEADS = ATTN_WIDTH // ATTN_HEAD_DIM
DILATION_PATTERNS = ((128, 1), (512, 4), (2048, 16))
ATTN_BLOCK = 128
REL_BUCKETS = 32
REL_MAX_DISTANCE = 2048

HGRN_HEAD_DIM = 128
HGRN_WIDTH = D_MODEL - ATTN_WIDTH
HGRN_HEADS = HGRN_WIDTH // HGRN_HEAD_DIM
HGRN_CHUNK = 64

MIX_WIDTH = ATTN_WIDTH + HGRN_WIDTH
IN_SPLITS = (ATTN_WIDTH, 2 * ATTN_WIDTH, 3 * ATTN_WIDTH,
             3 * ATTN_WIDTH + HGRN_WIDTH, 3 * ATTN_WIDTH + 2 * HGRN_WIDTH,
             3 * ATTN_WIDTH + 3 * HGRN_WIDTH)
IN_PROJ_WIDTH = 3 * ATTN_WIDTH + 4 * HGRN_WIDTH

N_EXPERTS = 32
TOP_K = 4
D_EXPERT = D_MODEL
SWIGLU_LIMIT = 7.0
SWIGLU_ALPHA = 1.702
EXPERT_BLOCK = 128
RMS_EPS = 1e-5

kernel_name = 'hybrid_dilated_attn_hgrn2_moe_block'

def rms_norm(x, w):
    xf = x.astype(jnp.float32)
    y = xf * lax.rsqrt(jnp.mean(xf * xf, axis=-1, keepdims=True) + RMS_EPS)
    return (y * w.astype(jnp.float32)).astype(x.dtype)

def t5_causal_bucket(dist):
    n = np.maximum(dist, 0)
    max_exact = REL_BUCKETS // 2
    large = max_exact + (np.log(np.maximum(n, 1) / max_exact)
                         / np.log(REL_MAX_DISTANCE / max_exact)
                         * (REL_BUCKETS - max_exact)).astype(np.int32)
    large = np.minimum(large, REL_BUCKETS - 1)
    return np.where(n < max_exact, n, large).astype(np.int32)

def dilated_window_attention(q, k, v, rel_bias, window, dilation):
    b, h, s, hd = q.shape
    blk = ATTN_BLOCK
    span = window // dilation
    unit = blk * dilation
    s_pad = -(-s // unit) * unit
    n_sub = s_pad // dilation
    nb = n_sub // blk

    def to_blocks(t):
        t = jnp.pad(t, ((0, 0), (0, 0), (0, s_pad - s), (0, 0)))
        t = t.reshape(b, h, n_sub, dilation, hd).transpose(0, 1, 3, 2, 4)
        return t.reshape(b, h, dilation, nb, blk, hd)

    def with_prev(t):
        prev = jnp.pad(t[:, :, :, :-1], ((0, 0), (0, 0), (0, 0), (1, 0), (0, 0), (0, 0)))
        return jnp.concatenate([prev, t], axis=-2)

    qb = to_blocks(q)
    kk = with_prev(to_blocks(k))
    vv = with_prev(to_blocks(v))

    qi = np.arange(blk)[:, None]
    kj = np.arange(2 * blk)[None, :]
    dist_sub = blk + qi - kj
    band = (dist_sub >= 0) & (dist_sub <= span)
    valid = band[None] & ((np.arange(nb)[:, None, None] > 0) | (kj[None] >= blk))
    buckets = t5_causal_bucket(dist_sub * dilation)
    bias = jnp.transpose(rel_bias[buckets], (2, 0, 1)).astype(jnp.float32)

    scores = jnp.einsum('bhrnqe,bhrnke->bhrnqk', qb, kk).astype(jnp.float32) * (hd ** -0.5)
    scores = scores + bias[None, :, None, None]
    scores = jnp.where(valid, scores, -1e30)
    m = jnp.max(scores, axis=-1, keepdims=True)
    p = jnp.exp(scores - m)
    z = jnp.sum(p, axis=-1, keepdims=True)
    out = jnp.einsum('bhrnqk,bhrnke->bhrnqe', p, vv.astype(jnp.float32)) / z
    lse = (m + jnp.log(z))[..., 0]

    out = out.reshape(b, h, dilation, n_sub, hd).transpose(0, 1, 3, 2, 4).reshape(b, h, s_pad, hd)[:, :, :s]
    lse = lse.reshape(b, h, dilation, n_sub).transpose(0, 1, 3, 2).reshape(b, h, s_pad)[:, :, :s]
    return out, lse

def hgrn2_chunkwise(q, f_logit, i, lower_bound):
    b, s, h, dk = q.shape
    dv = i.shape[-1]
    c = HGRN_CHUNK
    nc = s // c
    lb = lower_bound.astype(jnp.float32)
    f = lb + (1.0 - lb) * jax.nn.sigmoid(f_logit.astype(jnp.float32))
    log_f = jnp.log(f)
    key = 1.0 - f
    qf = jax.nn.silu(q.astype(jnp.float32)) * (dk ** -0.5)

    def chunks(t):
        return t.astype(jnp.float32).reshape(b, nc, c, h, t.shape[-1]).transpose(1, 0, 3, 2, 4)

    causal = jnp.tril(jnp.ones((c, c), dtype=bool))

    def step(state, inp):
        qc, kc, vc, gc = inp
        cum = jnp.cumsum(gc, axis=-2)
        o_inter = jnp.einsum('bhtk,bhkv->bhtv', qc * jnp.exp(cum), state)
        diff = cum[:, :, :, None, :] - cum[:, :, None, :, :]
        decay = jnp.exp(jnp.where(causal[:, :, None], diff, -jnp.inf))
        attn = jnp.einsum('bhtk,bhsk,bhtsk->bhts', qc, kc, decay)
        o_intra = jnp.einsum('bhts,bhsv->bhtv', attn, vc)
        last = cum[:, :, -1:, :]
        state = (jnp.exp(last[:, :, 0, :])[..., None] * state
                 + jnp.einsum('bhsk,bhsv->bhkv', kc * jnp.exp(last - cum), vc))
        return state, o_inter + o_intra

    s0 = jnp.zeros((b, h, dk, dv), jnp.float32)
    _, o = lax.scan(step, s0, (chunks(qf), chunks(key), chunks(i), chunks(log_f)))
    return o.transpose(1, 0, 3, 2, 4).reshape(b, s, h, dv)

def token_mixer(xn, w_in_l, rel_bias, lower_bound_l, hgrn_norm_w_l, w_out_l):
    b, s, _ = xn.shape
    proj = xn @ w_in_l
    q_a, k_a, v_a, q_h, f_h, i_h, g_h = jnp.split(proj, IN_SPLITS, axis=-1)

    def attn_heads(t):
        return t.reshape(b, s, ATTN_HEADS, ATTN_HEAD_DIM).transpose(0, 2, 1, 3)

    qa, ka, va = attn_heads(q_a), attn_heads(k_a), attn_heads(v_a)
    outs, lses = [], []
    for window, dilation in DILATION_PATTERNS:
        o, l = dilated_window_attention(qa, ka, va, rel_bias, window, dilation)
        outs.append(o)
        lses.append(l)
    weights = jax.nn.softmax(jnp.stack(lses), axis=0)
    attn = jnp.einsum('pbhs,pbhse->bshe', weights, jnp.stack(outs)).reshape(b, s, ATTN_WIDTH)

    def hgrn_heads(t):
        return t.reshape(b, s, HGRN_HEADS, HGRN_HEAD_DIM)

    hg = hgrn2_chunkwise(hgrn_heads(q_h), hgrn_heads(f_h), hgrn_heads(i_h),
                         lower_bound_l.reshape(HGRN_HEADS, HGRN_HEAD_DIM))
    hg = rms_norm(hg, hgrn_norm_w_l) * jax.nn.silu(hgrn_heads(g_h).astype(jnp.float32))

    mix = jnp.concatenate([attn.astype(xn.dtype), hg.reshape(b, s, HGRN_WIDTH).astype(xn.dtype)], axis=-1)
    return (mix @ w_out_l).astype(xn.dtype)

def expert_ffn(xn, router_w_l, router_b_l, w_gu_l, b_gu_l, w_dn_l, b_dn_l):
    b, s, d = xn.shape
    tokens = xn.reshape(b * s, d)
    n = b * s
    nk = n * TOP_K
    logits = (tokens @ router_w_l).astype(jnp.float32) + router_b_l.astype(jnp.float32)
    top_vals, top_idx = lax.top_k(logits, TOP_K)
    gates = jax.nn.softmax(top_vals, axis=-1)

    flat_e = top_idx.reshape(-1)
    flat_tok = jnp.arange(nk, dtype=jnp.int32) // TOP_K
    flat_g = gates.reshape(-1)
    order = jnp.argsort(flat_e)
    sorted_e = flat_e[order]
    counts = jnp.zeros((N_EXPERTS,), jnp.int32).at[flat_e].add(1)
    padded = (counts + EXPERT_BLOCK - 1) // EXPERT_BLOCK * EXPERT_BLOCK
    start = jnp.cumsum(counts) - counts
    pend = jnp.cumsum(padded)
    pstart = pend - padded
    dest = pstart[sorted_e] + (jnp.arange(nk, dtype=jnp.int32) - start[sorted_e])

    n_blocks = -(-nk // EXPERT_BLOCK) + N_EXPERTS
    cap = n_blocks * EXPERT_BLOCK
    tok_buf = jnp.full((cap,), n, jnp.int32).at[dest].set(flat_tok[order])
    gate_buf = jnp.zeros((cap,), jnp.float32).at[dest].set(flat_g[order])
    block_e = jnp.clip(jnp.searchsorted(pend, jnp.arange(n_blocks, dtype=jnp.int32) * EXPERT_BLOCK,
                                        side='right'), 0, N_EXPERTS - 1)
    tokens_pad = jnp.concatenate([tokens, jnp.zeros((1, d), tokens.dtype)], axis=0)

    def expert_block(args):
        ids, e = args
        xb = tokens_pad[ids]
        hgu = xb @ w_gu_l[e] + b_gu_l[e]
        gate = jnp.minimum(hgu[:, :D_EXPERT], SWIGLU_LIMIT)
        up = jnp.clip(hgu[:, D_EXPERT:], -SWIGLU_LIMIT, SWIGLU_LIMIT)
        act = gate * jax.nn.sigmoid(SWIGLU_ALPHA * gate) * (up + 1.0)
        return act @ w_dn_l[e] + b_dn_l[e]

    out_blocks = lax.map(expert_block, (tok_buf.reshape(n_blocks, EXPERT_BLOCK), block_e))
    y = jnp.zeros((n + 1, d), jnp.float32).at[tok_buf].add(
        out_blocks.reshape(cap, d).astype(jnp.float32) * gate_buf[:, None])
    return y[:n].reshape(b, s, d).astype(xn.dtype)

def setup_inputs(seed: int = 0) -> dict:
    key = jax.random.key(seed)
    ks = jax.random.split(key, 16)
    f32 = jnp.float32

    def nrm(k, shape, scale):
        return jax.random.normal(k, shape, f32) * scale

    return {
        'x': nrm(ks[0], (BATCH, SEQ, D_MODEL), 1.0),
        'norm_mix_w': 1.0 + nrm(ks[1], (DEPTH, D_MODEL), 0.02),
        'w_in': nrm(ks[2], (DEPTH, D_MODEL, IN_PROJ_WIDTH), D_MODEL ** -0.5),
        'rel_bias': nrm(ks[3], (REL_BUCKETS, ATTN_HEADS), 0.5),
        'hgrn_lb_logits': nrm(ks[4], (DEPTH + 1, HGRN_WIDTH), 1.0),
        'hgrn_norm_w': 1.0 + nrm(ks[5], (DEPTH, HGRN_HEAD_DIM), 0.02),
        'w_out': nrm(ks[6], (DEPTH, MIX_WIDTH, D_MODEL), MIX_WIDTH ** -0.5),
        'norm_ffn_w': 1.0 + nrm(ks[7], (DEPTH, D_MODEL), 0.02),
        'router_w': nrm(ks[8], (DEPTH, D_MODEL, N_EXPERTS), D_MODEL ** -0.5),
        'router_b': nrm(ks[9], (DEPTH, N_EXPERTS), 0.01),
        'w_gate_up': nrm(ks[10], (DEPTH, N_EXPERTS, D_MODEL, 2 * D_EXPERT), D_MODEL ** -0.5),
        'b_gate_up': nrm(ks[11], (DEPTH, N_EXPERTS, 2 * D_EXPERT), 0.01),
        'w_down': nrm(ks[12], (DEPTH, N_EXPERTS, D_EXPERT, D_MODEL), D_EXPERT ** -0.5),
        'b_down': nrm(ks[13], (DEPTH, N_EXPERTS, D_MODEL), 0.01),
        'final_norm_w': 1.0 + nrm(ks[14], (D_MODEL,), 0.02),
    }

def reference(x, norm_mix_w, w_in, rel_bias, hgrn_lb_logits, hgrn_norm_w, w_out, norm_ffn_w,
              router_w, router_b, w_gate_up, b_gate_up, w_down, b_down, final_norm_w):
    lower_bounds = jnp.cumsum(jax.nn.softmax(hgrn_lb_logits.astype(jnp.float32), axis=0), axis=0)
    h = x
    for layer in range(DEPTH):
        h = h + token_mixer(rms_norm(h, norm_mix_w[layer]), w_in[layer], rel_bias,
                            lower_bounds[layer], hgrn_norm_w[layer], w_out[layer])
        h = h + expert_ffn(rms_norm(h, norm_ffn_w[layer]), router_w[layer], router_b[layer],
                           w_gate_up[layer], b_gate_up[layer], w_down[layer], b_down[layer])
    return rms_norm(h, final_norm_w)


_drawn_inputs = setup_inputs


def setup_inputs(seed=0):
    import zlib

    import numpy as np

    out = dict(_drawn_inputs(seed))
    spreads = {}
    factors = {'b_gate_up': 8.0, 'b_down': 8.0, 'final_norm_w': 2.878}
    for name, (base, spread) in spreads.items():
        noise = np.random.default_rng([zlib.crc32(name.encode()), seed]).standard_normal(out[name].shape)
        drawn = base * np.exp(spread * noise) if base else spread * noise
        out[name] = __import__('jax').numpy.asarray(drawn.astype(out[name].dtype))
    for name, factor in factors.items():
        out[name] = (out[name] * factor).astype(out[name].dtype)
    return out
```

```python
from contextlib import ExitStack

import numpy as np

import concourse.bass as bass
from concourse import mybir

F32 = mybir.dt.float32
I32 = mybir.dt.int32
U32 = mybir.dt.uint32
U8 = mybir.dt.uint8
ALU = mybir.AluOpType
ACT = mybir.ActivationFunctionType
AX_X = mybir.AxisListType.X

P = 128
S = 1024
D = 1024
TT = S // P
KD = D // P
AH, HD = 8, 64
GH_N = 4
NEXP, TOPK = 32, 4
EPS = 1e-5
BUCKETS, MAX_DISTANCE = 32, 2048
PATTERNS = ((128, 1), (512, 4), (2048, 16))
NEG = -1e30

LEVELS = 7
STEPS = LEVELS + 5
LROW = S + P

CAP = 160
ROUNDS = -(-S // CAP)
STRIDE = ROUNDS * CAP
PAD_ROW = NEXP * STRIDE
TABLE = -(-(PAD_ROW + CAP) // P) * P
TABLE_P = TABLE * 2 // P
PAIRS = NEXP * ROUNDS
MAX_ITEMS = NEXP + S * TOPK // CAP
LIMIT, ALPHA = 7.0, 1.702

COLUMN = {"qa": 0, "ka": 512, "va": 1024, "qh": 1536, "fh": 2048, "ih": 2560, "gh": 3072}
CHUNKS = [(kind, part) for kind in ("fh", "qh", "ih", "gh", "ka", "qa", "va") for part in range(2)]
EARLY = 8
GROUPS = 4 * len(CHUNKS)


def constant_arrays():
    i = np.arange(P)
    ident = np.eye(P, dtype=np.float32)
    before = (i[:, None] < i[None, :]).astype(np.float32)
    masks = np.zeros((P, LEVELS, P), np.float32)
    for level in range(LEVELS):
        h = 64 >> level
        same = (i[:, None] // (2 * h)) == (i[None, :] // (2 * h))
        masks[:, level] = same & ((i[:, None] // h) % 2 == 0) & ((i[None, :] // h) % 2 == 1)
    dist = S - 1 - np.arange(LROW)
    n = np.maximum(dist, 0)
    exact = BUCKETS // 2
    large = exact + (np.log(np.maximum(n, 1) / exact) / np.log(MAX_DISTANCE / exact)
                     * (BUCKETS - exact)).astype(np.int32)
    bucket = np.where(n < exact, n, np.minimum(large, BUCKETS - 1))
    times = sum(((dist >= 0) & (dist % d == 0) & (dist // d <= w // d)).astype(np.int64) for w, d in PATTERNS)
    onehot = ((bucket[None] == np.arange(BUCKETS)[:, None]) & (times > 0)[None]).astype(np.float32)
    log_times = np.where(times > 0, np.log(np.maximum(times, 1)), NEG).astype(np.float32)
    e, r = np.arange(PAIRS) // ROUNDS, np.arange(PAIRS) % ROUNDS
    pairs = np.stack([np.where(r > 0, CAP * r + 0.5, -0.5), (np.arange(PAIRS) - PAIRS) * CAP, e]).astype(np.float32)
    ids = np.zeros((P, TT, TOPK, 2), np.int32)
    tok = np.arange(TT)[None, :, None] * P + i[:, None, None]
    ids[..., 0] = tok * TOPK + np.arange(TOPK)
    ids[..., 1] = tok
    pad = np.tile(np.array([S * TOPK, S], np.int32), TABLE).reshape(P, TABLE_P)
    return {
        "c_ident": ident, "c_before": before, "c_masks": masks.reshape(P, LEVELS * P),
        "c_onehot": onehot, "c_times": log_times[None], "c_pairs": pairs.reshape(1, 3 * PAIRS),
        "c_lane": i[:, None].astype(np.float32), "c_experts": np.arange(NEXP, dtype=np.float32)[None],
        "c_ids": ids.reshape(P, -1), "c_pad": pad,
    }


def build(nc, x, norm_mix_w, w_in, rel_bias, hgrn_lb_logits, hgrn_norm_w, w_out, norm_ffn_w, router_w,
          router_b, w_gate_up, b_gate_up, w_down, b_down, final_norm_w, c_ident, c_before, c_masks,
          c_onehot, c_times, c_pairs, c_lane, c_experts, c_ids, c_pad, out):
    with ExitStack() as ctx:
        def sb(name, shape, dt=F32):
            return ctx.enter_context(nc.sbuf_tensor(name, shape, dt))

        def sem(name):
            return ctx.enter_context(nc.semaphore(name))

        ctx.enter_context(nc.allow_non_contiguous_dma(reason="small per-partition vectors"))

        RX = sb("RX", [P, 8192])
        RW = sb("RW", [P, 4096])
        RP = sb("RP", [P, 28672])
        RT = sb("RT", [P, 8704])

        xnT = RX[:, :].rearrange("p (k s) -> p k s", k=KD)
        win = [RW[:, 2048 * b:2048 * b + 2048].rearrange("p (k n) -> p k n", k=KD) for b in range(2)]
        region = {"qa": 0, "qh": 4096, "ka": 8192, "va": 12288, "gh": 16384, "fh": 20480, "ih": 24576}

        def by_feature(kind):
            return RP[:, region[kind]:region[kind] + 4096].rearrange("p (f s) -> p f s", f=4)

        def by_token(kind):
            return RP[:, region[kind]:region[kind] + 4096].rearrange("p (t n) -> p t n", t=TT)

        QA, KA, QH, FH = (by_feature(k) for k in ("qa", "ka", "qh", "fh"))
        VA, IH, GH = (by_token(k) for k in ("va", "ih", "gh"))

        xt = [RP[:, 16384 + 1024 * b:16384 + 1024 * (b + 1)] for b in range(2)]
        xsq = RP[:, 18432:19456]
        bgu_rows = RP[0:NEXP, 8192:10240]
        bdn_rows = RP[0:NEXP, 10240:11264]
        lrow = RP[0:AH, 12288:12288 + LROW]
        ltimes = RP[0:AH, 13440:13440 + LROW]
        onehot = RP[0:BUCKETS, 14592:14592 + LROW]

        masks_f = RT[:, 0:LEVELS * P]
        C = RT[:, 0:1024]
        DE = [RT[:, 1024:2048], RT[:, 2048:3072]]
        X = [RT[:, 3072:4096], RT[:, 4096:5120]]
        KT = RT[:, 5120:6144]
        QD = RT[:, 6144:7168]
        A = RT[:, 7168:8192]
        SA = X[1]
        BT = [RX[:, 1024 * b:1024 * (b + 1)] for b in range(2)]
        SC = [RX[:, 2048 + 1024 * b:2048 + 1024 * (b + 1)] for b in range(3)]
        PT = [RX[:, 5120 + 1024 * b:5120 + 1024 * (b + 1)] for b in range(2)]
        H = RX[:, :].rearrange("p (t d) -> p t d", t=TT)
        wout = [RP[:, region[k]:region[k] + 4096].rearrange("p (k n) -> p k n", k=4) for k in ("fh", "ih")]
        hsq = RW[:, 0:1024]
        xn2 = [RW[:, 1024:2048], RW[:, 2048:3072]]
        w2b = RW[:, 3072:4096]
        xn2T = [RT[:, 0:1024], RT[:, 1024:2048]]
        ring = [RP[:, region[k]:region[k] + 4096] for k in ("ka", "va", "gh", "fh", "ih", "qa")]
        gu_w = [ring[c].rearrange("p (g k n) -> p g k n", g=2, k=KD) for c in range(4)]
        dn_w = [ring[4 + c].rearrange("p (k n) -> p k n", k=KD) for c in range(2)]
        xT = RT[:, 0:1280].rearrange("p (k s) -> p k s", k=KD)
        actT = RT[:, 1280:2560].rearrange("p (k s) -> p k s", k=KD)
        oT = RT[:, 2560:3840].rearrange("p (k s) -> p k s", k=KD)
        xg, xg2 = RT[:, 3840:4864], RT[0:32, 4864:5888]
        og, og2 = RT[:, 5888:6912], RT[0:32, 6912:7936]
        gate = [RW[:, 320 * b:320 * b + 320].rearrange("p (f s) -> p f s", f=2) for b in range(2)]
        up = [RW[:, 640 + 320 * b:960 + 320 * b].rearrange("p (f s) -> p f s", f=2) for b in range(2)]
        sig = [RW[:, 1280 + 320 * b:1600 + 320 * b].rearrange("p (f s) -> p f s", f=2) for b in range(2)]
        yt = [ring[0], ring[1]]
        osq = ring[2][:, 0:1024]
        wfb = ring[2][:, 1024:2048]
        ot = [ring[3][:, 0:1024], ring[3][:, 1024:2048]]

        ident, before, ones = sb("ident", [P, P]), sb("before", [P, P]), sb("ones", [P, P])
        masks = sb("masks", [P, LEVELS, P], U8)
        relb = sb("relb", [BUCKETS, AH])
        nmw, hnw = sb("nmw", [P, KD]), sb("hnw", [P, 1])
        lbl = sb("lbl", [P, 2, GH_N])
        lb, omlb, lbt = sb("lb", [P, GH_N]), sb("omlb", [P, GH_N]), sb("lbt", [P, 4, GH_N])
        rw = sb("rw", [P, KD, NEXP])
        rb = sb("rb", [P, NEXP])
        biasT = sb("biasT", [P, 24, NEXP])
        pairs = sb("pairs", [P, 3, PAIRS])
        lane = sb("lane", [P, 1])
        experts = sb("experts", [P, NEXP])
        ids = sb("ids", [P, TT * TOPK, 2], I32)
        ss, rs = sb("ss", [P, TT]), sb("rs", [P, TT])
        dl, hss, hrs = sb("dl", [P, TT]), sb("hss", [P, TT]), sb("hrs", [P, TT])
        am, az = sb("am", [P, 8 * AH]), sb("az", [P, 8 * AH])
        def spare(at, n):
            return RT[:, at:at + n]

        lg, mask, macc, rk = (spare(2048 + 256 * c, 256).rearrange("p (t e) -> p t e", t=TT) for c in range(4))
        flags, posn, picked = (spare(7936 + PAIRS * c, PAIRS) for c in range(3))
        oh = hsq.rearrange("p (k t e) -> p k t e", k=TOPK, t=TT)
        vals = sb("vals", [P, TT, 8])
        idx, idxf = sb("idx", [P, TT, 8], U32), sb("idxf", [P, TT, 8])
        rkk = sb("rkk", [P, TOPK, TT])
        slots = sb("slots", [P, TT * TOPK], I32)
        gts, gsum = sb("gts", [P, TT, TOPK]), sb("gsum", [P, TT])
        icol = sb("icol", [P, 3])
        items = sb("items", [1, 3, P], I32)
        bcur = sb("bcur", [P, 24])
        tok, tok2 = sb("tok", [P, 2], I32), sb("tok2", [32, 2], I32)
        dst, dst2 = sb("dst", [P, 1], I32), sb("dst2", [32, 1], I32)
        zero, idle = sb("zero", [P, 1], I32), sb("idle", [P, 2], I32)

        PS = ctx.enter_context(nc.psum_tensor("PS", [P, 8, 512], F32))

        def pair(n):
            return PS[:, 2 * n:2 * n + 2, :].rearrange("p b n -> p (b n)")

        lrow_dram = nc.dram_tensor("lrow_dram", [AH, LROW], F32)
        shifted_dram = nc.dram_tensor("shifted_dram", [AH, P, LROW], F32)
        xn_dram = nc.dram_tensor("xn_dram", [S, D], F32)
        table = nc.dram_tensor("table", [TABLE, 2], I32)
        y_dram = nc.dram_tensor("y_dram", [S * TOPK, D], F32)

        consts_in = sem("consts_in")
        x_in = [sem(f"x_in{b}") for b in range(2)]
        w_in_sem = [sem(f"win_in{b}") for b in range(2)]
        bt_in = [sem(f"bt_in{b}") for b in range(2)]
        wout_in, w2b_in, wfb_in = sem("wout_in"), sem("w2b_in"), sem("wfb_in")
        h_in = sem("h_in")
        ones_set, xg_set = sem("ones_set"), sem("xg_set")
        lrow_sum, lrow_out, lrow_mm, shifted_out = sem("lrow_sum"), sem("lrow_out"), sem("lrow_mm"), sem("shifted_out")
        bias_mm, bias_copied = sem("bias_mm"), sem("bias_copied")
        ss_done, rs_done = sem("ss_done"), sem("rs_done")
        xs_ready, xT_mm, xnT_ready = sem("xs_ready"), sem("xT_mm"), sem("xnT_ready")
        proj_done, proj_out = sem("proj_done"), sem("proj_out")
        h_f, h_g, h_k, h_d, h_e, h_x = (sem(n) for n in ("h_f", "h_g", "h_k", "h_d", "h_e", "h_x"))
        h_step, h_dve_out, h_act_out, h_sq, h_ss = (sem(n) for n in ("h_step", "h_dve_out", "h_act_out", "h_sq", "h_ss"))
        lb_exp, lb_sub = sem("lb_exp"), sem("lb_sub")
        qk_done, att_m, att_p, att_n = sem("qk_done"), sem("att_m"), sem("att_p"), sem("att_n")
        tr_done, att_pt, pv_done, att_o = sem("tr_done"), sem("att_pt"), sem("pv_done"), sem("att_o")
        op_done, h_done, hss_done, xn2_ready = sem("op_done"), sem("h_done"), sem("hss_done"), sem("xn2_ready")
        xn2_out = [sem(f"xn2_out{b}") for b in range(2)]
        xn2T_mm, xn2T_ready, lg_done = sem("xn2T_mm"), sem("xn2T_ready"), sem("lg_done")
        gexp_in, gexp, mask_ready, rank_done = sem("gexp_in"), sem("gexp"), sem("mask_ready"), sem("rank_done")
        slots_ready, icol_ready, items_mm, items_ready = (sem(n) for n in ("slots_ready", "icol_ready", "items_mm", "items_ready"))
        table_pad, table_in = sem("table_pad"), sem("table_in")
        w_load = [sem(f"w_load{c}") for c in range(6)]
        gu_done, gu_free, g_ready, sig_ready, act_ready = (sem(n) for n in ("gu_done", "gu_free", "g_ready", "sig_ready", "act_ready"))
        tok_in, xg_in, t_done, t_free = (sem(n) for n in ("tok_in", "xg_in", "t_done", "t_free"))
        dn_done, dn_free, bcur_ready, dst_copied, y_out = (sem(n) for n in ("dn_done", "dn_free", "bcur_ready", "dst_copied", "y_out"))
        dve_step, act_step, pool_step = sem("dve_step"), sem("act_step"), sem("pool_step")
        y_in = [sem(f"y_in{b}") for b in range(2)]
        y_sum, oss_done, o_ready = sem("y_sum"), sem("oss_done"), sem("o_ready")
        o_out = [sem(f"o_out{b}") for b in range(2)]

        N_CONST = 17
        X2 = x[0]
        SCHEDULE = [("group", g) for g in range(4 * EARLY)]
        late = GROUPS - 4 * EARLY
        for g in range(late):
            SCHEDULE.append(("group", 4 * EARLY + g))
            SCHEDULE += [("step", s) for s in range(g * GH_N * STEPS // late, (g + 1) * GH_N * STEPS // late)]
        ITEMS_A = 8 * AH

        block = ctx.enter_context(nc.Block())

        def load_w_in(sp, c):
            kind, part = CHUNKS[c]
            at = COLUMN[kind] + 256 * part
            sp.dma_start(win[c % 2], w_in[0, :, at:at + 256].rearrange("(k p) n -> p k n", p=P)).then_inc(w_in_sem[c % 2], 16)

        def load_expert_chunk(sp, e, c):
            wg = w_gate_up[0, bass.ds(e, 1)].rearrange("a (k p) n -> p (a k) n", p=P)
            wd = w_down[0, bass.ds(e, 1)].rearrange("a (k p) n -> p (a k) n", p=P)
            if c < 4:
                for g in range(2):
                    sp.dma_start(gu_w[c][:, g], wg[:, :, g * D + 256 * c:g * D + 256 * (c + 1)]).then_inc(w_load[c], 16)
            else:
                sp.dma_start(dn_w[c - 4], wd[:, :, 512 * (c - 4):512 * (c - 3)]).then_inc(w_load[c], 16)

        @block.sync
        def _(sp):
            for dst_ap, src in (
                (ident[:, :], c_ident), (before[:, :], c_before), (masks_f, c_masks),
                (onehot, c_onehot), (ltimes, c_times[0, :].partition_broadcast(AH)), (relb[:, :], rel_bias),
                (nmw[:, :], norm_mix_w[0].rearrange("(k p) -> p k", p=P)),
                (hnw[:, :], hgrn_norm_w[0].rearrange("(p a) -> p a", a=1)),
                (lbl[:, :, :], hgrn_lb_logits.rearrange("l (h p) -> p l h", p=P)),
                (bgu_rows, b_gate_up[0]), (bdn_rows, b_down[0]),
                (rw[:, :, :], router_w[0].rearrange("(k p) e -> p k e", p=P)),
                (rb[:, :], router_b[0].partition_broadcast(P)),
                (pairs[:, :, :].rearrange("p a b -> p (a b)"), c_pairs[0, :].partition_broadcast(P)), (lane[:, :], c_lane),
                (experts[:, :], c_experts[0, :].partition_broadcast(P)),
                (ids[:, :, :].rearrange("p a b -> p (a b)"), c_ids),
            ):
                sp.dma_start(dst_ap, src).then_inc(consts_in, 16)
            sp.dma_start(table[:, :].rearrange("(p r) c -> p (r c)", p=P), c_pad).then_inc(table_pad, 16)
            for t in range(TT):
                if t >= 2:
                    sp.wait_ge(xT_mm, t - 1)
                sp.dma_start(xt[t % 2], X2[t * P:(t + 1) * P, :]).then_inc(x_in[t % 2], 16)
                if t < 2:
                    load_w_in(sp, t)
            for c in range(2, len(CHUNKS)):
                sp.wait_ge(proj_done, 4 * (c - 1))
                load_w_in(sp, c)
                if c == 5:
                    sp.wait_ge(lrow_out, 16)
                    for h in range(AH):
                        sp.dma_start(shifted_dram[h], lrow_dram[h, :].partition_broadcast(P)).then_inc(shifted_out, 16)
                if c == 3:
                    sp.wait_ge(lrow_sum, 3)
                    sp.dma_start(lrow_dram[:, :], lrow).then_inc(lrow_out, 16)
            sp.wait_ge(proj_done, GROUPS)
            sp.wait_ge(shifted_out, 16 * AH)
            for h in range(AH):
                if h >= 2:
                    sp.wait_ge(att_m, 8 * (h - 1))
                sp.dma_start(BT[h % 2], bass.AP(shifted_dram, h * P * LROW + P - 1, [[LROW - 1, P], [1, S]])).then_inc(bt_in[h % 2], 16)
                if h == 0:
                    sp.wait_ge(proj_out, GROUPS)
                    sp.dma_start(w2b, norm_ffn_w[0].partition_broadcast(P)).then_inc(w2b_in, 16)
                    sp.wait_ge(h_step, GH_N * STEPS)
                    for c in range(2):
                        sp.dma_start(wout[c], w_out[0, 512 * c:512 * (c + 1), :].rearrange("(k p) n -> p k n", p=P)).then_inc(wout_in, 16)
            sp.wait_ge(pv_done, ITEMS_A)
            sp.dma_start(H, X2.rearrange("(t p) d -> p t d", p=P)).then_inc(h_in, 16)
            sp.wait_ge(h_dve_out, 10 * GH_N)
            for c in range(3):
                load_expert_chunk(sp, 0, c)
            for t in range(TT):
                sp.wait_ge(xn2_ready, t + 1)
                sp.dma_start(xn_dram[t * P:(t + 1) * P, :], xn2[t % 2]).then_inc(xn2_out[t % 2], 16)
            sp.wait_ge(op_done, TT)
            for c in range(3, 6):
                load_expert_chunk(sp, 0, c)
            sp.wait_ge(items_ready, 3)
            n = sp.value_load(items[0:1, 2, 0:1], min_val=NEXP, max_val=MAX_ITEMS)
            with sp.Fori(1, n) as i:
                e = sp.value_load(items[0:1, 1, bass.ds(i, 1)], min_val=0, max_val=NEXP - 1)
                for c in range(6):
                    if c < 4:
                        sp.wait_ge(gu_done, 4 * i + (c - 3))
                    else:
                        sp.wait_ge(dn_done, 4 * i + (2 * c - 10))
                    load_expert_chunk(sp, e, c)
            sp.wait_ge(gu_done, 4 * n)
            sp.wait_ge(dn_done, 4 * n)
            sp.dma_start(wfb, final_norm_w.partition_broadcast(P)).then_inc(wfb_in, 16)
            sp.wait_ge(y_out, 32 * n)
            for t in range(TT):
                if t >= 2:
                    sp.wait_ge(y_sum, t - 1)
                sp.dma_start(yt[t % 2], y_dram[t * P * TOPK:(t + 1) * P * TOPK, :].rearrange("(p k) d -> p (k d)", k=TOPK)).then_inc(y_in[t % 2], 16)

        @block.gpsimd
        def _(pool):
            pool.memset(ones[:, :], 1.0).then_inc(ones_set, 1)
            pool.wait_ge(consts_in, 16 * N_CONST)
            pool.tensor_copy(masks[:, :, :].rearrange("p l t -> p (l t)"), masks_f).then_inc(ones_set, 1)
            pool.wait_ge(table_pad, 16)
            pool.wait_ge(h_step, GH_N * STEPS)
            pool.wait_ge(h_dve_out, 10 * GH_N)
            pool.wait_ge(h_act_out, 2 * GH_N)
            pool.memset(zero[:, :], 0).then_inc(t_free, 1)
            pool.memset(xg, 0.0).then_inc(xg_set, 1)
            pool.memset(xg2, 0.0).then_inc(xg_set, 1)
            pool.wait_ge(slots_ready, 4)
            for j in range(TT * TOPK):
                pool.indirect_dma_start(
                    table[:, :], bass.IndirectOffsetOnAxis(ap=slots[:, j:j + 1], axis=0),
                    ids[:, j, :], None, bounds_check=PAD_ROW - 1, oob_is_err=False).then_inc(table_in, 16)
            pool.wait_ge(table_in, 16 * TT * TOPK)
            for b in range(2):
                pool.wait_ge(xn2_out[b], 16 * TT // 2)
            pool.wait_ge(items_ready, 3)
            pool.wait_ge(xg_set, 2)
            pool.wait_ge(t_free, 1)

            last_row, last_place = pool.to_reg(S - 1), pool.to_reg(S * TOPK - 1)

            def load_tokens(at):
                pool.dma_start(tok[:, :], table[bass.ds(at, P), :]).then_inc(tok_in, 16)
                pool.dma_start(tok2[:, :], table[bass.ds(at + P, 32), :]).then_inc(tok_in, 16)

            def gather():
                pool.indirect_dma_start(xg, None, xn_dram[:, :], bass.IndirectOffsetOnAxis(ap=tok[:, 1:2], axis=0),
                                        bounds_check=last_row, oob_is_err=False).then_inc(xg_in, 16)
                pool.indirect_dma_start(xg2, None, xn_dram[:, :], bass.IndirectOffsetOnAxis(ap=tok2[:, 1:2], axis=0),
                                        bounds_check=last_row, oob_is_err=False).then_inc(xg_in, 16)

            load_tokens(pool.value_load(items[0:1, 0, 0:1], min_val=0, max_val=PAD_ROW))
            pool.wait_ge(tok_in, 32)
            gather()
            n = pool.value_load(items[0:1, 2, 0:1], min_val=NEXP, max_val=MAX_ITEMS)
            with pool.Fori(0, n) as i:
                at = pool.value_load(items[0:1, 0, bass.ds(i + 1, 1)], min_val=0, max_val=PAD_ROW)
                pool.tensor_tensor(dst[:, :], tok[:, 0:1], zero[:, :], ALU.add).then_inc(dst_copied, 1)
                pool.tensor_tensor(dst2[:, :], tok2[:, 0:1], zero[0:32, :], ALU.add).then_inc(dst_copied, 1)
                pool.wait_ge(dst_copied, 2 * i + 2)
                pool.wait_ge(xg_in, 32 * i + 32)
                load_tokens(at)
                pool.wait_ge(tok_in, 32 * i + 64)
                pool.wait_ge(t_done, 8 * i + 4)
                pool.tensor_tensor(idle[:, 0:1], zero[:, :], zero[:, :], ALU.add)
                gather()
                pool.wait_ge(t_free, 8 * i + 13)
                pool.tensor_tensor(idle[:, 1:2], zero[:, :], zero[:, :], ALU.add)
                pool.indirect_dma_start(y_dram[:, :], bass.IndirectOffsetOnAxis(ap=dst[:, 0:1], axis=0), og, None,
                                        bounds_check=last_place, oob_is_err=False).then_inc(y_out, 16)
                pool.indirect_dma_start(y_dram[:, :], bass.IndirectOffsetOnAxis(ap=dst2[:, 0:1], axis=0), og2, None,
                                        bounds_check=last_place, oob_is_err=False).then_inc(y_out, 16)
                pool.wait_ge(y_out, 32 * i + 32)
            pool.wait_ge(xg_in, 32 * n + 32)

        @block.scalar
        def _(act):
            act.wait_ge(consts_in, 16 * N_CONST)
            act.wait_ge(lb_sub, 1)
            act.activation(lbt[:, 2:4, :], lbt[:, 0:2, :], ACT.Exp).then_inc(lb_exp, 1)
            act.wait_ge(bias_mm, 1)
            act.activation(biasT[:, :, :].rearrange("p f e -> p (f e)"), pair(2)[:, 0:24 * NEXP], ACT.Copy).then_inc(bias_copied, 1)
            for t in range(TT):
                act.wait_ge(x_in[t % 2], 16 * (t // 2 + 1))
                if t >= 1:
                    act.wait_ge(ss_done, 2 * t)
                act.activation(xsq, xt[t % 2], ACT.Square, accum_out=ss[:, t:t + 1]).then_inc(ss_done, 1)
                act.wait_ge(ss_done, 2 * t + 1)
                act.activation(rs[:, t:t + 1], ss[:, t:t + 1], ACT.Sqrt, scale=1.0 / D, bias=EPS).then_inc(ss_done, 1)

            def evacuate(g):
                kind, part = CHUNKS[g // 4]
                act.wait_ge(proj_done, g + 1)
                bank = PS[:, 6 + g % 2, :]
                if kind in ("fh", "qh", "qa", "ka"):
                    ft, half = divmod(g % 4, 2)
                    to, src = by_feature(kind)[:, 2 * part + ft, 512 * half:512 * half + 512], bank
                else:
                    t = 2 * (g % 4)
                    to = by_token(kind)[:, t:t + 2, 256 * part:256 * part + 256]
                    src = bank.rearrange("p (t n) -> p t n", t=2)
                func = {"fh": ACT.Sigmoid, "qh": ACT.Silu, "gh": ACT.Silu}.get(kind, ACT.Copy)
                act.activation(to, src, func, scale=HD ** -0.5 if kind == "qa" else 1.0).then_inc(proj_out, 1)

            def decay(hd, m):
                act.wait_ge(h_d, 9 * hd + m + 2)
                act.activation(DE[m % 2], DE[m % 2], ACT.Exp).then_inc(h_e, 1)

            def head_start(hd):
                act.wait_ge(h_f, hd + 1)
                if hd:
                    act.wait_ge(h_x, 9 * hd)
                act.activation(DE[0], FH[:, hd, :], ACT.Ln).then_inc(h_g, 1)
                decay(hd, 0)
                decay(hd, 1)

            def step(s):
                hd, j = divmod(s, STEPS)
                if s == 0:
                    head_start(0)
                if 1 <= j <= 6:
                    decay(hd, j + 1)
                if j == 7:
                    act.activation(dl[:, :], C.rearrange("p (b t) -> p b t", b=TT)[:, :, P - 1], ACT.Exp).then_inc(h_e, 1)
                    act.wait_ge(h_x, 9 * hd + 7)
                    act.activation(DE[0], C, ACT.Exp).then_inc(h_e, 1)
                if j == 8:
                    act.wait_ge(h_step, s + 1)
                    act.activation(KT, pair(s % 2), ACT.Copy).then_inc(h_act_out, 1)
                    if hd + 1 < GH_N:
                        head_start(hd + 1)
                if j == 10:
                    act.wait_ge(h_step, s + 1)
                    act.activation(A, pair(s % 2), ACT.Square).then_inc(h_sq, 1)
                    act.wait_ge(h_ss, hd + 1)
                    act.activation(hrs[:, :], hss[:, :], ACT.Sqrt, scale=1.0 / P, bias=EPS * P).then_inc(h_sq, 1)
                if j == 11:
                    act.wait_ge(h_step, s + 1)
                    act.activation(QH[:, hd, :], pair(s % 2), ACT.Copy, scale=hnw[:, 0:1]).then_inc(h_act_out, 1)

            for what, n in SCHEDULE:
                evacuate(n) if what == "group" else step(n)

            def put_pt(a):
                w = (a % 8 + 1) * P
                act.wait_ge(tr_done, a + 1)
                if a >= 2:
                    act.wait_ge(pv_done, a - 1)
                act.activation(PT[a % 2][:, 0:w], pair(2)[:, 0:w], ACT.Copy).then_inc(att_pt, 1)

            for a in range(ITEMS_A):
                w = (a % 8 + 1) * P
                act.wait_ge(att_m, a + 1)
                act.activation(SC[a % 3][:, 0:w], SC[a % 3][:, 0:w], ACT.Exp, bias=am[:, a:a + 1],
                               accum_out=az[:, a:a + 1]).then_inc(att_p, 1)
                if a >= 1:
                    put_pt(a - 1)
            put_pt(ITEMS_A - 1)

            def put_xn2T(t):
                act.wait_ge(xn2T_mm, t + 1)
                if t >= 2:
                    act.wait_ge(lg_done, t - 1)
                act.activation(xn2T[t % 2], pair(2), ACT.Copy).then_inc(xn2T_ready, 1)

            for t in range(TT):
                act.wait_ge(h_done, t + 1)
                if t >= 1:
                    act.wait_ge(hss_done, 2 * t)
                act.activation(hsq, H[:, t, :], ACT.Square, accum_out=ss[:, t:t + 1]).then_inc(hss_done, 1)
                act.wait_ge(hss_done, 2 * t + 1)
                act.activation(rs[:, t:t + 1], ss[:, t:t + 1], ACT.Sqrt, scale=1.0 / D, bias=EPS).then_inc(hss_done, 1)
                if t >= 1:
                    put_xn2T(t - 1)
            put_xn2T(TT - 1)
            act.wait_ge(gexp_in, 1)
            act.activation(gts[:, :, :], gts[:, :, :], ACT.Exp).then_inc(gexp, 1)

            def put_x(r):
                act.activation(xT[:, 2 * r:2 * r + 2, :], PS[:, 6 + r % 2, 0:2 * CAP].rearrange("p (k s) -> p k s", k=2),
                               ACT.Copy).then_inc(t_free, 1)

            act.wait_ge(items_ready, 3)
            for r in range(4):
                act.wait_ge(t_done, r + 1)
                put_x(r)
            n = act.value_load(items[0:1, 2, 0:1], min_val=NEXP, max_val=MAX_ITEMS)
            with act.Fori(0, n) as i:
                for j in range(4):
                    act.wait_ge(g_ready, 4 * i + j + 1)
                    act.activation(sig[j % 2], gate[j % 2], ACT.Sigmoid, scale=ALPHA).then_inc(sig_ready, 1)
                for r in range(4):
                    act.wait_ge(t_done, 8 * i + r + 5)
                    put_x(r)
                for q in range(4):
                    act.wait_ge(dn_done, 4 * i + q + 1)
                    for f in range(2):
                        act.activation(oT[:, 2 * q + f, :], PS[:, 4 + q % 2, CAP * f:CAP * (f + 1)], ACT.Identity,
                                       bias=bcur[:, 16 + 2 * q + f:17 + 2 * q + f]).then_inc(dn_free, 1)
                act.wait_ge(dst_copied, 2 * i + 2)
                for g in range(2):
                    act.wait_ge(t_done, 8 * i + 2 * g + 9)
                    act.activation(og[:, 512 * g:512 * (g + 1)], PS[:, 6, :], ACT.Copy).then_inc(t_free, 1)
                    act.wait_ge(t_done, 8 * i + 2 * g + 10)
                    act.activation(og2[:, 512 * g:512 * (g + 1)], PS[0:32, 7, :], ACT.Copy).then_inc(t_free, 1)

            for t in range(TT):
                act.wait_ge(y_sum, t + 1)
                if t >= 1:
                    act.wait_ge(oss_done, 2 * t)
                act.activation(osq, H[:, t, :], ACT.Square, accum_out=ss[:, t:t + 1]).then_inc(oss_done, 1)
                act.wait_ge(oss_done, 2 * t + 1)
                act.activation(rs[:, t:t + 1], ss[:, t:t + 1], ACT.Sqrt, scale=1.0 / D, bias=EPS).then_inc(oss_done, 1)
                act.wait_ge(o_ready, t + 1)
                act.dma_start(out[0, t * P:(t + 1) * P, :], ot[t % 2]).then_inc(o_out[t % 2], 16)
            for b in range(2):
                act.wait_ge(o_out[b], 16 * TT // 2)

        @block.vector
        def _(dve):
            steps = [0]

            def link(ins):
                steps[0] += 1
                ins.then_inc(dve_step, 1)
                dve.wait_ge(dve_step, steps[0])

            dve.wait_ge(consts_in, 16 * N_CONST)
            link(dve.tensor_tensor(lbt[:, 2, :], lbl[:, 0, :], lbl[:, 1, :], ALU.max))
            link(dve.tensor_tensor(lbt[:, 0, :], lbl[:, 0, :], lbt[:, 2, :], ALU.subtract))
            dve.tensor_tensor(lbt[:, 1, :], lbl[:, 1, :], lbt[:, 2, :], ALU.subtract).then_inc(lb_sub, 1)
            dve.wait_ge(lb_exp, 1)
            link(dve.tensor_tensor(lbt[:, 0, :], lbt[:, 2, :], lbt[:, 3, :], ALU.add))
            link(dve.reciprocal(lbt[:, 1, :], lbt[:, 0, :]))
            link(dve.tensor_tensor(lb[:, :], lbt[:, 2, :], lbt[:, 1, :], ALU.mult))
            link(dve.tensor_scalar(omlb[:, :], lb[:, :], -1.0, 1.0, ALU.mult, ALU.add))
            for c, (bank, at, a, b) in enumerate(((6, 0, 0, 512), (7, 0, 512, 1024), (5, 256, 1024, LROW))):
                dve.wait_ge(lrow_mm, c + 1)
                dve.tensor_tensor(lrow[:, a:b], PS[0:AH, bank, at:at + b - a], ltimes[:, a:b], ALU.add).then_inc(lrow_sum, 1)
            for t in range(TT):
                dve.wait_ge(ss_done, 2 * t + 2)
                link(dve.reciprocal(rs[:, t:t + 1], rs[:, t:t + 1]))
                dve.tensor_scalar(xt[t % 2], xt[t % 2], rs[:, t:t + 1], None, ALU.mult).then_inc(xs_ready, 1)
                dve.wait_ge(xT_mm, t + 1)
                dve.tensor_tensor(xnT[:, :, t * P:(t + 1) * P], pair(t % 2).rearrange("p (k s) -> p k s", k=KD),
                                  nmw[:, :].unsqueeze(2).to_broadcast([P, KD, P]), ALU.mult).then_inc(xnT_ready, 1)

            def halves(ap, m):
                h = 64 >> m
                v = ap.rearrange("p (n two h) -> p n two h", two=2, h=h)
                return v[:, :, 0, :], v[:, :, 1, :], v[:, :, 0, h - 1:h].to_broadcast([P, S // (2 * h), h])

            Cb = C.rearrange("p (b t) -> p b t", b=TT)

            def difference(hd, m):
                d = DE[m % 2]
                if m < LEVELS:
                    left, right, mid = halves(C, m)
                    dl_, dr_, _ = halves(d, m)
                    link(dve.tensor_tensor(dl_, mid, left, ALU.subtract))
                    dve.tensor_tensor(dr_, right, mid, ALU.subtract).then_inc(h_d, 1)
                else:
                    dve.tensor_tensor(d.rearrange("p (b t) -> p b t", b=TT), Cb[:, :, P - 1:P].to_broadcast([P, TT, P]), Cb,
                                      ALU.subtract).then_inc(h_d, 1)

            def scaled(hd, m):
                if m < 8:
                    dve.wait_ge(h_e, 10 * hd + m + 1)
                    if m >= 2:
                        dve.wait_ge(h_step, STEPS * hd + m)
                    elif hd:
                        dve.wait_ge(h_step, STEPS * (hd - 1) + (9 if m == 0 else 11))
                if m < LEVELS:
                    el, er, _ = halves(DE[m % 2], m)
                    xl, xr, _ = halves(X[m % 2], m)
                    kl, _, _ = halves(FH[:, hd, :], m)
                    _, qr, _ = halves(QH[:, hd, :], m)
                    link(dve.tensor_tensor(xl, el, kl, ALU.mult))
                    dve.tensor_tensor(xr, er, qr, ALU.mult).then_inc(h_x, 1)
                elif m == 7:
                    dve.tensor_tensor(X[1], DE[1], FH[:, hd, :], ALU.mult).then_inc(h_x, 1)
                else:
                    dve.wait_ge(h_e, 10 * hd + 10)
                    dve.tensor_tensor(QD, DE[0], QH[:, hd, :], ALU.mult).then_inc(h_x, 1)

            def head_start(hd):
                link(dve.tensor_scalar(FH[:, hd, :], FH[:, hd, :], omlb[:, hd:hd + 1], lb[:, hd:hd + 1], ALU.mult, ALU.add))
                dve.tensor_copy(lbt[:, 0, :], lb[:, :]).then_inc(h_f, 1)
                dve.wait_ge(h_g, hd + 1)
                dve.tensor_scalar(FH[:, hd, :], FH[:, hd, :], -1.0, 1.0, ALU.mult, ALU.add).then_inc(h_k, 1)
                for b in range(TT):
                    ins = dve.tensor_tensor_scan(Cb[:, b, :], ones[:, :], DE[0][:, b * P:(b + 1) * P], 0.0, ALU.mult, ALU.add)
                ins.then_inc(h_d, 1)
                dve.wait_ge(h_d, 9 * hd + 1)
                difference(hd, 0)
                difference(hd, 1)
                scaled(hd, 0)

            def step(s):
                hd, j = divmod(s, STEPS)
                if s == 0:
                    dve.wait_ge(proj_out, 16)
                    dve.wait_ge(ones_set, 2)
                    head_start(0)
                if 1 <= j <= 7:
                    dve.wait_ge(h_x, 9 * hd + j)
                    if j + 1 <= 7:
                        difference(hd, j + 1)
                    scaled(hd, j)
                    if j == 7:
                        scaled(hd, 8)
                if j <= 7:
                    dve.wait_ge(h_step, s + 1)
                    to = A.rearrange("p (b t) -> p b t", b=TT)
                    src = pair(s % 2).rearrange("p (b t) -> p b t", b=TT)
                    if j == 0:
                        ins = dve.tensor_tensor(to, src, ident[:, :].unsqueeze(1).to_broadcast([P, TT, P]), ALU.mult)
                    else:
                        dve.wait_ge(h_dve_out, 10 * hd + j)
                        ins = dve.copy_predicated(to, masks[:, j - 1, :].unsqueeze(1).to_broadcast([P, TT, P]), src)
                    ins.then_inc(h_dve_out, 1)
                if j == 8 and hd + 1 < GH_N:
                    dve.wait_ge(h_x, 9 * hd + 9)
                    head_start(hd + 1)
                if j == 9:
                    dve.wait_ge(h_step, s + 1)
                    dve.wait_ge(h_e, 10 * hd + 9)
                    sa = SA.rearrange("p (b v) -> p b v", b=TT)
                    su = pair(s % 2).rearrange("p (b v) -> p b v", b=TT)
                    link(dve.tensor_copy(sa[:, 1, :], su[:, 0, :]))
                    for b in range(1, TT - 1):
                        ins = dve.scalar_tensor_tensor(sa[:, b + 1, :], sa[:, b, :], dl[:, b:b + 1], su[:, b, :], ALU.mult, ALU.add)
                        if b < TT - 2:
                            link(ins)
                    ins.then_inc(h_dve_out, 1)
                if j == 10:
                    dve.wait_ge(h_sq, 2 * hd + 1)
                    dve.tensor_reduce(hss[:, :], A.rearrange("p (b v) -> p b v", b=TT), AX_X, ALU.add).then_inc(h_ss, 1)
                    dve.wait_ge(h_sq, 2 * hd + 2)
                    link(dve.reciprocal(hrs[:, :], hrs[:, :]))
                    o = KT.rearrange("p (b v) -> p b v", b=TT)
                    link(dve.tensor_tensor(o, pair(s % 2).rearrange("p (b v) -> p b v", b=TT),
                                           hrs[:, :].unsqueeze(2).to_broadcast([P, TT, P]), ALU.mult))
                    dve.tensor_tensor(o, o, GH[:, :, P * hd:P * (hd + 1)], ALU.mult).then_inc(h_dve_out, 1)

            for what, n in SCHEDULE:
                if what == "step":
                    if n % STEPS == 10:
                        dve.wait_ge(proj_out, 4 * EARLY)
                    step(n)

            def normalise(a):
                w = (a % 8 + 1) * P
                dve.wait_ge(att_p, a + 1)
                link(dve.reciprocal(az[:, a:a + 1], az[:, a:a + 1]))
                dve.tensor_scalar(SC[a % 3][:, 0:w], SC[a % 3][:, 0:w], az[:, a:a + 1], None, ALU.mult).then_inc(att_n, 1)

            def put_o(quad):
                h, at, b0 = quad // 2, 512 * (quad % 2), HD * ((quad // 2) % 2)
                dve.wait_ge(pv_done, 4 * quad + 4)
                dve.tensor_copy(QA[b0:b0 + HD, h // 2, at:at + 512], PS[b0:b0 + HD, 6 + quad % 2, :]).then_inc(att_o, 1)

            for a in range(ITEMS_A + 2):
                h, n = divmod(a, 8)
                w = (n + 1) * P
                if a < ITEMS_A:
                    dve.wait_ge(qk_done, a + 1)
                    dve.wait_ge(bt_in[h % 2], 16 * (h // 2 + 1))
                    if a >= 3:
                        dve.wait_ge(tr_done, a - 2)
                    link(dve.tensor_tensor_reduce(SC[a % 3][:, 0:w], pair(a % 2)[:, 0:w], BT[h % 2][:, S - w:S], 1.0, -3e38,
                                                  ALU.add, ALU.max, am[:, a:a + 1]))
                    dve.tensor_scalar(am[:, a:a + 1], am[:, a:a + 1], -1.0, None, ALU.mult).then_inc(att_m, 1)
                if 1 <= a <= ITEMS_A:
                    normalise(a - 1)
                if a % 4 == 1 and a >= 5:
                    put_o((a - 5) // 4)

            dve.wait_ge(h_in, 16)
            dve.wait_ge(w2b_in, 16)

            def norm_rows(t):
                dve.wait_ge(hss_done, 2 * t + 2)
                link(dve.reciprocal(rs[:, t:t + 1], rs[:, t:t + 1]))
                if t >= 2:
                    dve.wait_ge(xn2_out[t % 2], 16 * (t // 2))
                    dve.wait_ge(xn2T_mm, t - 1)
                dve.scalar_tensor_tensor(xn2[t % 2], H[:, t, :], rs[:, t:t + 1], w2b, ALU.mult, ALU.mult).then_inc(xn2_ready, 1)

            for t in range(TT):
                dve.wait_ge(op_done, t + 1)
                dve.tensor_tensor(H[:, t, :], pair(t % 2), H[:, t, :], ALU.add).then_inc(h_done, 1)
                if t >= 1:
                    norm_rows(t - 1)
            norm_rows(TT - 1)

            dve.wait_ge(lg_done, TT)
            link(dve.tensor_tensor(lg[:, :, :], PS[:, 6, 0:TT * NEXP].rearrange("p (t e) -> p t e", t=TT),
                                   rb[:, :].unsqueeze(1).to_broadcast([P, TT, NEXP]), ALU.add))
            for t in range(TT):
                link(dve.max(vals[:, t, :], lg[:, t, :]))
                link(dve.max_index(idx[:, t, :], vals[:, t, :], lg[:, t, :]))
            link(dve.tensor_copy(idxf[:, :, :], idx[:, :, :]))
            dve.tensor_tensor(gts[:, :, :], vals[:, :, 0:TOPK], vals[:, :, 0:1].to_broadcast([P, TT, TOPK]),
                              ALU.subtract).then_inc(gexp_in, 1)
            for k in range(TOPK):
                link(dve.tensor_tensor(oh[:, k], experts[:, :].unsqueeze(1).to_broadcast([P, TT, NEXP]),
                                       idxf[:, :, k:k + 1].to_broadcast([P, TT, NEXP]), ALU.is_equal))
            link(dve.tensor_tensor(mask[:, :, :], oh[:, 0], oh[:, 1], ALU.add))
            link(dve.tensor_tensor(mask[:, :, :], mask[:, :, :], oh[:, 2], ALU.add))
            link(dve.tensor_tensor(mask[:, :, :], mask[:, :, :], oh[:, 3], ALU.add))
            link(dve.tensor_copy(macc[:, 0, :], mask[:, 0, :]))
            for t in range(1, TT):
                ins = dve.tensor_tensor(macc[:, t, :], macc[:, t - 1, :], mask[:, t, :], ALU.add)
                if t < TT - 1:
                    link(ins)
            ins.then_inc(mask_ready, 1)
            dve.wait_ge(rank_done, 1)
            link(dve.tensor_copy(rk[:, :, :], PS[:, 7, 0:TT * NEXP].rearrange("p (t e) -> p t e", t=TT)))
            for k in range(TOPK):
                link(dve.tensor_tensor(oh[:, k], oh[:, k], rk[:, :, :], ALU.mult))
                link(dve.tensor_reduce(rkk[:, k, :], oh[:, k], AX_X, ALU.add))
                dve.scalar_tensor_tensor(slots[:, :].rearrange("p (t k) -> p t k", k=TOPK)[:, :, k], idxf[:, :, k], float(STRIDE),
                                         rkk[:, k, :], ALU.mult, ALU.add).then_inc(slots_ready, 1)
            counts = PS[:, 7, TT * NEXP:TT * NEXP + NEXP]
            fl = flags[:, :].rearrange("p (e r) -> p e r", r=ROUNDS)
            link(dve.tensor_copy(rk[:, 0, :], counts))
            link(dve.tensor_tensor(fl, rk[:, 0, :].unsqueeze(2).to_broadcast([P, NEXP, ROUNDS]),
                                   pairs[:, 0, :].rearrange("p (e r) -> p e r", r=ROUNDS), ALU.is_gt))
            link(dve.memset(picked[:, :], 1.0))
            link(dve.tensor_tensor_scan(posn[:, :], picked[:, :], flags[:, :], 0.0, ALU.mult, ALU.add))
            link(dve.tensor_copy(icol[:, 2:3], posn[:, PAIRS - 1:PAIRS]))
            link(dve.tensor_tensor(posn[:, :], posn[:, :], flags[:, :], ALU.subtract))
            link(dve.scalar_tensor_tensor(flags[:, :], posn[:, :], lane[:, 0:1], flags[:, :], ALU.is_equal, ALU.mult))
            for c in range(2):
                link(dve.tensor_tensor(picked[:, :], flags[:, :], pairs[:, 1 + c, :], ALU.mult))
                link(dve.tensor_reduce(icol[:, c:c + 1], picked[:, :], AX_X, ALU.add))
            dve.tensor_scalar(icol[:, 0:1], icol[:, 0:1], float(PAD_ROW), None, ALU.add).then_inc(icol_ready, 1)
            dve.wait_ge(items_mm, 1)
            for c in range(3):
                dve.tensor_copy(items[0:1, c, :], PS[0:1, 7, P * c:P * (c + 1)]).then_inc(items_ready, 1)
            dve.wait_ge(gexp, 1)
            link(dve.tensor_reduce(gsum[:, :], gts[:, :, :], AX_X, ALU.add))
            dve.reciprocal(gsum[:, :], gsum[:, :]).then_inc(dn_free, 1)
            dve.wait_ge(dn_free, 1)
            dve.tensor_tensor(gts[:, :, :], gts[:, :, :], gsum[:, :].unsqueeze(2).to_broadcast([P, TT, TOPK]),
                              ALU.mult).then_inc(gu_free, 1)

            dve.wait_ge(items_ready, 3)
            dve.wait_ge(bias_copied, 1)
            n = dve.value_load(items[0:1, 2, 0:1], min_val=NEXP, max_val=MAX_ITEMS)
            with dve.Fori(0, n) as i:
                e = dve.value_load(items[0:1, 1, bass.ds(i, 1)], min_val=0, max_val=NEXP - 1)
                dve.wait_ge(dn_free, 8 * i + 1)
                dve.tensor_copy(bcur[:, :], biasT[:, :, bass.ds(e, 1)].rearrange("p f a -> p (f a)")).then_inc(bcur_ready, 1)
                dve.wait_ge(bcur_ready, 2 * i + 1)
                dve.tensor_scalar(bcur[:, 8:16], bcur[:, 8:16], 1.0, None, ALU.add).then_inc(bcur_ready, 1)
                dve.wait_ge(bcur_ready, 2 * i + 2)
                for j in range(4):
                    bank = [PS[:, 2 * (j % 2) + f, :] for f in range(2)]
                    dve.wait_ge(gu_done, 4 * i + j + 1)
                    dve.tensor_scalar(gate[j % 2][:, 0, :], bank[0][:, 0:CAP], bcur[:, 2 * j:2 * j + 1], LIMIT, ALU.add, ALU.min)
                    dve.tensor_scalar(gate[j % 2][:, 1, :], bank[1][:, 0:CAP], bcur[:, 2 * j + 1:2 * j + 2], LIMIT,
                                      ALU.add, ALU.min).then_inc(g_ready, 1)
                    dve.tensor_scalar(up[j % 2][:, 0, :], bank[0][:, CAP:2 * CAP], bcur[:, 8 + 2 * j:9 + 2 * j], LIMIT + 1.0, ALU.add, ALU.min)
                    dve.tensor_scalar(up[j % 2][:, 1, :], bank[1][:, CAP:2 * CAP], bcur[:, 9 + 2 * j:10 + 2 * j], LIMIT + 1.0,
                                      ALU.add, ALU.min).then_inc(gu_free, 1)
                    dve.wait_ge(sig_ready, 4 * i + j + 1)
                    dve.wait_ge(gu_free, 4 * i + j + 2)
                    dve.tensor_tensor(sig[j % 2], sig[j % 2], gate[j % 2], ALU.mult).then_inc(act_ready, 1)
                    dve.wait_ge(act_ready, 8 * i + 2 * j + 1)
                    dve.scalar_tensor_tensor(actT[:, 2 * j:2 * j + 2, :], up[j % 2], 1.0 - LIMIT, sig[j % 2], ALU.max, ALU.mult).then_inc(act_ready, 1)

            for t in range(TT):
                dve.wait_ge(y_in[t % 2], 16 * (t // 2 + 1))
                y = yt[t % 2].rearrange("p (k d) -> p k d", k=TOPK)
                for k in range(TOPK):
                    ins = dve.scalar_tensor_tensor(H[:, t, :], y[:, k, :], gts[:, t, k:k + 1], H[:, t, :], ALU.mult, ALU.add)
                    if k < TOPK - 1:
                        link(ins)
                ins.then_inc(y_sum, 1)
                dve.wait_ge(oss_done, 2 * t + 2)
                link(dve.reciprocal(rs[:, t:t + 1], rs[:, t:t + 1]))
                if t == 0:
                    dve.wait_ge(wfb_in, 16)
                if t >= 2:
                    dve.wait_ge(o_out[t % 2], 16 * (t // 2))
                dve.scalar_tensor_tensor(ot[t % 2], H[:, t, :], rs[:, t:t + 1], wfb, ALU.mult, ALU.mult).then_inc(o_ready, 1)

        @block.tensor
        def _(pe):
            pe.wait_ge(consts_in, 16 * N_CONST)
            for f in range(24):
                rows = bgu_rows if f < 16 else bdn_rows
                at = P * (f % 16)
                mm = pe.transpose(pair(2)[:, NEXP * f:NEXP * (f + 1)], rows[:, at:at + P], ident[0:NEXP, 0:NEXP])
            mm.then_inc(bias_mm, 1)
            for c, (bank, at, a, b) in enumerate(((6, 0, 0, 512), (7, 0, 512, 1024), (5, 256, 1024, LROW))):
                if c == 2:
                    pe.wait_ge(bias_copied, 1)
                pe.matmul(PS[0:AH, bank, at:at + b - a], relb[:, :], onehot[:, a:b], start=True, stop=True).then_inc(lrow_mm, 1)
            for t in range(TT):
                pe.wait_ge(xs_ready, t + 1)
                if t >= 2:
                    pe.wait_ge(xnT_ready, t - 1)
                for k in range(KD):
                    mm = pe.transpose(pair(t % 2)[:, P * k:P * (k + 1)], xt[t % 2][:, P * k:P * (k + 1)], ident[:, :])
                mm.then_inc(xT_mm, 1)

            def project(g):
                c = g // 4
                kind, part = CHUNKS[c]
                w = win[c % 2]
                bank = PS[:, 6 + g % 2, :]
                if g % 4 == 0:
                    pe.wait_ge(w_in_sem[c % 2], 16 * (c // 2 + 1))
                if g == 0:
                    pe.wait_ge(xnT_ready, TT)
                    pe.wait_ge(lrow_sum, 3)
                if g >= 2:
                    pe.wait_ge(proj_out, g - 1)
                if kind in ("fh", "qh", "qa", "ka"):
                    ft, half = divmod(g % 4, 2)
                    for k in range(KD):
                        mm = pe.matmul(bank, w[:, k, P * ft:P * (ft + 1)], xnT[:, k, 512 * half:512 * half + 512],
                                       start=(k == 0), stop=(k == KD - 1))
                else:
                    for tt in range(2):
                        t = 2 * (g % 4) + tt
                        for k in range(KD):
                            mm = pe.matmul(bank[:, 256 * tt:256 * tt + 256], xnT[:, k, t * P:(t + 1) * P], w[:, k, :],
                                           start=(k == 0), stop=(k == KD - 1))
                mm.then_inc(proj_done, 1)

            def step(s):
                hd, j = divmod(s, STEPS)
                to = pair(s % 2)
                if s >= 2:
                    ph, pj = divmod(s - 2, STEPS)
                    if pj in (8, 11):
                        pe.wait_ge(h_act_out, 2 * ph + (1 if pj == 8 else 2))
                    else:
                        pe.wait_ge(h_dve_out, 10 * ph + {9: 9, 10: 10}.get(pj, pj + 1))
                if j == 0:
                    pe.wait_ge(h_k, hd + 1)
                    ops = [(b, [(FH[:, hd, P * b:P * (b + 1)], QH[:, hd, P * b:P * (b + 1)])]) for b in range(TT)]
                elif j <= 7:
                    pe.wait_ge(h_x, 9 * hd + j)
                    xx = X[(j - 1) % 2]
                    ops = [(b, [(xx[:, P * b:P * (b + 1)], xx[:, P * b:P * (b + 1)])]) for b in range(TT)]
                elif j == 8:
                    pe.wait_ge(h_x, 9 * hd + 8)
                    for b in range(TT):
                        mm = pe.transpose(to[:, P * b:P * (b + 1)], X[1][:, P * b:P * (b + 1)], ident[:, :])
                    ops = []
                elif j == 9:
                    pe.wait_ge(h_act_out, 2 * hd + 1)
                    pe.wait_ge(proj_out, 24)
                    ops = [(b, [(KT[:, P * b:P * (b + 1)], IH[:, b, P * hd:P * (hd + 1)])]) for b in range(TT)]
                elif j == 10:
                    pe.wait_ge(h_dve_out, 10 * hd + 9)
                    pe.wait_ge(h_x, 9 * hd + 9)
                    ops = [(b, [(A[:, P * b:P * (b + 1)], IH[:, b, P * hd:P * (hd + 1)])]
                            + ([(QD[:, P * b:P * (b + 1)], SA[:, P * b:P * (b + 1)])] if b else [])) for b in range(TT)]
                else:
                    pe.wait_ge(h_dve_out, 10 * hd + 10)
                    for b in range(TT):
                        mm = pe.transpose(to[:, P * b:P * (b + 1)], KT[:, P * b:P * (b + 1)], ident[:, :])
                    ops = []
                for b, products in ops:
                    for m, (lhs, rhs) in enumerate(products):
                        mm = pe.matmul(to[:, P * b:P * (b + 1)], lhs, rhs, start=(m == 0), stop=(m == len(products) - 1))
                mm.then_inc(h_step, 1)

            for what, n in SCHEDULE:
                project(n) if what == "group" else step(n)

            def scores(a):
                h, n = divmod(a, 8)
                b0 = HD * (h % 2)
                if a >= 2:
                    pe.wait_ge(att_m, a - 1)
                w = (n + 1) * P
                for at in range(0, w, 512):
                    end = min(w, at + 512)
                    mm = pe.matmul(pair(a % 2)[:, at:end], QA[b0:b0 + HD, h // 2, n * P:(n + 1) * P], KA[b0:b0 + HD, h // 2, at:end],
                                   start=True, stop=True)
                mm.then_inc(qk_done, 1)

            def transposes(a):
                pe.wait_ge(att_n, a + 1)
                if a >= 1:
                    pe.wait_ge(att_pt, a)
                for b in range(a % 8 + 1):
                    mm = pe.transpose(pair(2)[:, P * b:P * (b + 1)], SC[a % 3][:, P * b:P * (b + 1)], ident[:, :])
                mm.then_inc(tr_done, 1)

            def values(a):
                h, n = divmod(a, 8)
                b0 = HD * (h % 2)
                quad = a // 4
                pe.wait_ge(att_pt, a + 1)
                if a % 4 == 0 and quad >= 2:
                    pe.wait_ge(att_o, quad - 1)
                for b in range(n + 1):
                    mm = pe.matmul(PS[b0:b0 + HD, 6 + quad % 2, P * (a % 4):P * (a % 4 + 1)], VA[:, b, HD * h:HD * (h + 1)],
                                   PT[a % 2][:, P * b:P * (b + 1)], start=(b == 0), stop=(b == n))
                mm.then_inc(pv_done, 1)

            pe.wait_ge(proj_out, GROUPS)
            pe.wait_ge(h_act_out, 2 * GH_N)
            pe.wait_ge(h_dve_out, 10 * GH_N)
            scores(0)
            scores(1)
            for a in range(ITEMS_A):
                if a + 2 < ITEMS_A:
                    scores(a + 2)
                transposes(a)
                if a >= 1:
                    values(a - 1)
            values(ITEMS_A - 1)

            pe.wait_ge(att_o, ITEMS_A // 4)
            pe.wait_ge(wout_in, 32)

            def out_rows(t):
                if t >= 2:
                    pe.wait_ge(h_done, t - 1)
                for half in range(2):
                    for k in range(KD):
                        mix = QA if k < 4 else QH
                        mm = pe.matmul(pair(t % 2)[:, 512 * half:512 * (half + 1)], mix[:, k % 4, t * P:(t + 1) * P],
                                       wout[k // 4][:, k % 4, 512 * half:512 * (half + 1)], start=(k == 0), stop=(k == KD - 1))
                mm.then_inc(op_done, 1)

            def route(t):
                pe.wait_ge(xn2_ready, t + 1)
                if t >= 1:
                    pe.wait_ge(xn2T_ready, t)
                for k in range(KD):
                    mm = pe.transpose(pair(2)[:, P * k:P * (k + 1)], xn2[t % 2][:, P * k:P * (k + 1)], ident[:, :])
                mm.then_inc(xn2T_mm, 1)

            def logits(t):
                pe.wait_ge(xn2T_ready, t + 1)
                for k in range(KD):
                    mm = pe.matmul(PS[:, 6, NEXP * t:NEXP * (t + 1)], xn2T[t % 2][:, P * k:P * (k + 1)], rw[:, k, :],
                                   start=(k == 0), stop=(k == KD - 1))
                mm.then_inc(lg_done, 1)

            for t in range(TT + 2):
                if t < TT:
                    out_rows(t)
                if t >= 2:
                    logits(t - 2)
                if 1 <= t <= TT:
                    route(t - 1)
            pe.wait_ge(ones_set, 1)
            pe.wait_ge(mask_ready, 1)
            for t in range(TT):
                to = PS[:, 7, NEXP * t:NEXP * (t + 1)]
                pe.matmul(to, before[:, :], mask[:, t, :], start=True, stop=(t == 0))
                if t:
                    pe.matmul(to, ones[:, :], macc[:, t - 1, :], start=False, stop=True)
            pe.matmul(PS[:, 7, TT * NEXP:TT * NEXP + NEXP], ones[:, :], macc[:, TT - 1, :], start=True, stop=True).then_inc(rank_done, 1)
            pe.wait_ge(icol_ready, 1)
            for c in range(3):
                mm = pe.matmul(PS[0:1, 7, P * c:P * (c + 1)], icol[:, c:c + 1], ident[:, :], start=True, stop=True)
            mm.then_inc(items_mm, 1)

            def turn_x(r):
                for k in range(2 * r, 2 * r + 2):
                    at = CAP * (k % 2)
                    pe.transpose(PS[:, 6 + r % 2, at:at + P], xg[:, P * k:P * (k + 1)], ident[:, :])
                    mm = pe.transpose(PS[:, 6 + r % 2, at + P:at + CAP], xg2[:, P * k:P * (k + 1)], ident[0:32, 0:32])
                mm.then_inc(t_done, 1)

            pe.wait_ge(items_ready, 3)
            pe.wait_ge(xg_in, 32)
            for r in range(4):
                if r >= 2:
                    pe.wait_ge(t_free, r)
                turn_x(r)
            pe.wait_ge(t_free, 5)
            n = pe.value_load(items[0:1, 2, 0:1], min_val=NEXP, max_val=MAX_ITEMS)
            with pe.Fori(0, n) as i:
                for j in range(4):
                    pe.wait_ge(w_load[j], 32 * i + 32)
                    if j == 0:
                        pe.wait_ge(t_free, 8 * i + 1)
                    if j < 2:
                        pe.wait_ge(gu_free, 4 * i + 1)
                    else:
                        pe.wait_ge(gu_free, 4 * i + j)
                    for f in range(2):
                        for g in range(2):
                            to = PS[:, 2 * (j % 2) + f, CAP * g:CAP * (g + 1)]
                            for k in range(KD):
                                mm = pe.matmul(to, gu_w[j][:, g, k, P * f:P * (f + 1)], xT[:, k, :], start=(k == 0), stop=(k == KD - 1))
                    mm.then_inc(gu_done, 1)
                pe.wait_ge(xg_in, 32 * i + 64)
                for r in range(4):
                    pe.wait_ge(t_free, 8 * i + (5 if r < 2 else r + 4))
                    turn_x(r)
                for q in range(4):
                    if q % 2 == 0:
                        pe.wait_ge(w_load[4 + q // 2], 16 * i + 16)
                    if q == 0:
                        pe.wait_ge(act_ready, 8 * i + 8)
                    if q >= 2:
                        pe.wait_ge(dn_free, 8 * i + 2 * q - 1)
                    for f in range(2):
                        at = P * (2 * (q % 2) + f)
                        for k in range(KD):
                            mm = pe.matmul(PS[:, 4 + q % 2, CAP * f:CAP * (f + 1)], dn_w[q // 2][:, k, at:at + P], actT[:, k, :],
                                           start=(k == 0), stop=(k == KD - 1))
                    mm.then_inc(dn_done, 1)
                for g in range(2):
                    pe.wait_ge(dn_free, 8 * i + 4 * g + 5)
                    pe.wait_ge(t_free, 8 * i + (8 if g == 0 else 10))
                    for k in range(4):
                        mm = pe.transpose(PS[:, 6, P * k:P * (k + 1)], oT[:, 4 * g + k, 0:P], ident[:, :])
                    mm.then_inc(t_done, 1)
                    pe.wait_ge(t_free, 8 * i + (9 if g == 0 else 11))
                    for k in range(4):
                        mm = pe.transpose(PS[0:32, 7, P * k:P * (k + 1)], oT[:, 4 * g + k, P:CAP], ident[:, :])
                    mm.then_inc(t_done, 1)


_INS = ["x", "norm_mix_w", "w_in", "rel_bias", "hgrn_lb_logits", "hgrn_norm_w", "w_out", "norm_ffn_w", "router_w",
        "router_b", "w_gate_up", "b_gate_up", "w_down", "b_down", "final_norm_w"]


def kernel(**inputs):
    import numpy as _np
    import concourse.bacc as _bacc
    from concourse import mybir as _mybir
    from concourse.bass_utils import run_bass_kernel_spmd as _run

    nc = _bacc.Bacc("TRN2", target_bir_lowering=False, num_devices=1)
    arrays, args = {}, {}
    both = [(name, inputs[name]) for name in _INS] + list(constant_arrays().items())
    for name, a in both:
        a = _np.ascontiguousarray(a)
        arrays[f"in_{name}"] = a
        args[name] = nc.dram_tensor(f"in_{name}", a.shape, _mybir.dt.from_np(a.dtype), kind="ExternalInput").ap()
    out = nc.dram_tensor("out_0", (1, S, D), F32, kind="ExternalOutput").ap()
    build(nc, out=out, **args)
    r = _run(nc, [arrays], core_ids=[0])
    return r.results[0]["out_0"]
```

```python
from contextlib import ExitStack

import numpy as np

import concourse.bass as bass
from concourse import mybir

F32 = mybir.dt.float32
F16 = mybir.dt.float16
I32 = mybir.dt.int32
U32 = mybir.dt.uint32
U8 = mybir.dt.uint8
ALU = mybir.AluOpType
ACT = mybir.ActivationFunctionType
AX_X = mybir.AxisListType.X

P = 128
S = 1024
D = 1024
TT = S // P
KD = D // P
AH, HD = 8, 64
GH_N = 4
NEXP, TOPK = 32, 4
EPS = 1e-5
BUCKETS, MAX_DISTANCE = 32, 2048
PATTERNS = ((128, 1), (512, 4), (2048, 16))
NEG = -1e30

LEVELS = 7
STEPS = LEVELS + 5
LROW = S + P

CAP = 160
ROUNDS = -(-S // CAP)
STRIDE = ROUNDS * CAP
PAD_ROW = NEXP * STRIDE
TABLE = -(-(PAD_ROW + CAP) // P) * P
TABLE_P = TABLE * 2 // P
PAIRS = NEXP * ROUNDS
MAX_ITEMS = NEXP + S * TOPK // CAP
LIMIT, ALPHA = 7.0, 1.702

WS = 1024.0

COLUMN = {"qa": 0, "ka": 512, "va": 1024, "qh": 1536, "fh": 2048, "ih": 2560, "gh": 3072}
CHUNKS = [(kind, part) for kind in ("fh", "qh", "ih", "gh", "ka", "qa", "va") for part in range(2)]
EARLY = 8
GROUPS = 4 * len(CHUNKS)


def constant_arrays():
    i = np.arange(P)
    ident = np.eye(P, dtype=np.float32)
    before = (i[:, None] < i[None, :]).astype(np.float32)
    masks = np.zeros((P, LEVELS, P), np.float32)
    for level in range(LEVELS):
        h = 64 >> level
        same = (i[:, None] // (2 * h)) == (i[None, :] // (2 * h))
        masks[:, level] = same & ((i[:, None] // h) % 2 == 0) & ((i[None, :] // h) % 2 == 1)
    dist = S - 1 - np.arange(LROW)
    n = np.maximum(dist, 0)
    exact = BUCKETS // 2
    large = exact + (np.log(np.maximum(n, 1) / exact) / np.log(MAX_DISTANCE / exact)
                     * (BUCKETS - exact)).astype(np.int32)
    bucket = np.where(n < exact, n, np.minimum(large, BUCKETS - 1))
    times = sum(((dist >= 0) & (dist % d == 0) & (dist // d <= w // d)).astype(np.int64) for w, d in PATTERNS)
    onehot = ((bucket[None] == np.arange(BUCKETS)[:, None]) & (times > 0)[None]).astype(np.float32)
    log_times = np.where(times > 0, np.log(np.maximum(times, 1)), NEG).astype(np.float32)
    e, r = np.arange(PAIRS) // ROUNDS, np.arange(PAIRS) % ROUNDS
    pairs = np.stack([np.where(r > 0, CAP * r + 0.5, -0.5), (np.arange(PAIRS) - PAIRS) * CAP, e]).astype(np.float32)
    ids = np.zeros((P, TT, TOPK, 2), np.int32)
    tok = np.arange(TT)[None, :, None] * P + i[:, None, None]
    ids[..., 0] = tok * TOPK + np.arange(TOPK)
    ids[..., 1] = tok
    pad = np.tile(np.array([S * TOPK, S], np.int32), TABLE).reshape(P, TABLE_P)
    return {
        "c_ident": ident, "c_before": before, "c_masks": masks.reshape(P, LEVELS * P),
        "c_onehot": onehot, "c_times": log_times[None], "c_pairs": pairs.reshape(1, 3 * PAIRS),
        "c_lane": i[:, None].astype(np.float32), "c_experts": np.arange(NEXP, dtype=np.float32)[None],
        "c_ids": ids.reshape(P, -1), "c_pad": pad,
    }


def build(nc, x, norm_mix_w, w_in, rel_bias, hgrn_lb_logits, hgrn_norm_w, w_out, norm_ffn_w, router_w,
          router_b, w_gate_up, b_gate_up, w_down, b_down, final_norm_w, c_ident, c_before, c_masks,
          c_onehot, c_times, c_pairs, c_lane, c_experts, c_ids, c_pad, out):
    with ExitStack() as ctx:
        def sb(name, shape, dt=F32):
            return ctx.enter_context(nc.sbuf_tensor(name, shape, dt))

        def sem(name):
            return ctx.enter_context(nc.semaphore(name))

        ctx.enter_context(nc.allow_non_contiguous_dma(reason="small per-partition vectors"))

        RX = sb("RX", [P, 8192])
        RW = sb("RW", [P, 4096])
        RP = sb("RP", [P, 28672])
        RT = sb("RT", [P, 8704])

        xnT = RX[:, :].rearrange("p (k s) -> p k s", k=KD)
        win = [RW[:, 2048 * b:2048 * b + 2048].rearrange("p (k n) -> p k n", k=KD) for b in range(2)]
        region = {"qa": 0, "qh": 4096, "ka": 8192, "va": 12288, "gh": 16384, "fh": 20480, "ih": 24576}

        def by_feature(kind):
            return RP[:, region[kind]:region[kind] + 4096].rearrange("p (f s) -> p f s", f=4)

        def by_token(kind):
            return RP[:, region[kind]:region[kind] + 4096].rearrange("p (t n) -> p t n", t=TT)

        QA, KA, QH, FH = (by_feature(k) for k in ("qa", "ka", "qh", "fh"))
        VA, IH, GH = (by_token(k) for k in ("va", "ih", "gh"))

        xt = [RP[:, 16384 + 1024 * b:16384 + 1024 * (b + 1)] for b in range(2)]
        xsq = RP[:, 18432:19456]
        bgu_rows = RP[0:NEXP, 8192:10240]
        bdn_rows = RP[0:NEXP, 10240:11264]
        lrow = RP[0:AH, 12288:12288 + LROW]
        ltimes = RP[0:AH, 13440:13440 + LROW]
        onehot = RP[0:BUCKETS, 14592:14592 + LROW]

        masks_f = RT[:, 0:LEVELS * P]
        C = RT[:, 0:1024]
        DE = [RT[:, 1024:2048], RT[:, 2048:3072]]
        X = [RT[:, 3072:4096], RT[:, 4096:5120]]
        KT = RT[:, 5120:6144]
        QD = RT[:, 6144:7168]
        A = RT[:, 7168:8192]
        SA = X[1]
        BT = [RX[:, 1024 * b:1024 * (b + 1)] for b in range(2)]
        SC = [RX[:, 2048 + 1024 * b:2048 + 1024 * (b + 1)] for b in range(3)]
        PT = [RX[:, 5120 + 1024 * b:5120 + 1024 * (b + 1)] for b in range(2)]
        H = RX[:, :].rearrange("p (t d) -> p t d", t=TT)
        wout = [RP[:, region[k]:region[k] + 4096].rearrange("p (k n) -> p k n", k=4) for k in ("fh", "ih")]
        hsq = RW[:, 0:1024]
        xn2 = [RW[:, 1024:2048], RW[:, 2048:3072]]
        w2b = RW[:, 3072:4096]
        xn2T = [RT[:, 0:1024], RT[:, 1024:2048]]
        fresh = [RP[:, region[k]:region[k] + 4096].rearrange("p (k n) -> p k n", k=KD) for k in ("ka", "va", "gh")]
        halved = [RP[:, region[k]:region[k] + 4096].bitcast(F16).rearrange("p (m k n) -> p m k n", m=2, k=KD)
                  for k in ("fh", "ih", "qa")]

        def two(ap):
            return ap.bitcast(F16).rearrange("p (m k s) -> p m k s", m=2, k=KD)

        xT, actT = two(RT[:, 0:1280]), two(RT[:, 1280:2560])
        oT = RT[:, 2560:3840].rearrange("p (k s) -> p k s", k=KD)
        xg, xg2 = RT[:, 3840:4864], RT[0:32, 4864:5888]
        og, og2 = RT[:, 5888:6912], RT[0:32, 6912:7936]
        gate, up, sig, actf = ([RW[:, at + 320 * b:at + 320 * b + 320].rearrange("p (f s) -> p f s", f=2) for b in range(2)]
                               for at in (0, 640, 1280, 1920))
        yt = [RP[:, region[k]:region[k] + 4096] for k in ("fh", "ih")]
        last = RP[:, region["qa"]:region["qa"] + 4096]
        osq, wfb, ot = last[:, 0:1024], last[:, 1024:2048], [last[:, 2048:3072], last[:, 3072:4096]]

        ident, before, ones = sb("ident", [P, P]), sb("before", [P, P]), sb("ones", [P, P])
        masks = sb("masks", [P, LEVELS, P], U8)
        relb = sb("relb", [BUCKETS, AH])
        nmw, hnw = sb("nmw", [P, KD]), sb("hnw", [P, 1])
        lbl = sb("lbl", [P, 2, GH_N])
        lb, omlb, lbt = sb("lb", [P, GH_N]), sb("omlb", [P, GH_N]), sb("lbt", [P, 4, GH_N])
        rw = sb("rw", [P, KD, NEXP])
        rb = sb("rb", [P, NEXP])
        biasT = sb("biasT", [P, 24, NEXP])
        pairs = sb("pairs", [P, 3, PAIRS])
        lane = sb("lane", [P, 1])
        experts = sb("experts", [P, NEXP])
        ids = sb("ids", [P, TT * TOPK, 2], I32)
        ss, rs = sb("ss", [P, TT]), sb("rs", [P, TT])
        dl, hss, hrs = sb("dl", [P, TT]), sb("hss", [P, TT]), sb("hrs", [P, TT])
        am, az = sb("am", [P, 8 * AH]), sb("az", [P, 8 * AH])
        def spare(at, n):
            return RT[:, at:at + n]

        lg, mask, macc, rk = (spare(2048 + 256 * c, 256).rearrange("p (t e) -> p t e", t=TT) for c in range(4))
        flags, posn, picked = (spare(7936 + PAIRS * c, PAIRS) for c in range(3))
        oh = hsq.rearrange("p (k t e) -> p k t e", k=TOPK, t=TT)
        vals = sb("vals", [P, TT, 8])
        idx, idxf = sb("idx", [P, TT, 8], U32), sb("idxf", [P, TT, 8])
        rkk = sb("rkk", [P, TOPK, TT])
        slots = sb("slots", [P, TT * TOPK], I32)
        gts, gsum = sb("gts", [P, TT, TOPK]), sb("gsum", [P, TT])
        icol = sb("icol", [P, 3])
        items = sb("items", [1, 3, P], I32)
        bcur = sb("bcur", [P, 24])
        tok, tok2 = sb("tok", [P, 2], I32), sb("tok2", [32, 2], I32)
        dst, dst2 = sb("dst", [P, 1], I32), sb("dst2", [32, 1], I32)
        zero, idle = sb("zero", [P, 1], I32), sb("idle", [P, 2], I32)

        PS = ctx.enter_context(nc.psum_tensor("PS", [P, 8, 512], F32))

        def pair(n):
            return PS[:, 2 * n:2 * n + 2, :].rearrange("p b n -> p (b n)")

        lrow_dram = nc.dram_tensor("lrow_dram", [AH, LROW], F32)
        shifted_dram = nc.dram_tensor("shifted_dram", [AH, P, LROW], F32)
        xn_dram = nc.dram_tensor("xn_dram", [S, D], F32)
        table = nc.dram_tensor("table", [TABLE, 2], I32)
        y_dram = nc.dram_tensor("y_dram", [S * TOPK, D], F32)

        consts_in = sem("consts_in")
        x_in = [sem(f"x_in{b}") for b in range(2)]
        w_in_sem = [sem(f"win_in{b}") for b in range(2)]
        bt_in = [sem(f"bt_in{b}") for b in range(2)]
        wout_in, w2b_in, wfb_in = sem("wout_in"), sem("w2b_in"), sem("wfb_in")
        h_in = sem("h_in")
        ones_set, xg_set = sem("ones_set"), sem("xg_set")
        lrow_sum, lrow_out, lrow_mm, shifted_out = sem("lrow_sum"), sem("lrow_out"), sem("lrow_mm"), sem("shifted_out")
        bias_mm, bias_copied = sem("bias_mm"), sem("bias_copied")
        ss_done, rs_done = sem("ss_done"), sem("rs_done")
        xs_ready, xT_mm, xnT_ready = sem("xs_ready"), sem("xT_mm"), sem("xnT_ready")
        proj_done, proj_out = sem("proj_done"), sem("proj_out")
        h_f, h_g, h_k, h_d, h_e, h_x = (sem(n) for n in ("h_f", "h_g", "h_k", "h_d", "h_e", "h_x"))
        h_step, h_dve_out, h_act_out, h_sq, h_ss = (sem(n) for n in ("h_step", "h_dve_out", "h_act_out", "h_sq", "h_ss"))
        lb_exp, lb_sub = sem("lb_exp"), sem("lb_sub")
        qk_done, att_m, att_p, att_n = sem("qk_done"), sem("att_m"), sem("att_p"), sem("att_n")
        tr_done, att_pt, pv_done, att_o = sem("tr_done"), sem("att_pt"), sem("pv_done"), sem("att_o")
        op_done, h_done, hss_done, xn2_ready = sem("op_done"), sem("h_done"), sem("hss_done"), sem("xn2_ready")
        xn2_out = [sem(f"xn2_out{b}") for b in range(2)]
        xn2T_mm, xn2T_ready, lg_done = sem("xn2T_mm"), sem("xn2T_ready"), sem("lg_done")
        gexp_in, gexp, mask_ready, rank_done = sem("gexp_in"), sem("gexp"), sem("mask_ready"), sem("rank_done")
        slots_ready, icol_ready, items_mm, items_ready = (sem(n) for n in ("slots_ready", "icol_ready", "items_mm", "items_ready"))
        table_pad, table_in = sem("table_pad"), sem("table_in")
        w_load = [sem(f"w_load{c}") for c in range(3)]
        hi_done, lo_done = sem("hi_done"), sem("lo_done")
        gu_done, gu_free, sig_ready, prod_ready = (sem(n) for n in ("gu_done", "gu_free", "sig_ready", "prod_ready"))
        act_f, act_hi, act_lo = (sem(n) for n in ("act_f", "act_hi", "act_lo"))
        tok_in, xg_in, t_done, x_hi, x_lo, o_rows = (sem(n) for n in ("tok_in", "xg_in", "t_done", "x_hi", "x_lo", "o_rows"))
        dn_done, dn_free, bcur_ready, dst_copied, y_out = (sem(n) for n in ("dn_done", "dn_free", "bcur_ready", "dst_copied", "y_out"))
        dve_step, act_step, pool_step = sem("dve_step"), sem("act_step"), sem("pool_step")
        y_in = [sem(f"y_in{b}") for b in range(2)]
        y_sum, oss_done, o_ready = sem("y_sum"), sem("oss_done"), sem("o_ready")
        o_out = [sem(f"o_out{b}") for b in range(2)]

        N_CONST = 17
        X2 = x[0]
        SCHEDULE = [("group", g) for g in range(4 * EARLY)]
        late = GROUPS - 4 * EARLY
        for g in range(late):
            SCHEDULE.append(("group", 4 * EARLY + g))
            SCHEDULE += [("step", s) for s in range(g * GH_N * STEPS // late, (g + 1) * GH_N * STEPS // late)]
        ITEMS_A = 8 * AH

        block = ctx.enter_context(nc.Block())

        def load_w_in(sp, c):
            kind, part = CHUNKS[c]
            at = COLUMN[kind] + 256 * part
            sp.dma_start(win[c % 2], w_in[0, :, at:at + 256].rearrange("(k p) n -> p k n", p=P)).then_inc(w_in_sem[c % 2], 16)

        def load_expert_chunk(sp, e, c):
            wg = w_gate_up[0, bass.ds(e, 1)].rearrange("a (k p) n -> p (a k) n", p=P)
            wd = w_down[0, bass.ds(e, 1)].rearrange("a (k p) n -> p (a k) n", p=P)
            at = D * (c % 2) + 512 * (c // 2)
            src = wg[:, :, at:at + 512] if c < 4 else wd[:, :, 512 * (c - 4):512 * (c - 3)]
            sp.dma_start(fresh[c % 3], src).then_inc(w_load[c % 3], 16)

        @block.sync
        def _(sp):
            for dst_ap, src in (
                (ident[:, :], c_ident), (before[:, :], c_before), (masks_f, c_masks),
                (onehot, c_onehot), (ltimes, c_times[0, :].partition_broadcast(AH)), (relb[:, :], rel_bias),
                (nmw[:, :], norm_mix_w[0].rearrange("(k p) -> p k", p=P)),
                (hnw[:, :], hgrn_norm_w[0].rearrange("(p a) -> p a", a=1)),
                (lbl[:, :, :], hgrn_lb_logits.rearrange("l (h p) -> p l h", p=P)),
                (bgu_rows, b_gate_up[0]), (bdn_rows, b_down[0]),
                (rw[:, :, :], router_w[0].rearrange("(k p) e -> p k e", p=P)),
                (rb[:, :], router_b[0].partition_broadcast(P)),
                (pairs[:, :, :].rearrange("p a b -> p (a b)"), c_pairs[0, :].partition_broadcast(P)), (lane[:, :], c_lane),
                (experts[:, :], c_experts[0, :].partition_broadcast(P)),
                (ids[:, :, :].rearrange("p a b -> p (a b)"), c_ids),
            ):
                sp.dma_start(dst_ap, src).then_inc(consts_in, 16)
            sp.dma_start(table[:, :].rearrange("(p r) c -> p (r c)", p=P), c_pad).then_inc(table_pad, 16)
            for t in range(TT):
                if t >= 2:
                    sp.wait_ge(xT_mm, t - 1)
                sp.dma_start(xt[t % 2], X2[t * P:(t + 1) * P, :]).then_inc(x_in[t % 2], 16)
                if t < 2:
                    load_w_in(sp, t)
            for c in range(2, len(CHUNKS)):
                sp.wait_ge(proj_done, 4 * (c - 1))
                load_w_in(sp, c)
                if c == 5:
                    sp.wait_ge(lrow_out, 16)
                    for h in range(AH):
                        sp.dma_start(shifted_dram[h], lrow_dram[h, :].partition_broadcast(P)).then_inc(shifted_out, 16)
                if c == 3:
                    sp.wait_ge(lrow_sum, 3)
                    sp.dma_start(lrow_dram[:, :], lrow).then_inc(lrow_out, 16)
            sp.wait_ge(proj_done, GROUPS)
            sp.wait_ge(shifted_out, 16 * AH)
            for h in range(AH):
                if h >= 2:
                    sp.wait_ge(att_m, 8 * (h - 1))
                sp.dma_start(BT[h % 2], bass.AP(shifted_dram, h * P * LROW + P - 1, [[LROW - 1, P], [1, S]])).then_inc(bt_in[h % 2], 16)
                if h == 0:
                    sp.wait_ge(proj_out, GROUPS)
                    sp.dma_start(w2b, norm_ffn_w[0].partition_broadcast(P)).then_inc(w2b_in, 16)
                    sp.wait_ge(h_step, GH_N * STEPS)
                    for c in range(2):
                        sp.dma_start(wout[c], w_out[0, 512 * c:512 * (c + 1), :].rearrange("(k p) n -> p k n", p=P)).then_inc(wout_in, 16)
            sp.wait_ge(pv_done, ITEMS_A)
            sp.dma_start(H, X2.rearrange("(t p) d -> p t d", p=P)).then_inc(h_in, 16)
            sp.wait_ge(h_dve_out, 10 * GH_N)
            for c in range(3):
                load_expert_chunk(sp, 0, c)
            for t in range(TT):
                sp.wait_ge(xn2_ready, t + 1)
                sp.dma_start(xn_dram[t * P:(t + 1) * P, :], xn2[t % 2]).then_inc(xn2_out[t % 2], 16)
            sp.wait_ge(items_ready, 3)
            n = sp.value_load(items[0:1, 2, 0:1], min_val=NEXP, max_val=MAX_ITEMS)
            with sp.Fori(0, n) as i:
                now = sp.value_load(items[0:1, 1, bass.ds(i, 1)], min_val=0, max_val=NEXP - 1)
                after = sp.value_load(items[0:1, 1, bass.ds(i + 1, 1)], min_val=0, max_val=NEXP - 1)
                for c in range(3, 9):
                    sp.wait_ge(lo_done, 24 * i + 4 * (c - 2))
                    load_expert_chunk(sp, now if c < 6 else after, c % 6)
            sp.wait_ge(dn_done, 4 * n)
            sp.wait_ge(lo_done, 24 * n + 8)
            for c in range(3):
                sp.wait_ge(w_load[c], 32 * n + 16)
            sp.dma_start(wfb, final_norm_w.partition_broadcast(P)).then_inc(wfb_in, 16)
            sp.wait_ge(y_out, 32 * n)
            for t in range(TT):
                if t >= 2:
                    sp.wait_ge(y_sum, t - 1)
                sp.dma_start(yt[t % 2], y_dram[t * P * TOPK:(t + 1) * P * TOPK, :].rearrange("(p k) d -> p (k d)", k=TOPK)).then_inc(y_in[t % 2], 16)

        @block.gpsimd
        def _(pool):
            pool.memset(ones[:, :], 1.0).then_inc(ones_set, 1)
            pool.wait_ge(consts_in, 16 * N_CONST)
            pool.tensor_copy(masks[:, :, :].rearrange("p l t -> p (l t)"), masks_f).then_inc(ones_set, 1)
            pool.wait_ge(table_pad, 16)
            pool.wait_ge(h_step, GH_N * STEPS)
            pool.wait_ge(h_dve_out, 10 * GH_N)
            pool.wait_ge(h_act_out, 2 * GH_N)
            pool.memset(zero[:, :], 0).then_inc(o_rows, 1)
            pool.memset(xg, 0.0).then_inc(xg_set, 1)
            pool.memset(xg2, 0.0).then_inc(xg_set, 1)
            pool.wait_ge(slots_ready, 4)
            for j in range(TT * TOPK):
                pool.indirect_dma_start(
                    table[:, :], bass.IndirectOffsetOnAxis(ap=slots[:, j:j + 1], axis=0),
                    ids[:, j, :], None, bounds_check=PAD_ROW - 1, oob_is_err=False).then_inc(table_in, 16)
            pool.wait_ge(table_in, 16 * TT * TOPK)
            for b in range(2):
                pool.wait_ge(xn2_out[b], 16 * TT // 2)
            pool.wait_ge(items_ready, 3)
            pool.wait_ge(xg_set, 2)
            pool.wait_ge(o_rows, 1)

            last_row, last_place = pool.to_reg(S - 1), pool.to_reg(S * TOPK - 1)

            def load_tokens(at):
                pool.dma_start(tok[:, :], table[bass.ds(at, P), :]).then_inc(tok_in, 16)
                pool.dma_start(tok2[:, :], table[bass.ds(at + P, 32), :]).then_inc(tok_in, 16)

            def gather():
                pool.indirect_dma_start(xg, None, xn_dram[:, :], bass.IndirectOffsetOnAxis(ap=tok[:, 1:2], axis=0),
                                        bounds_check=last_row, oob_is_err=False).then_inc(xg_in, 16)
                pool.indirect_dma_start(xg2, None, xn_dram[:, :], bass.IndirectOffsetOnAxis(ap=tok2[:, 1:2], axis=0),
                                        bounds_check=last_row, oob_is_err=False).then_inc(xg_in, 16)

            load_tokens(pool.value_load(items[0:1, 0, 0:1], min_val=0, max_val=PAD_ROW))
            pool.wait_ge(tok_in, 32)
            gather()
            n = pool.value_load(items[0:1, 2, 0:1], min_val=NEXP, max_val=MAX_ITEMS)
            with pool.Fori(0, n) as i:
                at = pool.value_load(items[0:1, 0, bass.ds(i + 1, 1)], min_val=0, max_val=PAD_ROW)
                pool.tensor_tensor(dst[:, :], tok[:, 0:1], zero[:, :], ALU.add).then_inc(dst_copied, 1)
                pool.tensor_tensor(dst2[:, :], tok2[:, 0:1], zero[0:32, :], ALU.add).then_inc(dst_copied, 1)
                pool.wait_ge(dst_copied, 2 * i + 2)
                pool.wait_ge(xg_in, 32 * i + 32)
                load_tokens(at)
                pool.wait_ge(tok_in, 32 * i + 64)
                pool.wait_ge(t_done, 8 * i + 4)
                pool.tensor_tensor(idle[:, 0:1], zero[:, :], zero[:, :], ALU.add)
                gather()
                pool.wait_ge(o_rows, 4 * i + 5)
                pool.tensor_tensor(idle[:, 1:2], zero[:, :], zero[:, :], ALU.add)
                pool.indirect_dma_start(y_dram[:, :], bass.IndirectOffsetOnAxis(ap=dst[:, 0:1], axis=0), og, None,
                                        bounds_check=last_place, oob_is_err=False).then_inc(y_out, 16)
                pool.indirect_dma_start(y_dram[:, :], bass.IndirectOffsetOnAxis(ap=dst2[:, 0:1], axis=0), og2, None,
                                        bounds_check=last_place, oob_is_err=False).then_inc(y_out, 16)
                pool.wait_ge(y_out, 32 * i + 32)
            pool.wait_ge(xg_in, 32 * n + 32)

        @block.scalar
        def _(act):
            act.wait_ge(consts_in, 16 * N_CONST)
            act.wait_ge(lb_sub, 1)
            act.activation(lbt[:, 2:4, :], lbt[:, 0:2, :], ACT.Exp).then_inc(lb_exp, 1)
            act.wait_ge(bias_mm, 1)
            act.activation(biasT[:, 0:16, :].rearrange("p f e -> p (f e)"), pair(2)[:, 0:16 * NEXP], ACT.Copy, scale=WS)
            act.activation(biasT[:, 16:24, :].rearrange("p f e -> p (f e)"), pair(2)[:, 16 * NEXP:24 * NEXP], ACT.Copy).then_inc(bias_copied, 1)
            for t in range(TT):
                act.wait_ge(x_in[t % 2], 16 * (t // 2 + 1))
                if t >= 1:
                    act.wait_ge(ss_done, 2 * t)
                act.activation(xsq, xt[t % 2], ACT.Square, accum_out=ss[:, t:t + 1]).then_inc(ss_done, 1)
                act.wait_ge(ss_done, 2 * t + 1)
                act.activation(rs[:, t:t + 1], ss[:, t:t + 1], ACT.Sqrt, scale=1.0 / D, bias=EPS).then_inc(ss_done, 1)

            def evacuate(g):
                kind, part = CHUNKS[g // 4]
                act.wait_ge(proj_done, g + 1)
                bank = PS[:, 6 + g % 2, :]
                if kind in ("fh", "qh", "qa", "ka"):
                    ft, half = divmod(g % 4, 2)
                    to, src = by_feature(kind)[:, 2 * part + ft, 512 * half:512 * half + 512], bank
                else:
                    t = 2 * (g % 4)
                    to = by_token(kind)[:, t:t + 2, 256 * part:256 * part + 256]
                    src = bank.rearrange("p (t n) -> p t n", t=2)
                func = {"fh": ACT.Sigmoid, "qh": ACT.Silu, "gh": ACT.Silu}.get(kind, ACT.Copy)
                act.activation(to, src, func, scale=HD ** -0.5 if kind == "qa" else 1.0).then_inc(proj_out, 1)

            def decay(hd, m):
                act.wait_ge(h_d, 9 * hd + m + 2)
                act.activation(DE[m % 2], DE[m % 2], ACT.Exp).then_inc(h_e, 1)

            def head_start(hd):
                act.wait_ge(h_f, hd + 1)
                if hd:
                    act.wait_ge(h_x, 9 * hd)
                act.activation(DE[0], FH[:, hd, :], ACT.Ln).then_inc(h_g, 1)
                decay(hd, 0)
                decay(hd, 1)

            def step(s):
                hd, j = divmod(s, STEPS)
                if s == 0:
                    head_start(0)
                if 1 <= j <= 6:
                    decay(hd, j + 1)
                if j == 7:
                    act.activation(dl[:, :], C.rearrange("p (b t) -> p b t", b=TT)[:, :, P - 1], ACT.Exp).then_inc(h_e, 1)
                    act.wait_ge(h_x, 9 * hd + 7)
                    act.activation(DE[0], C, ACT.Exp).then_inc(h_e, 1)
                if j == 8:
                    act.wait_ge(h_step, s + 1)
                    act.activation(KT, pair(s % 2), ACT.Copy).then_inc(h_act_out, 1)
                    if hd + 1 < GH_N:
                        head_start(hd + 1)
                if j == 10:
                    act.wait_ge(h_step, s + 1)
                    act.activation(A, pair(s % 2), ACT.Square).then_inc(h_sq, 1)
                    act.wait_ge(h_ss, hd + 1)
                    act.activation(hrs[:, :], hss[:, :], ACT.Sqrt, scale=1.0 / P, bias=EPS * P).then_inc(h_sq, 1)
                if j == 11:
                    act.wait_ge(h_step, s + 1)
                    act.activation(QH[:, hd, :], pair(s % 2), ACT.Copy, scale=hnw[:, 0:1]).then_inc(h_act_out, 1)

            for what, n in SCHEDULE:
                evacuate(n) if what == "group" else step(n)

            def put_pt(a):
                w = (a % 8 + 1) * P
                act.wait_ge(tr_done, a + 1)
                if a >= 2:
                    act.wait_ge(pv_done, a - 1)
                act.activation(PT[a % 2][:, 0:w], pair(2)[:, 0:w], ACT.Copy).then_inc(att_pt, 1)

            for a in range(ITEMS_A):
                w = (a % 8 + 1) * P
                act.wait_ge(att_m, a + 1)
                act.activation(SC[a % 3][:, 0:w], SC[a % 3][:, 0:w], ACT.Exp, bias=am[:, a:a + 1],
                               accum_out=az[:, a:a + 1]).then_inc(att_p, 1)
                if a >= 1:
                    put_pt(a - 1)
            put_pt(ITEMS_A - 1)

            def put_xn2T(t):
                act.wait_ge(xn2T_mm, t + 1)
                if t >= 2:
                    act.wait_ge(lg_done, t - 1)
                act.activation(xn2T[t % 2], pair(2), ACT.Copy).then_inc(xn2T_ready, 1)

            for t in range(TT):
                act.wait_ge(h_done, t + 1)
                if t >= 1:
                    act.wait_ge(hss_done, 2 * t)
                act.activation(hsq, H[:, t, :], ACT.Square, accum_out=ss[:, t:t + 1]).then_inc(hss_done, 1)
                act.wait_ge(hss_done, 2 * t + 1)
                act.activation(rs[:, t:t + 1], ss[:, t:t + 1], ACT.Sqrt, scale=1.0 / D, bias=EPS).then_inc(hss_done, 1)
                if t >= 1:
                    put_xn2T(t - 1)
            put_xn2T(TT - 1)
            act.wait_ge(gexp_in, 1)
            act.activation(gts[:, :, :], gts[:, :, :], ACT.Exp).then_inc(gexp, 1)

            def halve(i, c, quarters=range(4)):
                to, src = halved[c % 3], fresh[c % 3]
                for q in quarters:
                    if q == 0:
                        act.wait_ge(w_load[c % 3], 32 * i + 16 * (c // 3) + 16)
                        if 3 <= c <= 6:
                            act.wait_ge(gu_done, 8 * i + 2 * c - 4)
                        if c == 7:
                            act.wait_ge(dn_done, 4 * i + 2)
                    act.activation(to[:, 0, 2 * q:2 * q + 2, :], src[:, 2 * q:2 * q + 2, :], ACT.Copy, scale=WS).then_inc(hi_done, 1)

            def put_x(i, r):
                act.wait_ge(t_done, 8 * i + r + 5 if i is not None else r + 1)
                act.activation(xT[:, 0, 2 * r:2 * r + 2, :], PS[:, 6 + r % 2, 0:2 * CAP].rearrange("p (k s) -> p k s", k=2),
                               ACT.Copy).then_inc(x_hi, 1)

            act.wait_ge(op_done, TT)
            halve(0, 0)
            halve(0, 1)
            act.wait_ge(items_ready, 3)
            for r in range(4):
                put_x(None, r)
            n = act.value_load(items[0:1, 2, 0:1], min_val=NEXP, max_val=MAX_ITEMS)
            with act.Fori(0, n) as i:
                def sigmoid(half, b):
                    act.wait_ge(gu_free, 8 * i + 4 * half + b + 2)
                    act.activation(sig[b], gate[b], ACT.Sigmoid, scale=ALPHA / WS).then_inc(sig_ready, 1)

                def act_half(half, b):
                    k = 4 * half + 2 * b
                    act.wait_ge(act_f, 4 * i + 2 * half + b + 1)
                    act.activation(actT[:, 0, k:k + 2, :], actf[b], ACT.Copy).then_inc(act_hi, 1)

                def put_o(q):
                    act.wait_ge(dn_done, 4 * i + q + 1)
                    for f in range(2):
                        act.activation(oT[:, 2 * q + f, :], PS[:, 4 + q % 2, CAP * f:CAP * (f + 1)], ACT.Identity,
                                       bias=bcur[:, 16 + 2 * q + f:17 + 2 * q + f], scale=1.0 / WS).then_inc(dn_free, 1)

                halve(i, 2)
                halve(i, 3, (0, 1))
                sigmoid(0, 0)
                halve(i, 3, (2,))
                sigmoid(0, 1)
                halve(i, 3, (3,))
                act_half(0, 0)
                halve(i, 4, (0,))
                act_half(0, 1)
                halve(i, 4, (1, 2, 3))
                halve(i, 5, (0,))
                sigmoid(1, 0)
                halve(i, 5, (1,))
                sigmoid(1, 1)
                halve(i, 5, (2,))
                act_half(1, 0)
                halve(i, 5, (3,))
                act_half(1, 1)
                for r in range(4):
                    put_x(i, r)
                halve(i, 6, (0, 1))
                put_o(0)
                halve(i, 6, (2, 3))
                put_o(1)
                halve(i, 7, (0, 1))
                put_o(2)
                halve(i, 7, (2, 3))
                put_o(3)
                act.wait_ge(dst_copied, 2 * i + 2)
                for g in range(2):
                    act.wait_ge(t_done, 8 * i + 2 * g + 9)
                    act.activation(og[:, 512 * g:512 * (g + 1)], PS[:, 6, :], ACT.Copy).then_inc(o_rows, 1)
                    act.wait_ge(t_done, 8 * i + 2 * g + 10)
                    act.activation(og2[:, 512 * g:512 * (g + 1)], PS[0:32, 7, :], ACT.Copy).then_inc(o_rows, 1)

            for t in range(TT):
                act.wait_ge(y_sum, t + 1)
                if t >= 1:
                    act.wait_ge(oss_done, 2 * t)
                act.activation(osq, H[:, t, :], ACT.Square, accum_out=ss[:, t:t + 1]).then_inc(oss_done, 1)
                act.wait_ge(oss_done, 2 * t + 1)
                act.activation(rs[:, t:t + 1], ss[:, t:t + 1], ACT.Sqrt, scale=1.0 / D, bias=EPS).then_inc(oss_done, 1)
                act.wait_ge(o_ready, t + 1)
                act.dma_start(out[0, t * P:(t + 1) * P, :], ot[t % 2]).then_inc(o_out[t % 2], 16)
            for b in range(2):
                act.wait_ge(o_out[b], 16 * TT // 2)

        @block.vector
        def _(dve):
            steps = [0]

            def link(ins):
                steps[0] += 1
                ins.then_inc(dve_step, 1)
                dve.wait_ge(dve_step, steps[0])

            dve.wait_ge(consts_in, 16 * N_CONST)
            link(dve.tensor_tensor(lbt[:, 2, :], lbl[:, 0, :], lbl[:, 1, :], ALU.max))
            link(dve.tensor_tensor(lbt[:, 0, :], lbl[:, 0, :], lbt[:, 2, :], ALU.subtract))
            dve.tensor_tensor(lbt[:, 1, :], lbl[:, 1, :], lbt[:, 2, :], ALU.subtract).then_inc(lb_sub, 1)
            dve.wait_ge(lb_exp, 1)
            link(dve.tensor_tensor(lbt[:, 0, :], lbt[:, 2, :], lbt[:, 3, :], ALU.add))
            link(dve.reciprocal(lbt[:, 1, :], lbt[:, 0, :]))
            link(dve.tensor_tensor(lb[:, :], lbt[:, 2, :], lbt[:, 1, :], ALU.mult))
            link(dve.tensor_scalar(omlb[:, :], lb[:, :], -1.0, 1.0, ALU.mult, ALU.add))
            for c, (bank, at, a, b) in enumerate(((6, 0, 0, 512), (7, 0, 512, 1024), (5, 256, 1024, LROW))):
                dve.wait_ge(lrow_mm, c + 1)
                dve.tensor_tensor(lrow[:, a:b], PS[0:AH, bank, at:at + b - a], ltimes[:, a:b], ALU.add).then_inc(lrow_sum, 1)
            for t in range(TT):
                dve.wait_ge(ss_done, 2 * t + 2)
                link(dve.reciprocal(rs[:, t:t + 1], rs[:, t:t + 1]))
                dve.tensor_scalar(xt[t % 2], xt[t % 2], rs[:, t:t + 1], None, ALU.mult).then_inc(xs_ready, 1)
                dve.wait_ge(xT_mm, t + 1)
                dve.tensor_tensor(xnT[:, :, t * P:(t + 1) * P], pair(t % 2).rearrange("p (k s) -> p k s", k=KD),
                                  nmw[:, :].unsqueeze(2).to_broadcast([P, KD, P]), ALU.mult).then_inc(xnT_ready, 1)

            def halves(ap, m):
                h = 64 >> m
                v = ap.rearrange("p (n two h) -> p n two h", two=2, h=h)
                return v[:, :, 0, :], v[:, :, 1, :], v[:, :, 0, h - 1:h].to_broadcast([P, S // (2 * h), h])

            Cb = C.rearrange("p (b t) -> p b t", b=TT)

            def difference(hd, m):
                d = DE[m % 2]
                if m < LEVELS:
                    left, right, mid = halves(C, m)
                    dl_, dr_, _ = halves(d, m)
                    link(dve.tensor_tensor(dl_, mid, left, ALU.subtract))
                    dve.tensor_tensor(dr_, right, mid, ALU.subtract).then_inc(h_d, 1)
                else:
                    dve.tensor_tensor(d.rearrange("p (b t) -> p b t", b=TT), Cb[:, :, P - 1:P].to_broadcast([P, TT, P]), Cb,
                                      ALU.subtract).then_inc(h_d, 1)

            def scaled(hd, m):
                if m < 8:
                    dve.wait_ge(h_e, 10 * hd + m + 1)
                    if m >= 2:
                        dve.wait_ge(h_step, STEPS * hd + m)
                    elif hd:
                        dve.wait_ge(h_step, STEPS * (hd - 1) + (9 if m == 0 else 11))
                if m < LEVELS:
                    el, er, _ = halves(DE[m % 2], m)
                    xl, xr, _ = halves(X[m % 2], m)
                    kl, _, _ = halves(FH[:, hd, :], m)
                    _, qr, _ = halves(QH[:, hd, :], m)
                    link(dve.tensor_tensor(xl, el, kl, ALU.mult))
                    dve.tensor_tensor(xr, er, qr, ALU.mult).then_inc(h_x, 1)
                elif m == 7:
                    dve.tensor_tensor(X[1], DE[1], FH[:, hd, :], ALU.mult).then_inc(h_x, 1)
                else:
                    dve.wait_ge(h_e, 10 * hd + 10)
                    dve.tensor_tensor(QD, DE[0], QH[:, hd, :], ALU.mult).then_inc(h_x, 1)

            def head_start(hd):
                link(dve.tensor_scalar(FH[:, hd, :], FH[:, hd, :], omlb[:, hd:hd + 1], lb[:, hd:hd + 1], ALU.mult, ALU.add))
                dve.tensor_copy(lbt[:, 0, :], lb[:, :]).then_inc(h_f, 1)
                dve.wait_ge(h_g, hd + 1)
                dve.tensor_scalar(FH[:, hd, :], FH[:, hd, :], -1.0, 1.0, ALU.mult, ALU.add).then_inc(h_k, 1)
                for b in range(TT):
                    ins = dve.tensor_tensor_scan(Cb[:, b, :], ones[:, :], DE[0][:, b * P:(b + 1) * P], 0.0, ALU.mult, ALU.add)
                ins.then_inc(h_d, 1)
                dve.wait_ge(h_d, 9 * hd + 1)
                difference(hd, 0)
                difference(hd, 1)
                scaled(hd, 0)

            def step(s):
                hd, j = divmod(s, STEPS)
                if s == 0:
                    dve.wait_ge(proj_out, 16)
                    dve.wait_ge(ones_set, 2)
                    head_start(0)
                if 1 <= j <= 7:
                    dve.wait_ge(h_x, 9 * hd + j)
                    if j + 1 <= 7:
                        difference(hd, j + 1)
                    scaled(hd, j)
                    if j == 7:
                        scaled(hd, 8)
                if j <= 7:
                    dve.wait_ge(h_step, s + 1)
                    to = A.rearrange("p (b t) -> p b t", b=TT)
                    src = pair(s % 2).rearrange("p (b t) -> p b t", b=TT)
                    if j == 0:
                        ins = dve.tensor_tensor(to, src, ident[:, :].unsqueeze(1).to_broadcast([P, TT, P]), ALU.mult)
                    else:
                        dve.wait_ge(h_dve_out, 10 * hd + j)
                        ins = dve.copy_predicated(to, masks[:, j - 1, :].unsqueeze(1).to_broadcast([P, TT, P]), src)
                    ins.then_inc(h_dve_out, 1)
                if j == 8 and hd + 1 < GH_N:
                    dve.wait_ge(h_x, 9 * hd + 9)
                    head_start(hd + 1)
                if j == 9:
                    dve.wait_ge(h_step, s + 1)
                    dve.wait_ge(h_e, 10 * hd + 9)
                    sa = SA.rearrange("p (b v) -> p b v", b=TT)
                    su = pair(s % 2).rearrange("p (b v) -> p b v", b=TT)
                    link(dve.tensor_copy(sa[:, 1, :], su[:, 0, :]))
                    for b in range(1, TT - 1):
                        ins = dve.scalar_tensor_tensor(sa[:, b + 1, :], sa[:, b, :], dl[:, b:b + 1], su[:, b, :], ALU.mult, ALU.add)
                        if b < TT - 2:
                            link(ins)
                    ins.then_inc(h_dve_out, 1)
                if j == 10:
                    dve.wait_ge(h_sq, 2 * hd + 1)
                    dve.tensor_reduce(hss[:, :], A.rearrange("p (b v) -> p b v", b=TT), AX_X, ALU.add).then_inc(h_ss, 1)
                    dve.wait_ge(h_sq, 2 * hd + 2)
                    link(dve.reciprocal(hrs[:, :], hrs[:, :]))
                    o = KT.rearrange("p (b v) -> p b v", b=TT)
                    link(dve.tensor_tensor(o, pair(s % 2).rearrange("p (b v) -> p b v", b=TT),
                                           hrs[:, :].unsqueeze(2).to_broadcast([P, TT, P]), ALU.mult))
                    dve.tensor_tensor(o, o, GH[:, :, P * hd:P * (hd + 1)], ALU.mult).then_inc(h_dve_out, 1)

            for what, n in SCHEDULE:
                if what == "step":
                    if n % STEPS == 10:
                        dve.wait_ge(proj_out, 4 * EARLY)
                    step(n)

            def normalise(a):
                w = (a % 8 + 1) * P
                dve.wait_ge(att_p, a + 1)
                link(dve.reciprocal(az[:, a:a + 1], az[:, a:a + 1]))
                dve.tensor_scalar(SC[a % 3][:, 0:w], SC[a % 3][:, 0:w], az[:, a:a + 1], None, ALU.mult).then_inc(att_n, 1)

            def put_o(quad):
                h, at, b0 = quad // 2, 512 * (quad % 2), HD * ((quad // 2) % 2)
                dve.wait_ge(pv_done, 4 * quad + 4)
                dve.tensor_copy(QA[b0:b0 + HD, h // 2, at:at + 512], PS[b0:b0 + HD, 6 + quad % 2, :]).then_inc(att_o, 1)

            for a in range(ITEMS_A + 2):
                h, n = divmod(a, 8)
                w = (n + 1) * P
                if a < ITEMS_A:
                    dve.wait_ge(qk_done, a + 1)
                    dve.wait_ge(bt_in[h % 2], 16 * (h // 2 + 1))
                    if a >= 3:
                        dve.wait_ge(tr_done, a - 2)
                    link(dve.tensor_tensor_reduce(SC[a % 3][:, 0:w], pair(a % 2)[:, 0:w], BT[h % 2][:, S - w:S], 1.0, -3e38,
                                                  ALU.add, ALU.max, am[:, a:a + 1]))
                    dve.tensor_scalar(am[:, a:a + 1], am[:, a:a + 1], -1.0, None, ALU.mult).then_inc(att_m, 1)
                if 1 <= a <= ITEMS_A:
                    normalise(a - 1)
                if a % 4 == 1 and a >= 5:
                    put_o((a - 5) // 4)

            dve.wait_ge(h_in, 16)
            dve.wait_ge(w2b_in, 16)

            def norm_rows(t):
                dve.wait_ge(hss_done, 2 * t + 2)
                link(dve.reciprocal(rs[:, t:t + 1], rs[:, t:t + 1]))
                if t >= 2:
                    dve.wait_ge(xn2_out[t % 2], 16 * (t // 2))
                    dve.wait_ge(xn2T_mm, t - 1)
                dve.scalar_tensor_tensor(xn2[t % 2], H[:, t, :], rs[:, t:t + 1], w2b, ALU.mult, ALU.mult).then_inc(xn2_ready, 1)

            for t in range(TT):
                dve.wait_ge(op_done, t + 1)
                dve.tensor_tensor(H[:, t, :], pair(t % 2), H[:, t, :], ALU.add).then_inc(h_done, 1)
                if t >= 1:
                    norm_rows(t - 1)
            norm_rows(TT - 1)

            dve.wait_ge(lg_done, TT)
            link(dve.tensor_tensor(lg[:, :, :], PS[:, 6, 0:TT * NEXP].rearrange("p (t e) -> p t e", t=TT),
                                   rb[:, :].unsqueeze(1).to_broadcast([P, TT, NEXP]), ALU.add))
            for t in range(TT):
                link(dve.max(vals[:, t, :], lg[:, t, :]))
                link(dve.max_index(idx[:, t, :], vals[:, t, :], lg[:, t, :]))
            link(dve.tensor_copy(idxf[:, :, :], idx[:, :, :]))
            dve.tensor_tensor(gts[:, :, :], vals[:, :, 0:TOPK], vals[:, :, 0:1].to_broadcast([P, TT, TOPK]),
                              ALU.subtract).then_inc(gexp_in, 1)
            for k in range(TOPK):
                link(dve.tensor_tensor(oh[:, k], experts[:, :].unsqueeze(1).to_broadcast([P, TT, NEXP]),
                                       idxf[:, :, k:k + 1].to_broadcast([P, TT, NEXP]), ALU.is_equal))
            link(dve.tensor_tensor(mask[:, :, :], oh[:, 0], oh[:, 1], ALU.add))
            link(dve.tensor_tensor(mask[:, :, :], mask[:, :, :], oh[:, 2], ALU.add))
            link(dve.tensor_tensor(mask[:, :, :], mask[:, :, :], oh[:, 3], ALU.add))
            link(dve.tensor_copy(macc[:, 0, :], mask[:, 0, :]))
            for t in range(1, TT):
                ins = dve.tensor_tensor(macc[:, t, :], macc[:, t - 1, :], mask[:, t, :], ALU.add)
                if t < TT - 1:
                    link(ins)
            ins.then_inc(mask_ready, 1)
            dve.wait_ge(rank_done, 1)
            link(dve.tensor_copy(rk[:, :, :], PS[:, 7, 0:TT * NEXP].rearrange("p (t e) -> p t e", t=TT)))
            for k in range(TOPK):
                link(dve.tensor_tensor(oh[:, k], oh[:, k], rk[:, :, :], ALU.mult))
                link(dve.tensor_reduce(rkk[:, k, :], oh[:, k], AX_X, ALU.add))
                dve.scalar_tensor_tensor(slots[:, :].rearrange("p (t k) -> p t k", k=TOPK)[:, :, k], idxf[:, :, k], float(STRIDE),
                                         rkk[:, k, :], ALU.mult, ALU.add).then_inc(slots_ready, 1)
            counts = PS[:, 7, TT * NEXP:TT * NEXP + NEXP]
            fl = flags[:, :].rearrange("p (e r) -> p e r", r=ROUNDS)
            link(dve.tensor_copy(rk[:, 0, :], counts))
            link(dve.tensor_tensor(fl, rk[:, 0, :].unsqueeze(2).to_broadcast([P, NEXP, ROUNDS]),
                                   pairs[:, 0, :].rearrange("p (e r) -> p e r", r=ROUNDS), ALU.is_gt))
            link(dve.memset(picked[:, :], 1.0))
            link(dve.tensor_tensor_scan(posn[:, :], picked[:, :], flags[:, :], 0.0, ALU.mult, ALU.add))
            link(dve.tensor_copy(icol[:, 2:3], posn[:, PAIRS - 1:PAIRS]))
            link(dve.tensor_tensor(posn[:, :], posn[:, :], flags[:, :], ALU.subtract))
            link(dve.scalar_tensor_tensor(flags[:, :], posn[:, :], lane[:, 0:1], flags[:, :], ALU.is_equal, ALU.mult))
            for c in range(2):
                link(dve.tensor_tensor(picked[:, :], flags[:, :], pairs[:, 1 + c, :], ALU.mult))
                link(dve.tensor_reduce(icol[:, c:c + 1], picked[:, :], AX_X, ALU.add))
            dve.tensor_scalar(icol[:, 0:1], icol[:, 0:1], float(PAD_ROW), None, ALU.add).then_inc(icol_ready, 1)
            dve.wait_ge(items_mm, 1)
            for c in range(3):
                dve.tensor_copy(items[0:1, c, :], PS[0:1, 7, P * c:P * (c + 1)]).then_inc(items_ready, 1)
            dve.wait_ge(gexp, 1)
            link(dve.tensor_reduce(gsum[:, :], gts[:, :, :], AX_X, ALU.add))
            link(dve.reciprocal(gsum[:, :], gsum[:, :]))
            dve.tensor_tensor(gts[:, :, :], gts[:, :, :], gsum[:, :].unsqueeze(2).to_broadcast([P, TT, TOPK]),
                              ALU.mult).then_inc(dn_free, 1)

            def halve(i, c, quarters=range(4)):
                to, src = halved[c % 3], fresh[c % 3]
                for q in quarters:
                    dve.wait_ge(hi_done, 24 * i + 4 * c + q + 1)
                    dve.scalar_tensor_tensor(to[:, 1, 2 * q:2 * q + 2, :], src[:, 2 * q:2 * q + 2, :], WS,
                                             to[:, 0, 2 * q:2 * q + 2, :], ALU.mult, ALU.subtract).then_inc(lo_done, 1)

            def put_x(i, r):
                dve.wait_ge(x_hi, 4 * i + r + 5 if i is not None else r + 1)
                dve.tensor_tensor(xT[:, 1, 2 * r:2 * r + 2, :], PS[:, 6 + r % 2, 0:2 * CAP].rearrange("p (k s) -> p k s", k=2),
                                  xT[:, 0, 2 * r:2 * r + 2, :], ALU.subtract).then_inc(x_lo, 1)

            halve(0, 0)
            halve(0, 1)
            for r in range(4):
                put_x(None, r)
            dve.wait_ge(items_ready, 3)
            dve.wait_ge(bias_copied, 1)
            n = dve.value_load(items[0:1, 2, 0:1], min_val=NEXP, max_val=MAX_ITEMS)
            with dve.Fori(0, n) as i:
                e = dve.value_load(items[0:1, 1, bass.ds(i, 1)], min_val=0, max_val=NEXP - 1)
                dve.wait_ge(dn_free, 8 * i + 1)
                dve.tensor_copy(bcur[:, :], biasT[:, :, bass.ds(e, 1)].rearrange("p f a -> p (f a)")).then_inc(bcur_ready, 1)
                dve.wait_ge(bcur_ready, 2 * i + 1)
                dve.tensor_scalar(bcur[:, 8:16], bcur[:, 8:16], WS, None, ALU.add).then_inc(bcur_ready, 1)
                dve.wait_ge(bcur_ready, 2 * i + 2)

                def gates(half, b):
                    dve.wait_ge(gu_done, 8 * i + 4 * half + b + 1)
                    for f in range(2):
                        k = 4 * half + 2 * b + f
                        ins = dve.tensor_scalar(gate[b][:, f, :], PS[:, b, CAP * f:CAP * (f + 1)], bcur[:, k:k + 1], WS * LIMIT,
                                                ALU.add, ALU.min)
                    ins.then_inc(gu_free, 1)

                def product(half, b):
                    dve.wait_ge(sig_ready, 4 * i + 2 * half + b + 1)
                    dve.wait_ge(gu_free, 8 * i + 4 * half + b + 1)
                    dve.scalar_tensor_tensor(sig[b], gate[b], 1.0 / (WS * WS), sig[b], ALU.mult, ALU.mult).then_inc(prod_ready, 1)

                def ups(half, b):
                    dve.wait_ge(gu_done, 8 * i + 4 * half + b + 3)
                    for f in range(2):
                        k = 8 + 4 * half + 2 * b + f
                        ins = dve.tensor_scalar(up[b][:, f, :], PS[:, 2 + b, CAP * f:CAP * (f + 1)], bcur[:, k:k + 1],
                                                WS * (LIMIT + 1.0), ALU.add, ALU.min)
                    ins.then_inc(gu_free, 1)
                    dve.wait_ge(gu_free, 8 * i + 4 * half + b + 3)
                    dve.wait_ge(prod_ready, 4 * i + 2 * half + b + 1)
                    dve.scalar_tensor_tensor(actf[b], up[b], WS * (1.0 - LIMIT), sig[b], ALU.max, ALU.mult).then_inc(act_f, 1)

                def act_rest(half, b):
                    k = 4 * half + 2 * b
                    dve.wait_ge(act_hi, 4 * i + 2 * half + b + 1)
                    dve.tensor_tensor(actT[:, 1, k:k + 2, :], actf[b], actT[:, 0, k:k + 2, :], ALU.subtract).then_inc(act_lo, 1)

                halve(i, 2, (0, 1))
                gates(0, 0)
                halve(i, 2, (2, 3))
                gates(0, 1)
                halve(i, 3, (0, 1))
                product(0, 0)
                ups(0, 0)
                halve(i, 3, (2, 3))
                product(0, 1)
                ups(0, 1)
                act_rest(0, 0)
                halve(i, 4, (0, 1))
                gates(1, 0)
                act_rest(0, 1)
                halve(i, 4, (2, 3))
                gates(1, 1)
                halve(i, 5, (0, 1))
                product(1, 0)
                ups(1, 0)
                product(1, 1)
                halve(i, 5, (2,))
                act_rest(1, 0)
                halve(i, 5, (3,))
                ups(1, 1)
                act_rest(1, 1)
                for r in range(4):
                    put_x(i, r)
                halve(i, 6)
                halve(i, 7)

            for t in range(TT):
                dve.wait_ge(y_in[t % 2], 16 * (t // 2 + 1))
                y = yt[t % 2].rearrange("p (k d) -> p k d", k=TOPK)
                for k in range(TOPK):
                    ins = dve.scalar_tensor_tensor(H[:, t, :], y[:, k, :], gts[:, t, k:k + 1], H[:, t, :], ALU.mult, ALU.add)
                    if k < TOPK - 1:
                        link(ins)
                ins.then_inc(y_sum, 1)
                dve.wait_ge(oss_done, 2 * t + 2)
                link(dve.reciprocal(rs[:, t:t + 1], rs[:, t:t + 1]))
                if t == 0:
                    dve.wait_ge(wfb_in, 16)
                if t >= 2:
                    dve.wait_ge(o_out[t % 2], 16 * (t // 2))
                dve.scalar_tensor_tensor(ot[t % 2], H[:, t, :], rs[:, t:t + 1], wfb, ALU.mult, ALU.mult).then_inc(o_ready, 1)

        @block.tensor
        def _(pe):
            pe.wait_ge(consts_in, 16 * N_CONST)
            for f in range(24):
                rows = bgu_rows if f < 16 else bdn_rows
                at = P * (f % 16)
                mm = pe.transpose(pair(2)[:, NEXP * f:NEXP * (f + 1)], rows[:, at:at + P], ident[0:NEXP, 0:NEXP])
            mm.then_inc(bias_mm, 1)
            for c, (bank, at, a, b) in enumerate(((6, 0, 0, 512), (7, 0, 512, 1024), (5, 256, 1024, LROW))):
                if c == 2:
                    pe.wait_ge(bias_copied, 1)
                pe.matmul(PS[0:AH, bank, at:at + b - a], relb[:, :], onehot[:, a:b], start=True, stop=True).then_inc(lrow_mm, 1)
            for t in range(TT):
                pe.wait_ge(xs_ready, t + 1)
                if t >= 2:
                    pe.wait_ge(xnT_ready, t - 1)
                for k in range(KD):
                    mm = pe.transpose(pair(t % 2)[:, P * k:P * (k + 1)], xt[t % 2][:, P * k:P * (k + 1)], ident[:, :])
                mm.then_inc(xT_mm, 1)

            def project(g):
                c = g // 4
                kind, part = CHUNKS[c]
                w = win[c % 2]
                bank = PS[:, 6 + g % 2, :]
                if g % 4 == 0:
                    pe.wait_ge(w_in_sem[c % 2], 16 * (c // 2 + 1))
                if g == 0:
                    pe.wait_ge(xnT_ready, TT)
                    pe.wait_ge(lrow_sum, 3)
                if g >= 2:
                    pe.wait_ge(proj_out, g - 1)
                if kind in ("fh", "qh", "qa", "ka"):
                    ft, half = divmod(g % 4, 2)
                    for k in range(KD):
                        mm = pe.matmul(bank, w[:, k, P * ft:P * (ft + 1)], xnT[:, k, 512 * half:512 * half + 512],
                                       start=(k == 0), stop=(k == KD - 1))
                else:
                    for tt in range(2):
                        t = 2 * (g % 4) + tt
                        for k in range(KD):
                            mm = pe.matmul(bank[:, 256 * tt:256 * tt + 256], xnT[:, k, t * P:(t + 1) * P], w[:, k, :],
                                           start=(k == 0), stop=(k == KD - 1))
                mm.then_inc(proj_done, 1)

            def step(s):
                hd, j = divmod(s, STEPS)
                to = pair(s % 2)
                if s >= 2:
                    ph, pj = divmod(s - 2, STEPS)
                    if pj in (8, 11):
                        pe.wait_ge(h_act_out, 2 * ph + (1 if pj == 8 else 2))
                    else:
                        pe.wait_ge(h_dve_out, 10 * ph + {9: 9, 10: 10}.get(pj, pj + 1))
                if j == 0:
                    pe.wait_ge(h_k, hd + 1)
                    ops = [(b, [(FH[:, hd, P * b:P * (b + 1)], QH[:, hd, P * b:P * (b + 1)])]) for b in range(TT)]
                elif j <= 7:
                    pe.wait_ge(h_x, 9 * hd + j)
                    xx = X[(j - 1) % 2]
                    ops = [(b, [(xx[:, P * b:P * (b + 1)], xx[:, P * b:P * (b + 1)])]) for b in range(TT)]
                elif j == 8:
                    pe.wait_ge(h_x, 9 * hd + 8)
                    for b in range(TT):
                        mm = pe.transpose(to[:, P * b:P * (b + 1)], X[1][:, P * b:P * (b + 1)], ident[:, :])
                    ops = []
                elif j == 9:
                    pe.wait_ge(h_act_out, 2 * hd + 1)
                    pe.wait_ge(proj_out, 24)
                    ops = [(b, [(KT[:, P * b:P * (b + 1)], IH[:, b, P * hd:P * (hd + 1)])]) for b in range(TT)]
                elif j == 10:
                    pe.wait_ge(h_dve_out, 10 * hd + 9)
                    pe.wait_ge(h_x, 9 * hd + 9)
                    ops = [(b, [(A[:, P * b:P * (b + 1)], IH[:, b, P * hd:P * (hd + 1)])]
                            + ([(QD[:, P * b:P * (b + 1)], SA[:, P * b:P * (b + 1)])] if b else [])) for b in range(TT)]
                else:
                    pe.wait_ge(h_dve_out, 10 * hd + 10)
                    for b in range(TT):
                        mm = pe.transpose(to[:, P * b:P * (b + 1)], KT[:, P * b:P * (b + 1)], ident[:, :])
                    ops = []
                for b, products in ops:
                    for m, (lhs, rhs) in enumerate(products):
                        mm = pe.matmul(to[:, P * b:P * (b + 1)], lhs, rhs, start=(m == 0), stop=(m == len(products) - 1))
                mm.then_inc(h_step, 1)

            for what, n in SCHEDULE:
                project(n) if what == "group" else step(n)

            def scores(a):
                h, n = divmod(a, 8)
                b0 = HD * (h % 2)
                if a >= 2:
                    pe.wait_ge(att_m, a - 1)
                w = (n + 1) * P
                for at in range(0, w, 512):
                    end = min(w, at + 512)
                    mm = pe.matmul(pair(a % 2)[:, at:end], QA[b0:b0 + HD, h // 2, n * P:(n + 1) * P], KA[b0:b0 + HD, h // 2, at:end],
                                   start=True, stop=True)
                mm.then_inc(qk_done, 1)

            def transposes(a):
                pe.wait_ge(att_n, a + 1)
                if a >= 1:
                    pe.wait_ge(att_pt, a)
                for b in range(a % 8 + 1):
                    mm = pe.transpose(pair(2)[:, P * b:P * (b + 1)], SC[a % 3][:, P * b:P * (b + 1)], ident[:, :])
                mm.then_inc(tr_done, 1)

            def values(a):
                h, n = divmod(a, 8)
                b0 = HD * (h % 2)
                quad = a // 4
                pe.wait_ge(att_pt, a + 1)
                if a % 4 == 0 and quad >= 2:
                    pe.wait_ge(att_o, quad - 1)
                for b in range(n + 1):
                    mm = pe.matmul(PS[b0:b0 + HD, 6 + quad % 2, P * (a % 4):P * (a % 4 + 1)], VA[:, b, HD * h:HD * (h + 1)],
                                   PT[a % 2][:, P * b:P * (b + 1)], start=(b == 0), stop=(b == n))
                mm.then_inc(pv_done, 1)

            pe.wait_ge(proj_out, GROUPS)
            pe.wait_ge(h_act_out, 2 * GH_N)
            pe.wait_ge(h_dve_out, 10 * GH_N)
            scores(0)
            scores(1)
            for a in range(ITEMS_A):
                if a + 2 < ITEMS_A:
                    scores(a + 2)
                transposes(a)
                if a >= 1:
                    values(a - 1)
            values(ITEMS_A - 1)

            pe.wait_ge(att_o, ITEMS_A // 4)
            pe.wait_ge(wout_in, 32)

            def out_rows(t):
                if t >= 2:
                    pe.wait_ge(h_done, t - 1)
                for half in range(2):
                    for k in range(KD):
                        mix = QA if k < 4 else QH
                        mm = pe.matmul(pair(t % 2)[:, 512 * half:512 * (half + 1)], mix[:, k % 4, t * P:(t + 1) * P],
                                       wout[k // 4][:, k % 4, 512 * half:512 * (half + 1)], start=(k == 0), stop=(k == KD - 1))
                mm.then_inc(op_done, 1)

            def route(t):
                pe.wait_ge(xn2_ready, t + 1)
                if t >= 1:
                    pe.wait_ge(xn2T_ready, t)
                for k in range(KD):
                    mm = pe.transpose(pair(2)[:, P * k:P * (k + 1)], xn2[t % 2][:, P * k:P * (k + 1)], ident[:, :])
                mm.then_inc(xn2T_mm, 1)

            def logits(t):
                pe.wait_ge(xn2T_ready, t + 1)
                for k in range(KD):
                    mm = pe.matmul(PS[:, 6, NEXP * t:NEXP * (t + 1)], xn2T[t % 2][:, P * k:P * (k + 1)], rw[:, k, :],
                                   start=(k == 0), stop=(k == KD - 1))
                mm.then_inc(lg_done, 1)

            for t in range(TT + 2):
                if t < TT:
                    out_rows(t)
                if t >= 2:
                    logits(t - 2)
                if 1 <= t <= TT:
                    route(t - 1)
            pe.wait_ge(ones_set, 1)
            pe.wait_ge(mask_ready, 1)
            for t in range(TT):
                to = PS[:, 7, NEXP * t:NEXP * (t + 1)]
                pe.matmul(to, before[:, :], mask[:, t, :], start=True, stop=(t == 0))
                if t:
                    pe.matmul(to, ones[:, :], macc[:, t - 1, :], start=False, stop=True)
            pe.matmul(PS[:, 7, TT * NEXP:TT * NEXP + NEXP], ones[:, :], macc[:, TT - 1, :], start=True, stop=True).then_inc(rank_done, 1)
            pe.wait_ge(icol_ready, 1)
            for c in range(3):
                mm = pe.matmul(PS[0:1, 7, P * c:P * (c + 1)], icol[:, c:c + 1], ident[:, :], start=True, stop=True)
            mm.then_inc(items_mm, 1)

            def turn_x(r):
                for k in range(2 * r, 2 * r + 2):
                    at = CAP * (k % 2)
                    pe.transpose(PS[:, 6 + r % 2, at:at + P], xg[:, P * k:P * (k + 1)], ident[:, :])
                    mm = pe.transpose(PS[:, 6 + r % 2, at + P:at + CAP], xg2[:, P * k:P * (k + 1)], ident[0:32, 0:32])
                mm.then_inc(t_done, 1)

            def three(to, w, cols, moving):
                for k in range(KD):
                    for m, (a, b) in enumerate(((0, 0), (0, 1), (1, 0))):
                        mm = pe.matmul(to, w[:, a, k, cols:cols + P], moving[:, b, k, :],
                                       start=(k == 0 and m == 0), stop=(k == KD - 1 and m == 2))
                return mm

            pe.wait_ge(items_ready, 3)
            pe.wait_ge(xg_in, 32)
            for r in range(4):
                if r >= 2:
                    pe.wait_ge(x_lo, r - 1)
                turn_x(r)
            pe.wait_ge(x_lo, 4)
            n = pe.value_load(items[0:1, 2, 0:1], min_val=NEXP, max_val=MAX_ITEMS)
            with pe.Fori(0, n) as i:
                for c in range(4):
                    pe.wait_ge(hi_done, 24 * i + 4 * c + 4)
                    pe.wait_ge(lo_done, 24 * i + 4 * c + 4)
                    if c == 0:
                        pe.wait_ge(x_lo, 4 * i + 4)
                    for b in range(2):
                        if c >= 2:
                            pe.wait_ge(gu_free, 8 * i + 2 * c + b - 3)
                        for f in range(2):
                            mm = three(PS[:, 2 * (c % 2) + b, CAP * f:CAP * (f + 1)], halved[c % 3], P * (2 * b + f), xT)
                        if b == 0:
                            mm.then_inc(gu_done, 1)
                    mm.then_inc(gu_done, 1)
                pe.wait_ge(xg_in, 32 * i + 64)
                for r in range(4):
                    if r < 2:
                        pe.wait_ge(o_rows, 4 * i + 1)
                    else:
                        pe.wait_ge(x_lo, 4 * i + r + 3)
                    turn_x(r)
                for q in range(4):
                    c = 4 + q // 2
                    if q % 2 == 0:
                        pe.wait_ge(hi_done, 24 * i + 4 * c + 4)
                        pe.wait_ge(lo_done, 24 * i + 4 * c + 4)
                    if q == 0:
                        pe.wait_ge(act_hi, 4 * i + 4)
                        pe.wait_ge(act_lo, 4 * i + 4)
                    if q >= 2:
                        pe.wait_ge(dn_free, 8 * i + 2 * q - 1)
                    for f in range(2):
                        mm = three(PS[:, 4 + q % 2, CAP * f:CAP * (f + 1)], halved[c % 3], P * (2 * (q % 2) + f), actT)
                    mm.then_inc(dn_done, 1)
                for g in range(2):
                    pe.wait_ge(dn_free, 8 * i + 4 * g + 5)
                    pe.wait_ge(*((x_lo, 4 * i + 7) if g == 0 else (o_rows, 4 * i + 2)))
                    for k in range(4):
                        mm = pe.transpose(PS[:, 6, P * k:P * (k + 1)], oT[:, 4 * g + k, 0:P], ident[:, :])
                    mm.then_inc(t_done, 1)
                    pe.wait_ge(*((x_lo, 4 * i + 8) if g == 0 else (o_rows, 4 * i + 3)))
                    for k in range(4):
                        mm = pe.transpose(PS[0:32, 7, P * k:P * (k + 1)], oT[:, 4 * g + k, P:CAP], ident[:, :])
                    mm.then_inc(t_done, 1)


_INS = ["x", "norm_mix_w", "w_in", "rel_bias", "hgrn_lb_logits", "hgrn_norm_w", "w_out", "norm_ffn_w", "router_w",
        "router_b", "w_gate_up", "b_gate_up", "w_down", "b_down", "final_norm_w"]


def kernel(**inputs):
    import numpy as _np
    import concourse.bacc as _bacc
    from concourse import mybir as _mybir
    from concourse.bass_utils import run_bass_kernel_spmd as _run

    nc = _bacc.Bacc("TRN2", target_bir_lowering=False, num_devices=1)
    arrays, args = {}, {}
    both = [(name, inputs[name]) for name in _INS] + list(constant_arrays().items())
    for name, a in both:
        a = _np.ascontiguousarray(a)
        arrays[f"in_{name}"] = a
        args[name] = nc.dram_tensor(f"in_{name}", a.shape, _mybir.dt.from_np(a.dtype), kind="ExternalInput").ap()
    out = nc.dram_tensor("out_0", (1, S, D), F32, kind="ExternalOutput").ap()
    build(nc, out=out, **args)
    r = _run(nc, [arrays], core_ids=[0])
    return r.results[0]["out_0"]
```

```python
from contextlib import ExitStack

import numpy as np

import concourse.bass as bass
from concourse import mybir

F32 = mybir.dt.float32
F16 = mybir.dt.float16
I32 = mybir.dt.int32
U32 = mybir.dt.uint32
U8 = mybir.dt.uint8
ALU = mybir.AluOpType
ACT = mybir.ActivationFunctionType
AX_X = mybir.AxisListType.X

P = 128
S = 1024
D = 1024
TT = S // P
KD = D // P
AH, HD = 8, 64
GH_N = 4
NEXP, TOPK = 32, 4
EPS = 1e-5
BUCKETS, MAX_DISTANCE = 32, 2048
PATTERNS = ((128, 1), (512, 4), (2048, 16))
NEG = -1e30

LEVELS = 7
STEPS = LEVELS + 5
LROW = S + P

CAP = 160
ROUNDS = -(-S // CAP)
STRIDE = ROUNDS * CAP
PAD_ROW = NEXP * STRIDE
TABLE = -(-(PAD_ROW + CAP) // P) * P
TABLE_P = TABLE * 2 // P
PAIRS = NEXP * ROUNDS
MAX_ITEMS = NEXP + S * TOPK // CAP
LIMIT, ALPHA = 7.0, 1.702

WS = 1024.0

COLUMN = {"qa": 0, "ka": 512, "va": 1024, "qh": 1536, "fh": 2048, "ih": 2560, "gh": 3072}
CHUNKS = [(kind, part) for kind in ("fh", "qh", "ih", "gh", "ka", "qa", "va") for part in range(2)]
EARLY = 6
GROUPS = 4 * len(CHUNKS)


def constant_arrays():
    i = np.arange(P)
    ident = np.eye(P, dtype=np.float32)
    before = (i[:, None] < i[None, :]).astype(np.float32)
    masks = np.zeros((P, LEVELS, P), np.float32)
    for level in range(LEVELS):
        h = 64 >> level
        same = (i[:, None] // (2 * h)) == (i[None, :] // (2 * h))
        masks[:, level] = same & ((i[:, None] // h) % 2 == 0) & ((i[None, :] // h) % 2 == 1)
    dist = S - 1 - np.arange(LROW)
    n = np.maximum(dist, 0)
    exact = BUCKETS // 2
    large = exact + (np.log(np.maximum(n, 1) / exact) / np.log(MAX_DISTANCE / exact)
                     * (BUCKETS - exact)).astype(np.int32)
    bucket = np.where(n < exact, n, np.minimum(large, BUCKETS - 1))
    times = sum(((dist >= 0) & (dist % d == 0) & (dist // d <= w // d)).astype(np.int64) for w, d in PATTERNS)
    onehot = ((bucket[None] == np.arange(BUCKETS)[:, None]) & (times > 0)[None]).astype(np.float32)
    log_times = np.where(times > 0, np.log(np.maximum(times, 1)), NEG).astype(np.float32)
    e, r = np.arange(PAIRS) // ROUNDS, np.arange(PAIRS) % ROUNDS
    pairs = np.stack([np.where(r > 0, CAP * r + 0.5, -0.5), (np.arange(PAIRS) - PAIRS) * CAP, e]).astype(np.float32)
    ids = np.zeros((P, TT, TOPK, 2), np.int32)
    tok = np.arange(TT)[None, :, None] * P + i[:, None, None]
    ids[..., 0] = tok * TOPK + np.arange(TOPK)
    ids[..., 1] = tok
    pad = np.tile(np.array([S * TOPK, S], np.int32), TABLE).reshape(P, TABLE_P)
    return {
        "c_ident": ident, "c_before": before, "c_masks": masks.reshape(P, LEVELS * P),
        "c_onehot": onehot, "c_times": log_times[None], "c_pairs": pairs.reshape(1, 3 * PAIRS),
        "c_lane": i[:, None].astype(np.float32), "c_experts": np.arange(NEXP, dtype=np.float32)[None],
        "c_ids": ids.reshape(P, -1), "c_pad": pad,
    }


def build(nc, x, norm_mix_w, w_in, rel_bias, hgrn_lb_logits, hgrn_norm_w, w_out, norm_ffn_w, router_w,
          router_b, w_gate_up, b_gate_up, w_down, b_down, final_norm_w, c_ident, c_before, c_masks,
          c_onehot, c_times, c_pairs, c_lane, c_experts, c_ids, c_pad, out):
    with ExitStack() as ctx:
        def sb(name, shape, dt=F32):
            return ctx.enter_context(nc.sbuf_tensor(name, shape, dt))

        def sem(name):
            return ctx.enter_context(nc.semaphore(name))

        ctx.enter_context(nc.allow_non_contiguous_dma(reason="small per-partition vectors"))

        RX = sb("RX", [P, 8192])
        RW = sb("RW", [P, 4096])
        RP = sb("RP", [P, 28672])
        RT = sb("RT", [P, 8704])
        RQ = sb("RQ", [P, 512])

        xnT = RX[:, :].bitcast(F16).rearrange("p (m k s) -> p m k s", m=2, k=KD)
        win = [RW[:, 2048 * b:2048 * b + 2048].bitcast(F16).rearrange("p (m k n) -> p m k n", m=2, k=KD) for b in range(2)]
        quarter = [ap.rearrange("p (k n) -> p k n", k=2) for ap in (RT[:, 8192:8704], RQ[:, :])]
        region = {"qa": 0, "qh": 4096, "ka": 8192, "va": 12288, "gh": 16384, "fh": 20480, "ih": 24576}

        def by_feature(kind):
            return RP[:, region[kind]:region[kind] + 4096].rearrange("p (f s) -> p f s", f=4)

        def by_token(kind):
            return RP[:, region[kind]:region[kind] + 4096].rearrange("p (t n) -> p t n", t=TT)

        QA, KA, QH, FH = (by_feature(k) for k in ("qa", "ka", "qh", "fh"))
        VA, IH, GH = (by_token(k) for k in ("va", "ih", "gh"))

        xt = [RP[:, 16384 + 1024 * b:16384 + 1024 * (b + 1)] for b in range(2)]
        xsq = RP[:, 18432:19456]
        bgu_rows = RP[0:NEXP, 8192:10240]
        bdn_rows = RP[0:NEXP, 10240:11264]
        lrow = RP[0:AH, 12288:12288 + LROW]
        ltimes = RP[0:AH, 13440:13440 + LROW]
        onehot = RP[0:BUCKETS, 14592:14592 + LROW]

        masks_f = RT[:, 0:LEVELS * P]
        C = RT[:, 0:1024]
        DE = [RT[:, 1024:2048], RT[:, 2048:3072]]
        X = [RT[:, 3072:4096], RT[:, 4096:5120]]
        KT = RT[:, 5120:6144]
        QD = RT[:, 6144:7168]
        A = RT[:, 7168:8192]
        SA = X[1]
        BT = [RX[:, 1024 * b:1024 * (b + 1)] for b in range(2)]
        SC = [RX[:, 2048 + 1024 * b:2048 + 1024 * (b + 1)] for b in range(3)]
        PT = [RX[:, 5120 + 1024 * b:5120 + 1024 * (b + 1)] for b in range(2)]
        H = RX[:, :].rearrange("p (t d) -> p t d", t=TT)
        wout = [RP[:, region[k]:region[k] + 4096].rearrange("p (k n) -> p k n", k=4) for k in ("fh", "ih")]
        hsq = RW[:, 0:1024]
        xn2 = [RW[:, 1024:2048], RW[:, 2048:3072]]
        w2b = RW[:, 3072:4096]
        xn2T = [RT[:, 0:1024], RT[:, 1024:2048]]
        xn2h = [RT[:, 5888 + 1024 * b:6912 + 1024 * b] for b in range(2)]
        fresh = [RP[:, region[k]:region[k] + 4096].rearrange("p (k n) -> p k n", k=KD) for k in ("ka", "va", "gh")]
        halved = [RP[:, region[k]:region[k] + 4096].bitcast(F16).rearrange("p (m k n) -> p m k n", m=2, k=KD)
                  for k in ("fh", "ih", "qa")]

        def two(ap):
            return ap.bitcast(F16).rearrange("p (m k s) -> p m k s", m=2, k=KD)

        xT, actT = two(RT[:, 0:1280]), two(RT[:, 1280:2560])
        oT = RT[:, 2560:3840].rearrange("p (k s) -> p k s", k=KD)
        xg, xg2 = RT[:, 3840:4864], RT[0:32, 4864:5888]
        xgh, xgh2 = (ap.bitcast(F16).rearrange("p (m n) -> p m n", m=2) for ap in (xg, xg2))
        og, og2 = RT[:, 5888:6912], RT[0:32, 6912:7936]
        gate, up, sig, actf = ([RW[:, at + 320 * b:at + 320 * b + 320].rearrange("p (f s) -> p f s", f=2) for b in range(2)]
                               for at in (0, 640, 1280, 1920))
        yt = [RP[:, region[k]:region[k] + 4096] for k in ("fh", "ih", "ka", "va")]
        last = RP[:, region["qa"]:region["qa"] + 4096]
        osq, wfb, ot = last[:, 0:1024], last[:, 1024:2048], [last[:, 2048:3072], last[:, 3072:4096]]

        ident, before, ones = sb("ident", [P, P]), sb("before", [P, P]), sb("ones", [P, P])
        ident16, warm = sb("ident16", [P, P], F16), sb("warm", [P, 1])
        masks = sb("masks", [P, LEVELS, P], U8)
        relb = sb("relb", [BUCKETS, AH])
        nmw, hnw = sb("nmw", [P, KD]), sb("hnw", [P, 1])
        lbl = sb("lbl", [P, 2, GH_N])
        lb, omlb, lbt = sb("lb", [P, GH_N]), sb("omlb", [P, GH_N]), sb("lbt", [P, 4, GH_N])
        rw = sb("rw", [P, KD, NEXP])
        rb = sb("rb", [P, NEXP])
        biasT = sb("biasT", [P, 24, NEXP])
        pairs = sb("pairs", [P, 3, PAIRS])
        lane = sb("lane", [P, 1])
        experts = sb("experts", [P, NEXP])
        ids = sb("ids", [P, TT * TOPK, 2], I32)
        ss, rs = sb("ss", [P, TT]), sb("rs", [P, TT])
        dl, hss, hrs = sb("dl", [P, TT]), sb("hss", [P, TT]), sb("hrs", [P, TT])
        am, az = sb("am", [P, 8 * AH]), sb("az", [P, 8 * AH])
        def spare(at, n):
            return RT[:, at:at + n]

        lg, mask, macc, rk = (spare(2048 + 256 * c, 256).rearrange("p (t e) -> p t e", t=TT) for c in range(4))
        flags, posn, picked = (spare(7936 + PAIRS * c, PAIRS) for c in range(3))
        oh = hsq.rearrange("p (k t e) -> p k t e", k=TOPK, t=TT)
        items = RQ[0:1, 0:3 * P].bitcast(I32).rearrange("p (a b) -> p a b", a=3)
        vals = RQ[:, 3 * P:3 * P + 64].rearrange("p (t v) -> p t v", t=TT)
        idx = RQ[:, 3 * P + 64:4 * P].bitcast(U32).rearrange("p (t v) -> p t v", t=TT)
        idxf = sb("idxf", [P, TT, 8])
        rkk = sb("rkk", [P, TOPK, TT])
        slots = sb("slots", [P, TT * TOPK], I32)
        gts, gsum = sb("gts", [P, TT, TOPK]), sb("gsum", [P, TT])
        icol = sb("icol", [P, 3])
        bcur = sb("bcur", [P, 24])
        tok, tok2 = sb("tok", [P, 2], I32), sb("tok2", [32, 2], I32)
        dst, dst2 = sb("dst", [P, 1], I32), sb("dst2", [32, 1], I32)
        zero, idle = sb("zero", [P, 1], I32), sb("idle", [P, 2], I32)

        PS = ctx.enter_context(nc.psum_tensor("PS", [P, 8, 512], F32))

        def turned(r):
            return PS[:, (6, 7, 0, 1)[r], :].bitcast(F16)[:, 0:4 * CAP].rearrange("p (m k s) -> p m k s", m=2, k=2)

        def pair(n):
            return PS[:, 2 * n:2 * n + 2, :].rearrange("p b n -> p (b n)")

        lrow_dram = nc.dram_tensor("lrow_dram", [AH, LROW], F32)
        shifted_dram = nc.dram_tensor("shifted_dram", [AH, P, LROW], F32)
        xn_dram = nc.dram_tensor("xn_dram", [S, D], F32)
        table = nc.dram_tensor("table", [TABLE, 2], I32)
        y_dram = nc.dram_tensor("y_dram", [S * TOPK, D], F32)

        consts_in = sem("consts_in")
        x_in = [sem(f"x_in{b}") for b in range(2)]
        w_in_sem = [sem(f"win_in{b}") for b in range(2)]
        bt_in = [sem(f"bt_in{b}") for b in range(2)]
        wout_in, w2b_in, wfb_in = sem("wout_in"), sem("w2b_in"), sem("wfb_in")
        h_in = sem("h_in")
        ones_set, xg_set = sem("ones_set"), sem("xg_set")
        lrow_sum, lrow_out, lrow_mm, shifted_out = sem("lrow_sum"), sem("lrow_out"), sem("lrow_mm"), sem("shifted_out")
        bias_mm, bias_copied = sem("bias_mm"), sem("bias_copied")
        ss_done, win_hi, win_lo = sem("ss_done"), sem("win_hi"), sem("win_lo")
        xs_ready, xT_mm, xnT_hi, xnT_ready = sem("xs_ready"), sem("xT_mm"), sem("xnT_hi"), sem("xnT_ready")
        proj_done, proj_out = sem("proj_done"), sem("proj_out")
        h_f, h_g, h_k, h_d, h_e, h_x = (sem(n) for n in ("h_f", "h_g", "h_k", "h_d", "h_e", "h_x"))
        h_step, h_dve_out, h_act_out, h_sq, h_ss = (sem(n) for n in ("h_step", "h_dve_out", "h_act_out", "h_sq", "h_ss"))
        lb_exp, lb_sub = sem("lb_exp"), sem("lb_sub")
        qk_done, att_m, att_p, att_n = sem("qk_done"), sem("att_m"), sem("att_p"), sem("att_n")
        tr_done, att_pt, pv_done, att_o = sem("tr_done"), sem("att_pt"), sem("pv_done"), sem("att_o")
        op_done, h_done, hss_done, xn2_ready = sem("op_done"), sem("h_done"), sem("hss_done"), sem("xn2_ready")
        xn2_hi, xn2_lo, warmed = sem("xn2_hi"), sem("xn2_lo"), sem("warmed")
        xn2_out = [sem(f"xn2_out{b}") for b in range(2)]
        xn2T_mm, xn2T_ready, lg_done = sem("xn2T_mm"), sem("xn2T_ready"), sem("lg_done")
        gexp_in, gexp, mask_ready, rank_done = sem("gexp_in"), sem("gexp"), sem("mask_ready"), sem("rank_done")
        slots_ready, icol_ready, items_mm, items_ready = (sem(n) for n in ("slots_ready", "icol_ready", "items_mm", "items_ready"))
        table_pad, table_in = sem("table_pad"), sem("table_in")
        w_load = [sem(f"w_load{c}") for c in range(3)]
        hi_done, lo_done = sem("hi_done"), sem("lo_done")
        gu_done, gu_free, sig_ready, prod_ready = (sem(n) for n in ("gu_done", "gu_free", "sig_ready", "prod_ready"))
        act_f, act_hi, act_lo = (sem(n) for n in ("act_f", "act_hi", "act_lo"))
        tok_in, xg_in, t_done, x_act, x_dve, o_rows = (sem(n) for n in ("tok_in", "xg_in", "t_done", "x_act", "x_dve", "o_rows"))
        dn_done, dn_free, bcur_ready, dst_copied, y_out = (sem(n) for n in ("dn_done", "dn_free", "bcur_ready", "dst_copied", "y_out"))
        dve_step, act_step, pool_step = sem("dve_step"), sem("act_step"), sem("pool_step")
        y_in = [sem(f"y_in{b}") for b in range(len(yt))]
        y_sum, oss_done, o_ready = sem("y_sum"), sem("oss_done"), sem("o_ready")
        o_out = [sem(f"o_out{b}") for b in range(2)]

        N_CONST = 17
        X2 = x[0]
        SCHEDULE = [("group", g) for g in range(4 * EARLY)]
        late = GROUPS - 4 * EARLY
        for g in range(late):
            SCHEDULE.append(("group", 4 * EARLY + g))
            SCHEDULE += [("step", s) for s in range(g * GH_N * STEPS // late, (g + 1) * GH_N * STEPS // late)]
        ITEMS_A = 8 * AH

        block = ctx.enter_context(nc.Block())

        def load_w_in(sp, n):
            kind, part = CHUNKS[n // 4]
            at = COLUMN[kind] + 256 * part
            rows = w_in[0, 2 * P * (n % 4):2 * P * (n % 4 + 1), at:at + 256]
            if n >= 2:
                sp.wait_ge(win_lo, n - 1)
            sp.dma_start(quarter[n % 2], rows.rearrange("(k p) n -> p k n", p=P)).then_inc(w_in_sem[n % 2], 16)

        def quarters_at(g):
            if g // 4 == 0 or g // 4 == len(CHUNKS) - 1:
                return []
            return [4 * (g // 4 + 1) + q for q in ((0, 1), (2,), (3,), ())[g % 4]]

        def load_expert_chunk(sp, e, c):
            wg = w_gate_up[0, bass.ds(e, 1)].rearrange("a (k p) n -> p (a k) n", p=P)
            wd = w_down[0, bass.ds(e, 1)].rearrange("a (k p) n -> p (a k) n", p=P)
            at = D * (c % 2) + 512 * (c // 2)
            src = wg[:, :, at:at + 512] if c < 4 else wd[:, :, 512 * (c - 4):512 * (c - 3)]
            sp.dma_start(fresh[c % 3], src).then_inc(w_load[c % 3], 16)

        @block.sync
        def _(sp):
            for dst_ap, src in (
                (ident[:, :], c_ident), (before[:, :], c_before), (masks_f, c_masks),
                (onehot, c_onehot), (ltimes, c_times[0, :].partition_broadcast(AH)), (relb[:, :], rel_bias),
                (nmw[:, :], norm_mix_w[0].rearrange("(k p) -> p k", p=P)),
                (hnw[:, :], hgrn_norm_w[0].rearrange("(p a) -> p a", a=1)),
                (lbl[:, :, :], hgrn_lb_logits.rearrange("l (h p) -> p l h", p=P)),
                (bgu_rows, b_gate_up[0]), (bdn_rows, b_down[0]),
                (rw[:, :, :], router_w[0].rearrange("(k p) e -> p k e", p=P)),
                (rb[:, :], router_b[0].partition_broadcast(P)),
                (pairs[:, :, :].rearrange("p a b -> p (a b)"), c_pairs[0, :].partition_broadcast(P)), (lane[:, :], c_lane),
                (experts[:, :], c_experts[0, :].partition_broadcast(P)),
                (ids[:, :, :].rearrange("p a b -> p (a b)"), c_ids),
            ):
                sp.dma_start(dst_ap, src).then_inc(consts_in, 16)
            sp.dma_start(table[:, :].rearrange("(p r) c -> p (r c)", p=P), c_pad).then_inc(table_pad, 16)
            for t in range(TT):
                if t >= 2:
                    sp.wait_ge(xT_mm, t - 1)
                sp.dma_start(xt[t % 2], X2[t * P:(t + 1) * P, :]).then_inc(x_in[t % 2], 16)
                load_w_in(sp, t)
            for c in range(2, len(CHUNKS)):
                for q in range(4):
                    load_w_in(sp, 4 * c + q)
                if c == 5:
                    sp.wait_ge(lrow_out, 16)
                    for h in range(AH):
                        sp.dma_start(shifted_dram[h], lrow_dram[h, :].partition_broadcast(P)).then_inc(shifted_out, 16)
                if c == 3:
                    sp.wait_ge(lrow_sum, 3)
                    sp.dma_start(lrow_dram[:, :], lrow).then_inc(lrow_out, 16)
            sp.wait_ge(proj_done, GROUPS)
            sp.wait_ge(shifted_out, 16 * AH)
            for h in range(AH):
                if h >= 2:
                    sp.wait_ge(att_m, 8 * (h - 1))
                sp.dma_start(BT[h % 2], bass.AP(shifted_dram, h * P * LROW + P - 1, [[LROW - 1, P], [1, S]])).then_inc(bt_in[h % 2], 16)
                if h == 0:
                    sp.wait_ge(proj_out, GROUPS)
                    sp.dma_start(w2b, norm_ffn_w[0].partition_broadcast(P)).then_inc(w2b_in, 16)
                    sp.wait_ge(h_step, GH_N * STEPS)
                    for c in range(2):
                        sp.dma_start(wout[c], w_out[0, 512 * c:512 * (c + 1), :].rearrange("(k p) n -> p k n", p=P)).then_inc(wout_in, 16)
            sp.wait_ge(pv_done, ITEMS_A)
            sp.dma_start(H, X2.rearrange("(t p) d -> p t d", p=P)).then_inc(h_in, 16)
            sp.wait_ge(h_dve_out, 10 * GH_N)
            for c in range(3):
                load_expert_chunk(sp, 0, c)
            for t in range(TT):
                sp.wait_ge(xn2_lo, t + 1)
                sp.dma_start(xn_dram[t * P:(t + 1) * P, :], xn2h[t % 2]).then_inc(xn2_out[t % 2], 16)
            sp.wait_ge(items_ready, 3)
            n = sp.value_load(items[0:1, 2, 0:1], min_val=NEXP, max_val=MAX_ITEMS)
            with sp.Fori(0, n) as i:
                now = sp.value_load(items[0:1, 1, bass.ds(i, 1)], min_val=0, max_val=NEXP - 1)
                after = sp.value_load(items[0:1, 1, bass.ds(i + 1, 1)], min_val=0, max_val=NEXP - 1)
                for c in range(3, 9):
                    sp.wait_ge(lo_done, 24 * i + 4 * (c - 2))
                    load_expert_chunk(sp, now if c < 6 else after, c % 6)
            sp.wait_ge(dn_done, 4 * n)
            sp.wait_ge(lo_done, 24 * n + 8)
            for c in range(3):
                sp.wait_ge(w_load[c], 32 * n + 16)
            sp.dma_start(wfb, final_norm_w.partition_broadcast(P)).then_inc(wfb_in, 16)
            sp.wait_ge(y_out, 32 * n)
            for t in range(TT):
                if t >= len(yt):
                    sp.wait_ge(y_sum, t - len(yt) + 1)
                sp.dma_start(yt[t % len(yt)], y_dram[t * P * TOPK:(t + 1) * P * TOPK, :].rearrange("(p k) d -> p (k d)", k=TOPK)
                             ).then_inc(y_in[t % len(yt)], 16)

        @block.gpsimd
        def _(pool):
            pool.memset(ones[:, :], 1.0).then_inc(ones_set, 1)
            pool.wait_ge(consts_in, 16 * N_CONST)
            pool.tensor_copy(masks[:, :, :].rearrange("p l t -> p (l t)"), masks_f).then_inc(ones_set, 1)
            pool.tensor_tensor(ident16[:, :], ident[:, :], ident[:, :], ALU.mult).then_inc(ones_set, 1)
            pool.wait_ge(table_pad, 16)
            pool.wait_ge(h_step, GH_N * STEPS)
            pool.wait_ge(h_dve_out, 10 * GH_N)
            pool.wait_ge(h_act_out, 2 * GH_N)
            pool.memset(zero[:, :], 0).then_inc(o_rows, 1)
            pool.memset(xg, 0.0).then_inc(xg_set, 1)
            pool.memset(xg2, 0.0).then_inc(xg_set, 1)
            for n in range(TT * TOPK):
                if n % TT == 0:
                    pool.wait_ge(slots_ready, n // TT + 1)
                j = TOPK * (n % TT) + n // TT
                pool.indirect_dma_start(
                    table[:, :], bass.IndirectOffsetOnAxis(ap=slots[:, j:j + 1], axis=0),
                    ids[:, j, :], None, bounds_check=PAD_ROW - 1, oob_is_err=False).then_inc(table_in, 16)
            pool.wait_ge(table_in, 16 * TT * TOPK)
            for b in range(2):
                pool.wait_ge(xn2_out[b], 16 * TT // 2)
            pool.wait_ge(items_ready, 3)
            pool.wait_ge(xg_set, 2)
            pool.wait_ge(o_rows, 1)

            last_row, last_place = pool.to_reg(S - 1), pool.to_reg(S * TOPK - 1)

            def load_tokens(at):
                pool.dma_start(tok[:, :], table[bass.ds(at, P), :]).then_inc(tok_in, 16)
                pool.dma_start(tok2[:, :], table[bass.ds(at + P, 32), :]).then_inc(tok_in, 16)

            def gather():
                pool.indirect_dma_start(xg, None, xn_dram[:, :], bass.IndirectOffsetOnAxis(ap=tok[:, 1:2], axis=0),
                                        bounds_check=last_row, oob_is_err=False).then_inc(xg_in, 16)
                pool.indirect_dma_start(xg2, None, xn_dram[:, :], bass.IndirectOffsetOnAxis(ap=tok2[:, 1:2], axis=0),
                                        bounds_check=last_row, oob_is_err=False).then_inc(xg_in, 16)

            load_tokens(pool.value_load(items[0:1, 0, 0:1], min_val=0, max_val=PAD_ROW))
            pool.wait_ge(tok_in, 32)
            gather()
            n = pool.value_load(items[0:1, 2, 0:1], min_val=NEXP, max_val=MAX_ITEMS)
            with pool.Fori(0, n) as i:
                at = pool.value_load(items[0:1, 0, bass.ds(i + 1, 1)], min_val=0, max_val=PAD_ROW)
                pool.tensor_tensor(dst[:, :], tok[:, 0:1], zero[:, :], ALU.add).then_inc(dst_copied, 1)
                pool.tensor_tensor(dst2[:, :], tok2[:, 0:1], zero[0:32, :], ALU.add).then_inc(dst_copied, 1)
                pool.wait_ge(dst_copied, 2 * i + 2)
                pool.wait_ge(xg_in, 32 * i + 32)
                load_tokens(at)
                pool.wait_ge(tok_in, 32 * i + 64)
                pool.wait_ge(t_done, 8 * i + 4)
                pool.tensor_tensor(idle[:, 0:1], zero[:, :], zero[:, :], ALU.add)
                gather()
                pool.wait_ge(o_rows, 4 * i + 5)
                pool.tensor_tensor(idle[:, 1:2], zero[:, :], zero[:, :], ALU.add)
                pool.indirect_dma_start(y_dram[:, :], bass.IndirectOffsetOnAxis(ap=dst[:, 0:1], axis=0), og, None,
                                        bounds_check=last_place, oob_is_err=False).then_inc(y_out, 16)
                pool.indirect_dma_start(y_dram[:, :], bass.IndirectOffsetOnAxis(ap=dst2[:, 0:1], axis=0), og2, None,
                                        bounds_check=last_place, oob_is_err=False).then_inc(y_out, 16)
                pool.wait_ge(y_out, 32 * i + 32)
            pool.wait_ge(xg_in, 32 * n + 32)

        @block.scalar
        def _(act):
            act.wait_ge(consts_in, 16 * N_CONST)
            act.wait_ge(lb_sub, 1)
            act.activation(lbt[:, 2:4, :], lbt[:, 0:2, :], ACT.Exp).then_inc(lb_exp, 1)
            act.wait_ge(bias_mm, 1)
            act.activation(biasT[:, 0:16, :].rearrange("p f e -> p (f e)"), pair(2)[:, 0:16 * NEXP], ACT.Copy, scale=WS)
            act.activation(biasT[:, 16:24, :].rearrange("p f e -> p (f e)"), pair(2)[:, 16 * NEXP:24 * NEXP], ACT.Copy).then_inc(bias_copied, 1)
            def win_hi_part(n):
                act.wait_ge(w_in_sem[n % 2], 16 * (n // 2 + 1))
                if n >= 8:
                    act.wait_ge(proj_done, 4 * (n // 4 - 1))
                q = n % 4
                act.activation(win[n // 4 % 2][:, 0, 2 * q:2 * q + 2, :], quarter[n % 2], ACT.Copy, scale=WS).then_inc(win_hi, 1)

            def xnT_hi_part(t):
                act.wait_ge(xT_mm, t + 1)
                for k in range(KD):
                    ins = act.activation(xnT[:, 0, k, t * P:(t + 1) * P], pair(t % 2)[:, P * k:P * (k + 1)], ACT.Copy,
                                         scale=nmw[:, k:k + 1])
                ins.then_inc(xnT_hi, 1)

            for t in range(TT):
                act.wait_ge(x_in[t % 2], 16 * (t // 2 + 1))
                if t >= 1:
                    act.wait_ge(ss_done, 2 * t)
                act.activation(xsq, xt[t % 2], ACT.Square, accum_out=ss[:, t:t + 1]).then_inc(ss_done, 1)
                act.wait_ge(ss_done, 2 * t + 1)
                act.activation(rs[:, t:t + 1], ss[:, t:t + 1], ACT.Sqrt, scale=1.0 / D, bias=EPS).then_inc(ss_done, 1)
                if t >= 1:
                    xnT_hi_part(t - 1)
                win_hi_part(t)
            xnT_hi_part(TT - 1)

            def evacuate(g):
                for n in quarters_at(g):
                    win_hi_part(n)
                kind, part = CHUNKS[g // 4]
                act.wait_ge(proj_done, g + 1)
                bank = PS[:, 6 + g % 2, :]
                if kind in ("fh", "qh", "qa", "ka"):
                    ft, half = divmod(g % 4, 2)
                    to, src = by_feature(kind)[:, 2 * part + ft, 512 * half:512 * half + 512], bank
                else:
                    t = 2 * (g % 4)
                    to = by_token(kind)[:, t:t + 2, 256 * part:256 * part + 256]
                    src = bank.rearrange("p (t n) -> p t n", t=2)
                func = {"fh": ACT.Sigmoid, "qh": ACT.Silu, "gh": ACT.Silu}.get(kind, ACT.Copy)
                act.activation(to, src, func, scale=(HD ** -0.5 if kind == "qa" else 1.0) / WS).then_inc(proj_out, 1)

            def decay(hd, m):
                act.wait_ge(h_d, 9 * hd + m + 2)
                act.activation(DE[m % 2], DE[m % 2], ACT.Exp).then_inc(h_e, 1)

            def head_start(hd):
                act.wait_ge(h_f, hd + 1)
                if hd:
                    act.wait_ge(h_x, 9 * hd)
                act.activation(DE[0], FH[:, hd, :], ACT.Ln).then_inc(h_g, 1)
                decay(hd, 0)
                decay(hd, 1)

            def step(s):
                hd, j = divmod(s, STEPS)
                if s == 0:
                    head_start(0)
                if 1 <= j <= 6:
                    decay(hd, j + 1)
                if j == 7:
                    act.activation(dl[:, :], C.rearrange("p (b t) -> p b t", b=TT)[:, :, P - 1], ACT.Exp).then_inc(h_e, 1)
                    act.wait_ge(h_x, 9 * hd + 7)
                    act.activation(DE[0], C, ACT.Exp).then_inc(h_e, 1)
                if j == 8:
                    act.wait_ge(h_step, s + 1)
                    act.activation(KT, pair(s % 2), ACT.Copy).then_inc(h_act_out, 1)
                    if hd + 1 < GH_N:
                        head_start(hd + 1)
                if j == 10:
                    act.wait_ge(h_step, s + 1)
                    act.activation(A, pair(s % 2), ACT.Square).then_inc(h_sq, 1)
                    act.wait_ge(h_ss, hd + 1)
                    act.activation(hrs[:, :], hss[:, :], ACT.Sqrt, scale=1.0 / P, bias=EPS * P).then_inc(h_sq, 1)
                if j == 11:
                    act.wait_ge(h_step, s + 1)
                    act.activation(QH[:, hd, :], pair(s % 2), ACT.Copy, scale=hnw[:, 0:1]).then_inc(h_act_out, 1)

            for what, n in SCHEDULE:
                evacuate(n) if what == "group" else step(n)

            def put_pt(a):
                w = (a % 8 + 1) * P
                act.wait_ge(tr_done, a + 1)
                if a >= 2:
                    act.wait_ge(pv_done, a - 1)
                act.activation(PT[a % 2][:, 0:w], pair(2)[:, 0:w], ACT.Copy).then_inc(att_pt, 1)

            for a in range(ITEMS_A):
                w = (a % 8 + 1) * P
                act.wait_ge(att_m, a + 1)
                act.activation(SC[a % 3][:, 0:w], SC[a % 3][:, 0:w], ACT.Exp, bias=am[:, a:a + 1],
                               accum_out=az[:, a:a + 1]).then_inc(att_p, 1)
                if a >= 1:
                    put_pt(a - 1)
            put_pt(ITEMS_A - 1)

            def put_xn2T(t):
                act.wait_ge(xn2T_mm, t + 1)
                if t >= 2:
                    act.wait_ge(lg_done, t - 1)
                act.activation(xn2T[t % 2], pair(2), ACT.Copy).then_inc(xn2T_ready, 1)

            def xn2_hi_part(t):
                act.wait_ge(xn2_ready, t + 1)
                if t >= 2:
                    act.wait_ge(xn2_out[t % 2], 16 * (t // 2))
                act.activation(xn2h[t % 2].bitcast(F16)[:, 0:D], xn2[t % 2], ACT.Copy).then_inc(xn2_hi, 1)

            for t in range(TT):
                act.wait_ge(h_done, t + 1)
                if t >= 1:
                    act.wait_ge(hss_done, 2 * t)
                act.activation(hsq, H[:, t, :], ACT.Square, accum_out=ss[:, t:t + 1]).then_inc(hss_done, 1)
                act.wait_ge(hss_done, 2 * t + 1)
                act.activation(rs[:, t:t + 1], ss[:, t:t + 1], ACT.Sqrt, scale=1.0 / D, bias=EPS).then_inc(hss_done, 1)
                if t >= 1:
                    xn2_hi_part(t - 1)
                    put_xn2T(t - 1)
            xn2_hi_part(TT - 1)
            put_xn2T(TT - 1)
            act.wait_ge(gexp_in, 1)
            act.activation(gts[:, :, :], gts[:, :, :], ACT.Exp).then_inc(gexp, 1)

            def halve(i, c, quarters=range(4)):
                to, src = halved[c % 3], fresh[c % 3]
                for q in quarters:
                    if q == 0:
                        act.wait_ge(w_load[c % 3], 32 * i + 16 * (c // 3) + 16)
                        if 3 <= c <= 6:
                            act.wait_ge(gu_done, 8 * i + 2 * c - 4)
                        if c == 7:
                            act.wait_ge(dn_done, 4 * i + 2)
                    act.activation(to[:, 0, 2 * q:2 * q + 2, :], src[:, 2 * q:2 * q + 2, :], ACT.Copy, scale=WS).then_inc(hi_done, 1)

            def put_x(i, r):
                act.wait_ge(t_done, 8 * i + r + 5 if i is not None else r + 1)
                act.activation(xT[:, :, 2 * r:2 * r + 2, :], turned(r), ACT.Copy).then_inc(x_act, 1)

            act.wait_ge(op_done, TT)
            halve(0, 0)
            halve(0, 1)
            act.wait_ge(items_ready, 3)
            for r in (0, 2):
                put_x(None, r)
            act.wait_ge(dn_free, 1)
            n = act.value_load(items[0:1, 2, 0:1], min_val=NEXP, max_val=MAX_ITEMS)
            with act.Fori(0, n) as i:
                act.activation(warm[:, :], lane[:, :], ACT.Sigmoid).then_inc(warmed, 1)
                act.wait_ge(warmed, i + 1)

                def sigmoid(half, b):
                    act.wait_ge(gu_free, 8 * i + 4 * half + b + 1)
                    act.activation(sig[b], gate[b], ACT.Sigmoid, scale=ALPHA / WS).then_inc(sig_ready, 1)

                def act_half(half, b):
                    k = 4 * half + 2 * b
                    act.wait_ge(act_f, 4 * i + 2 * half + b + 1)
                    act.activation(actT[:, 0, k:k + 2, :], actf[b], ACT.Copy).then_inc(act_hi, 1)

                def put_o(q):
                    act.wait_ge(dn_done, 4 * i + q + 1)
                    for f in range(2):
                        act.activation(oT[:, 2 * q + f, :], PS[:, 4 + q % 2, CAP * f:CAP * (f + 1)], ACT.Identity,
                                       bias=bcur[:, 16 + 2 * q + f:17 + 2 * q + f], scale=1.0 / WS).then_inc(dn_free, 1)

                halve(i, 2)
                sigmoid(0, 0)
                halve(i, 3, (0, 1))
                sigmoid(0, 1)
                halve(i, 3, (2, 3))
                act_half(0, 0)
                halve(i, 4, (0, 1))
                act_half(0, 1)
                halve(i, 4, (2, 3))
                sigmoid(1, 0)
                halve(i, 5, (0,))
                sigmoid(1, 1)
                halve(i, 5, (1, 2))
                act_half(1, 0)
                act_half(1, 1)
                for r in (0, 2):
                    put_x(i, r)
                halve(i, 5, (3,))
                halve(i, 6, (0, 1))
                put_o(0)
                halve(i, 6, (2, 3))
                put_o(1)
                halve(i, 7, (0, 1))
                put_o(2)
                halve(i, 7, (2, 3))
                put_o(3)
                act.wait_ge(dst_copied, 2 * i + 2)
                for g in range(2):
                    act.wait_ge(t_done, 8 * i + 2 * g + 9)
                    act.activation(og[:, 512 * g:512 * (g + 1)], PS[:, 6 - 4 * g, :], ACT.Copy).then_inc(o_rows, 1)
                    act.wait_ge(t_done, 8 * i + 2 * g + 10)
                    act.activation(og2[:, 512 * g:512 * (g + 1)], PS[0:32, 7 - 4 * g, :], ACT.Copy).then_inc(o_rows, 1)

            def put_rows(t):
                act.wait_ge(o_ready, t + 1)
                act.dma_start(out[0, t * P:(t + 1) * P, :], ot[t % 2]).then_inc(o_out[t % 2], 16)

            for t in range(TT):
                act.wait_ge(y_sum, t + 1)
                if t >= 1:
                    act.wait_ge(oss_done, 2 * t)
                act.activation(osq, H[:, t, :], ACT.Square, accum_out=ss[:, t:t + 1]).then_inc(oss_done, 1)
                act.wait_ge(oss_done, 2 * t + 1)
                act.activation(rs[:, t:t + 1], ss[:, t:t + 1], ACT.Sqrt, scale=1.0 / D, bias=EPS).then_inc(oss_done, 1)
                if t >= 1:
                    put_rows(t - 1)
            put_rows(TT - 1)
            for b in range(2):
                act.wait_ge(o_out[b], 16 * TT // 2)

        @block.vector
        def _(dve):
            steps = [0]

            def link(ins):
                steps[0] += 1
                ins.then_inc(dve_step, 1)
                dve.wait_ge(dve_step, steps[0])

            dve.wait_ge(consts_in, 16 * N_CONST)
            link(dve.tensor_tensor(lbt[:, 2, :], lbl[:, 0, :], lbl[:, 1, :], ALU.max))
            link(dve.tensor_tensor(lbt[:, 0, :], lbl[:, 0, :], lbt[:, 2, :], ALU.subtract))
            dve.tensor_tensor(lbt[:, 1, :], lbl[:, 1, :], lbt[:, 2, :], ALU.subtract).then_inc(lb_sub, 1)
            dve.wait_ge(lb_exp, 1)
            link(dve.tensor_tensor(lbt[:, 0, :], lbt[:, 2, :], lbt[:, 3, :], ALU.add))
            link(dve.reciprocal(lbt[:, 1, :], lbt[:, 0, :]))
            link(dve.tensor_tensor(lb[:, :], lbt[:, 2, :], lbt[:, 1, :], ALU.mult))
            link(dve.tensor_scalar(omlb[:, :], lb[:, :], -1.0, 1.0, ALU.mult, ALU.add))
            for c, (bank, at, a, b) in enumerate(((6, 0, 0, 512), (7, 0, 512, 1024), (5, 256, 1024, LROW))):
                dve.wait_ge(lrow_mm, c + 1)
                dve.tensor_tensor(lrow[:, a:b], PS[0:AH, bank, at:at + b - a], ltimes[:, a:b], ALU.add).then_inc(lrow_sum, 1)
            def win_lo_part(n):
                dve.wait_ge(win_hi, n + 1)
                q, to = n % 4, win[n // 4 % 2]
                dve.scalar_tensor_tensor(to[:, 1, 2 * q:2 * q + 2, :], quarter[n % 2], WS, to[:, 0, 2 * q:2 * q + 2, :],
                                         ALU.mult, ALU.subtract).then_inc(win_lo, 1)

            def xnT_lo_part(t):
                dve.wait_ge(xnT_hi, t + 1)
                for k in range(KD):
                    ins = dve.scalar_tensor_tensor(xnT[:, 1, k, t * P:(t + 1) * P], pair(t % 2)[:, P * k:P * (k + 1)],
                                                   nmw[:, k:k + 1], xnT[:, 0, k, t * P:(t + 1) * P], ALU.mult, ALU.subtract)
                ins.then_inc(xnT_ready, 1)

            for t in range(TT):
                dve.wait_ge(ss_done, 2 * t + 2)
                link(dve.reciprocal(rs[:, t:t + 1], rs[:, t:t + 1]))
                dve.tensor_scalar(xt[t % 2], xt[t % 2], rs[:, t:t + 1], None, ALU.mult).then_inc(xs_ready, 1)
                if t >= 1:
                    xnT_lo_part(t - 1)
                win_lo_part(t)
            xnT_lo_part(TT - 1)

            def halves(ap, m):
                h = 64 >> m
                v = ap.rearrange("p (n two h) -> p n two h", two=2, h=h)
                return v[:, :, 0, :], v[:, :, 1, :], v[:, :, 0, h - 1:h].to_broadcast([P, S // (2 * h), h])

            Cb = C.rearrange("p (b t) -> p b t", b=TT)

            def difference(hd, m):
                d = DE[m % 2]
                if m < LEVELS:
                    left, right, mid = halves(C, m)
                    dl_, dr_, _ = halves(d, m)
                    link(dve.tensor_tensor(dl_, mid, left, ALU.subtract))
                    dve.tensor_tensor(dr_, right, mid, ALU.subtract).then_inc(h_d, 1)
                else:
                    dve.tensor_tensor(d.rearrange("p (b t) -> p b t", b=TT), Cb[:, :, P - 1:P].to_broadcast([P, TT, P]), Cb,
                                      ALU.subtract).then_inc(h_d, 1)

            def scaled(hd, m):
                if m < 8:
                    dve.wait_ge(h_e, 10 * hd + m + 1)
                    if m >= 2:
                        dve.wait_ge(h_step, STEPS * hd + m)
                    elif hd:
                        dve.wait_ge(h_step, STEPS * (hd - 1) + (9 if m == 0 else 11))
                if m < LEVELS:
                    el, er, _ = halves(DE[m % 2], m)
                    xl, xr, _ = halves(X[m % 2], m)
                    kl, _, _ = halves(FH[:, hd, :], m)
                    _, qr, _ = halves(QH[:, hd, :], m)
                    link(dve.tensor_tensor(xl, el, kl, ALU.mult))
                    dve.tensor_tensor(xr, er, qr, ALU.mult).then_inc(h_x, 1)
                elif m == 7:
                    dve.tensor_tensor(X[1], DE[1], FH[:, hd, :], ALU.mult).then_inc(h_x, 1)
                else:
                    dve.wait_ge(h_e, 10 * hd + 10)
                    dve.tensor_tensor(QD, DE[0], QH[:, hd, :], ALU.mult).then_inc(h_x, 1)

            def head_start(hd):
                link(dve.tensor_scalar(FH[:, hd, :], FH[:, hd, :], omlb[:, hd:hd + 1], lb[:, hd:hd + 1], ALU.mult, ALU.add))
                dve.tensor_copy(lbt[:, 0, :], lb[:, :]).then_inc(h_f, 1)
                dve.wait_ge(h_g, hd + 1)
                dve.tensor_scalar(FH[:, hd, :], FH[:, hd, :], -1.0, 1.0, ALU.mult, ALU.add).then_inc(h_k, 1)
                for b in range(TT):
                    ins = dve.tensor_tensor_scan(Cb[:, b, :], ones[:, :], DE[0][:, b * P:(b + 1) * P], 0.0, ALU.mult, ALU.add)
                ins.then_inc(h_d, 1)
                dve.wait_ge(h_d, 9 * hd + 1)
                difference(hd, 0)
                difference(hd, 1)
                scaled(hd, 0)

            def step(s):
                hd, j = divmod(s, STEPS)
                if s == 0:
                    dve.wait_ge(proj_out, 16)
                    dve.wait_ge(ones_set, 2)
                    head_start(0)
                if 1 <= j <= 7:
                    dve.wait_ge(h_x, 9 * hd + j)
                    if j + 1 <= 7:
                        difference(hd, j + 1)
                    scaled(hd, j)
                    if j == 7:
                        scaled(hd, 8)
                if j <= 7:
                    dve.wait_ge(h_step, s + 1)
                    to = A.rearrange("p (b t) -> p b t", b=TT)
                    src = pair(s % 2).rearrange("p (b t) -> p b t", b=TT)
                    if j == 0:
                        ins = dve.tensor_tensor(to, src, ident[:, :].unsqueeze(1).to_broadcast([P, TT, P]), ALU.mult)
                    else:
                        dve.wait_ge(h_dve_out, 10 * hd + j)
                        ins = dve.copy_predicated(to, masks[:, j - 1, :].unsqueeze(1).to_broadcast([P, TT, P]), src)
                    ins.then_inc(h_dve_out, 1)
                if j == 8 and hd + 1 < GH_N:
                    dve.wait_ge(h_x, 9 * hd + 9)
                    head_start(hd + 1)
                if j == 9:
                    dve.wait_ge(h_step, s + 1)
                    dve.wait_ge(h_e, 10 * hd + 9)
                    sa = SA.rearrange("p (b v) -> p b v", b=TT)
                    su = pair(s % 2).rearrange("p (b v) -> p b v", b=TT)
                    link(dve.tensor_copy(sa[:, 1, :], su[:, 0, :]))
                    for b in range(1, TT - 1):
                        ins = dve.scalar_tensor_tensor(sa[:, b + 1, :], sa[:, b, :], dl[:, b:b + 1], su[:, b, :], ALU.mult, ALU.add)
                        if b < TT - 2:
                            link(ins)
                    ins.then_inc(h_dve_out, 1)
                if j == 10:
                    dve.wait_ge(h_sq, 2 * hd + 1)
                    dve.tensor_reduce(hss[:, :], A.rearrange("p (b v) -> p b v", b=TT), AX_X, ALU.add).then_inc(h_ss, 1)
                    dve.wait_ge(h_sq, 2 * hd + 2)
                    link(dve.reciprocal(hrs[:, :], hrs[:, :]))
                    o = KT.rearrange("p (b v) -> p b v", b=TT)
                    link(dve.tensor_tensor(o, pair(s % 2).rearrange("p (b v) -> p b v", b=TT),
                                           hrs[:, :].unsqueeze(2).to_broadcast([P, TT, P]), ALU.mult))
                    dve.tensor_tensor(o, o, GH[:, :, P * hd:P * (hd + 1)], ALU.mult).then_inc(h_dve_out, 1)

            for what, n in SCHEDULE:
                if what == "group":
                    for m in quarters_at(n):
                        win_lo_part(m)
                if what == "step":
                    if n % STEPS == 10:
                        dve.wait_ge(proj_out, 32)
                    step(n)

            def normalise(a):
                w = (a % 8 + 1) * P
                dve.wait_ge(att_p, a + 1)
                link(dve.reciprocal(az[:, a:a + 1], az[:, a:a + 1]))
                dve.tensor_scalar(SC[a % 3][:, 0:w], SC[a % 3][:, 0:w], az[:, a:a + 1], None, ALU.mult).then_inc(att_n, 1)

            def put_o(quad):
                h, at, b0 = quad // 2, 512 * (quad % 2), HD * ((quad // 2) % 2)
                dve.wait_ge(pv_done, 4 * quad + 4)
                dve.tensor_copy(QA[b0:b0 + HD, h // 2, at:at + 512], PS[b0:b0 + HD, 6 + quad % 2, :]).then_inc(att_o, 1)

            for a in range(ITEMS_A + 2):
                h, n = divmod(a, 8)
                w = (n + 1) * P
                if a < ITEMS_A:
                    dve.wait_ge(qk_done, a + 1)
                    dve.wait_ge(bt_in[h % 2], 16 * (h // 2 + 1))
                    if a >= 3:
                        dve.wait_ge(tr_done, a - 2)
                    link(dve.tensor_tensor_reduce(SC[a % 3][:, 0:w], pair(a % 2)[:, 0:w], BT[h % 2][:, S - w:S], 1.0, -3e38,
                                                  ALU.add, ALU.max, am[:, a:a + 1]))
                    dve.tensor_scalar(am[:, a:a + 1], am[:, a:a + 1], -1.0, None, ALU.mult).then_inc(att_m, 1)
                if 1 <= a <= ITEMS_A:
                    normalise(a - 1)
                if a % 4 == 1 and a >= 5:
                    put_o((a - 5) // 4)

            dve.wait_ge(h_in, 16)
            dve.wait_ge(w2b_in, 16)

            def norm_rows(t):
                dve.wait_ge(hss_done, 2 * t + 2)
                link(dve.reciprocal(rs[:, t:t + 1], rs[:, t:t + 1]))
                if t >= 2:
                    dve.wait_ge(xn2T_mm, t - 1)
                dve.scalar_tensor_tensor(xn2[t % 2], H[:, t, :], rs[:, t:t + 1], w2b, ALU.mult, ALU.mult).then_inc(xn2_ready, 1)

            def lo_part(t):
                dve.wait_ge(xn2_hi, t + 1)
                xh = xn2h[t % 2].bitcast(F16)
                dve.tensor_tensor(xh[:, D:2 * D], xn2[t % 2], xh[:, 0:D], ALU.subtract).then_inc(xn2_lo, 1)

            for t in range(TT):
                dve.wait_ge(op_done, t + 1)
                dve.tensor_tensor(H[:, t, :], pair(t % 2), H[:, t, :], ALU.add).then_inc(h_done, 1)
                if t >= 1:
                    norm_rows(t - 1)
                if t >= 2:
                    lo_part(t - 2)
            norm_rows(TT - 1)
            lo_part(TT - 2)
            lo_part(TT - 1)

            dve.wait_ge(lg_done, TT)
            link(dve.tensor_tensor(lg[:, :, :], PS[:, 6, 0:TT * NEXP].rearrange("p (t e) -> p t e", t=TT),
                                   rb[:, :].unsqueeze(1).to_broadcast([P, TT, NEXP]), ALU.add))
            for t in range(TT):
                link(dve.max(vals[:, t, :], lg[:, t, :]))
                link(dve.max_index(idx[:, t, :], vals[:, t, :], lg[:, t, :]))
            link(dve.tensor_copy(idxf[:, :, :], idx[:, :, :]))
            dve.tensor_tensor(gts[:, :, :], vals[:, :, 0:TOPK], vals[:, :, 0:1].to_broadcast([P, TT, TOPK]),
                              ALU.subtract).then_inc(gexp_in, 1)
            for k in range(TOPK):
                link(dve.tensor_tensor(oh[:, k], experts[:, :].unsqueeze(1).to_broadcast([P, TT, NEXP]),
                                       idxf[:, :, k:k + 1].to_broadcast([P, TT, NEXP]), ALU.is_equal))
            link(dve.tensor_tensor(mask[:, :, :], oh[:, 0], oh[:, 1], ALU.add))
            link(dve.tensor_tensor(mask[:, :, :], mask[:, :, :], oh[:, 2], ALU.add))
            link(dve.tensor_tensor(mask[:, :, :], mask[:, :, :], oh[:, 3], ALU.add))
            link(dve.tensor_copy(macc[:, 0, :], mask[:, 0, :]))
            for t in range(1, TT):
                ins = dve.tensor_tensor(macc[:, t, :], macc[:, t - 1, :], mask[:, t, :], ALU.add)
                if t < TT - 1:
                    link(ins)
            ins.then_inc(mask_ready, 1)
            dve.wait_ge(rank_done, 1)
            link(dve.tensor_copy(rk[:, :, :], PS[:, 7, 0:TT * NEXP].rearrange("p (t e) -> p t e", t=TT)))
            for k in range(TOPK):
                link(dve.tensor_tensor(oh[:, k], oh[:, k], rk[:, :, :], ALU.mult))
                link(dve.tensor_reduce(rkk[:, k, :], oh[:, k], AX_X, ALU.add))
                dve.scalar_tensor_tensor(slots[:, :].rearrange("p (t k) -> p t k", k=TOPK)[:, :, k], idxf[:, :, k], float(STRIDE),
                                         rkk[:, k, :], ALU.mult, ALU.add).then_inc(slots_ready, 1)
            counts = PS[:, 7, TT * NEXP:TT * NEXP + NEXP]
            fl = flags[:, :].rearrange("p (e r) -> p e r", r=ROUNDS)
            link(dve.tensor_copy(rk[:, 0, :], counts))
            link(dve.tensor_tensor(fl, rk[:, 0, :].unsqueeze(2).to_broadcast([P, NEXP, ROUNDS]),
                                   pairs[:, 0, :].rearrange("p (e r) -> p e r", r=ROUNDS), ALU.is_gt))
            link(dve.memset(picked[:, :], 1.0))
            link(dve.tensor_tensor_scan(posn[:, :], picked[:, :], flags[:, :], 0.0, ALU.mult, ALU.add))
            link(dve.tensor_copy(icol[:, 2:3], posn[:, PAIRS - 1:PAIRS]))
            link(dve.tensor_tensor(posn[:, :], posn[:, :], flags[:, :], ALU.subtract))
            link(dve.scalar_tensor_tensor(flags[:, :], posn[:, :], lane[:, 0:1], flags[:, :], ALU.is_equal, ALU.mult))
            for c in range(2):
                link(dve.tensor_tensor(picked[:, :], flags[:, :], pairs[:, 1 + c, :], ALU.mult))
                link(dve.tensor_reduce(icol[:, c:c + 1], picked[:, :], AX_X, ALU.add))
            dve.tensor_scalar(icol[:, 0:1], icol[:, 0:1], float(PAD_ROW), None, ALU.add).then_inc(icol_ready, 1)
            dve.wait_ge(items_mm, 1)
            for c in range(3):
                dve.tensor_copy(items[0:1, c, :], PS[0:1, 7, P * c:P * (c + 1)]).then_inc(items_ready, 1)
            dve.wait_ge(gexp, 1)
            link(dve.tensor_reduce(gsum[:, :], gts[:, :, :], AX_X, ALU.add))
            link(dve.reciprocal(gsum[:, :], gsum[:, :]))
            dve.tensor_tensor(gts[:, :, :], gts[:, :, :], gsum[:, :].unsqueeze(2).to_broadcast([P, TT, TOPK]),
                              ALU.mult).then_inc(dn_free, 1)

            def halve(i, c, quarters=range(4)):
                to, src = halved[c % 3], fresh[c % 3]
                for q in quarters:
                    dve.wait_ge(hi_done, 24 * i + 4 * c + q + 1)
                    dve.scalar_tensor_tensor(to[:, 1, 2 * q:2 * q + 2, :], src[:, 2 * q:2 * q + 2, :], WS,
                                             to[:, 0, 2 * q:2 * q + 2, :], ALU.mult, ALU.subtract).then_inc(lo_done, 1)

            def put_x(i, r):
                dve.wait_ge(t_done, 8 * i + r + 5 if i is not None else r + 1)
                dve.tensor_copy(xT[:, :, 2 * r:2 * r + 2, :], turned(r)).then_inc(x_dve, 1)

            halve(0, 0)
            halve(0, 1)
            for r in (1, 3):
                put_x(None, r)
            dve.wait_ge(items_ready, 3)
            dve.wait_ge(bias_copied, 1)
            n = dve.value_load(items[0:1, 2, 0:1], min_val=NEXP, max_val=MAX_ITEMS)
            with dve.Fori(0, n) as i:
                e = dve.value_load(items[0:1, 1, bass.ds(i, 1)], min_val=0, max_val=NEXP - 1)
                dve.wait_ge(dn_free, 8 * i + 1)
                dve.tensor_copy(bcur[:, :], biasT[:, :, bass.ds(e, 1)].rearrange("p f a -> p (f a)")).then_inc(bcur_ready, 1)
                dve.wait_ge(bcur_ready, 2 * i + 1)
                dve.tensor_scalar(bcur[:, 8:16], bcur[:, 8:16], WS, None, ALU.add).then_inc(bcur_ready, 1)
                dve.wait_ge(bcur_ready, 2 * i + 2)

                def gates(half, b):
                    dve.wait_ge(gu_done, 8 * i + 4 * half + b + 1)
                    for f in range(2):
                        k = 4 * half + 2 * b + f
                        ins = dve.tensor_scalar(gate[b][:, f, :], PS[:, b, CAP * f:CAP * (f + 1)], bcur[:, k:k + 1], WS * LIMIT,
                                                ALU.add, ALU.min)
                    ins.then_inc(gu_free, 1)

                def product(half, b):
                    dve.wait_ge(sig_ready, 4 * i + 2 * half + b + 1)
                    dve.wait_ge(gu_free, 8 * i + 4 * half + b + 1)
                    dve.scalar_tensor_tensor(sig[b], gate[b], 1.0 / (WS * WS), sig[b], ALU.mult, ALU.mult).then_inc(prod_ready, 1)

                def ups(half, b):
                    dve.wait_ge(gu_done, 8 * i + 4 * half + b + 3)
                    for f in range(2):
                        k = 8 + 4 * half + 2 * b + f
                        ins = dve.tensor_scalar(up[b][:, f, :], PS[:, 2 + b, CAP * f:CAP * (f + 1)], bcur[:, k:k + 1],
                                                WS * (LIMIT + 1.0), ALU.add, ALU.min)
                    ins.then_inc(gu_free, 1)
                    dve.wait_ge(gu_free, 8 * i + 4 * half + b + 3)
                    dve.wait_ge(prod_ready, 4 * i + 2 * half + b + 1)
                    dve.scalar_tensor_tensor(actf[b], up[b], WS * (1.0 - LIMIT), sig[b], ALU.max, ALU.mult).then_inc(act_f, 1)

                def act_rest(half, b):
                    k = 4 * half + 2 * b
                    dve.wait_ge(act_hi, 4 * i + 2 * half + b + 1)
                    dve.tensor_tensor(actT[:, 1, k:k + 2, :], actf[b], actT[:, 0, k:k + 2, :], ALU.subtract).then_inc(act_lo, 1)

                halve(i, 2, (0, 1))
                gates(0, 0)
                halve(i, 2, (2, 3))
                gates(0, 1)
                halve(i, 3, (0, 1))
                product(0, 0)
                ups(0, 0)
                halve(i, 3, (2, 3))
                product(0, 1)
                ups(0, 1)
                act_rest(0, 0)
                halve(i, 4, (0, 1))
                act_rest(0, 1)
                gates(1, 0)
                halve(i, 4, (2, 3))
                product(1, 0)
                gates(1, 1)
                halve(i, 5, (0,))
                product(1, 1)
                ups(1, 0)
                halve(i, 5, (1,))
                act_rest(1, 0)
                ups(1, 1)
                act_rest(1, 1)
                for r in (1, 3):
                    put_x(i, r)
                halve(i, 5, (2, 3))
                halve(i, 6)
                halve(i, 7)

            def norm_out(t):
                dve.wait_ge(oss_done, 2 * t + 2)
                link(dve.reciprocal(rs[:, t:t + 1], rs[:, t:t + 1]))
                if t == 0:
                    dve.wait_ge(wfb_in, 16)
                if t >= 2:
                    dve.wait_ge(o_out[t % 2], 16 * (t // 2))
                dve.scalar_tensor_tensor(ot[t % 2], H[:, t, :], rs[:, t:t + 1], wfb, ALU.mult, ALU.mult).then_inc(o_ready, 1)

            for t in range(TT):
                dve.wait_ge(y_in[t % len(yt)], 16 * (t // len(yt) + 1))
                y = yt[t % len(yt)].rearrange("p (k d) -> p k d", k=TOPK)
                for k in range(TOPK):
                    ins = dve.scalar_tensor_tensor(H[:, t, :], y[:, k, :], gts[:, t, k:k + 1], H[:, t, :], ALU.mult, ALU.add)
                    if k < TOPK - 1:
                        link(ins)
                ins.then_inc(y_sum, 1)
                if t >= 1:
                    norm_out(t - 1)
            norm_out(TT - 1)

        @block.tensor
        def _(pe):
            pe.wait_ge(consts_in, 16 * N_CONST)
            for f in range(24):
                rows = bgu_rows if f < 16 else bdn_rows
                at = P * (f % 16)
                mm = pe.transpose(pair(2)[:, NEXP * f:NEXP * (f + 1)], rows[:, at:at + P], ident[0:NEXP, 0:NEXP])
            mm.then_inc(bias_mm, 1)
            for c, (bank, at, a, b) in enumerate(((6, 0, 0, 512), (7, 0, 512, 1024), (5, 256, 1024, LROW))):
                if c == 2:
                    pe.wait_ge(bias_copied, 1)
                pe.matmul(PS[0:AH, bank, at:at + b - a], relb[:, :], onehot[:, a:b], start=True, stop=True).then_inc(lrow_mm, 1)
            for t in range(TT):
                pe.wait_ge(xs_ready, t + 1)
                if t >= 2:
                    pe.wait_ge(xnT_ready, t - 1)
                for k in range(KD):
                    mm = pe.transpose(pair(t % 2)[:, P * k:P * (k + 1)], xt[t % 2][:, P * k:P * (k + 1)], ident[:, :])
                mm.then_inc(xT_mm, 1)

            def project(g):
                c = g // 4
                kind, part = CHUNKS[c]
                w = win[c % 2]
                bank = PS[:, 6 + g % 2, :]
                if g % 4 == 0:
                    pe.wait_ge(win_lo, 4 * c + 4)
                if g == 0:
                    pe.wait_ge(xnT_ready, TT)
                    pe.wait_ge(lrow_sum, 3)
                if g >= 2:
                    pe.wait_ge(proj_out, g - 1)
                passes = [(k, a, b) for k in range(KD) for a, b in ((0, 0), (0, 1), (1, 0))]
                last = len(passes) - 1
                if kind in ("fh", "qh", "qa", "ka"):
                    ft, half = divmod(g % 4, 2)
                    for n, (k, a, b) in enumerate(passes):
                        mm = pe.matmul(bank, w[:, a, k, P * ft:P * (ft + 1)], xnT[:, b, k, 512 * half:512 * half + 512],
                                       start=(n == 0), stop=(n == last))
                else:
                    for tt in range(2):
                        t = 2 * (g % 4) + tt
                        for n, (k, a, b) in enumerate(passes):
                            mm = pe.matmul(bank[:, 256 * tt:256 * tt + 256], xnT[:, b, k, t * P:(t + 1) * P], w[:, a, k, :],
                                           start=(n == 0), stop=(n == last))
                mm.then_inc(proj_done, 1)

            def step(s):
                hd, j = divmod(s, STEPS)
                to = pair(s % 2)
                if s >= 2:
                    ph, pj = divmod(s - 2, STEPS)
                    if pj in (8, 11):
                        pe.wait_ge(h_act_out, 2 * ph + (1 if pj == 8 else 2))
                    else:
                        pe.wait_ge(h_dve_out, 10 * ph + {9: 9, 10: 10}.get(pj, pj + 1))
                if j == 0:
                    pe.wait_ge(h_k, hd + 1)
                    ops = [(b, [(FH[:, hd, P * b:P * (b + 1)], QH[:, hd, P * b:P * (b + 1)])]) for b in range(TT)]
                elif j <= 7:
                    pe.wait_ge(h_x, 9 * hd + j)
                    xx = X[(j - 1) % 2]
                    ops = [(b, [(xx[:, P * b:P * (b + 1)], xx[:, P * b:P * (b + 1)])]) for b in range(TT)]
                elif j == 8:
                    pe.wait_ge(h_x, 9 * hd + 8)
                    for b in range(TT):
                        mm = pe.transpose(to[:, P * b:P * (b + 1)], X[1][:, P * b:P * (b + 1)], ident[:, :])
                    ops = []
                elif j == 9:
                    pe.wait_ge(h_act_out, 2 * hd + 1)
                    pe.wait_ge(proj_out, 24)
                    ops = [(b, [(KT[:, P * b:P * (b + 1)], IH[:, b, P * hd:P * (hd + 1)])]) for b in range(TT)]
                elif j == 10:
                    pe.wait_ge(h_dve_out, 10 * hd + 9)
                    pe.wait_ge(h_x, 9 * hd + 9)
                    ops = [(b, [(A[:, P * b:P * (b + 1)], IH[:, b, P * hd:P * (hd + 1)])]
                            + ([(QD[:, P * b:P * (b + 1)], SA[:, P * b:P * (b + 1)])] if b else [])) for b in range(TT)]
                else:
                    pe.wait_ge(h_dve_out, 10 * hd + 10)
                    for b in range(TT):
                        mm = pe.transpose(to[:, P * b:P * (b + 1)], KT[:, P * b:P * (b + 1)], ident[:, :])
                    ops = []
                for b, products in ops:
                    for m, (lhs, rhs) in enumerate(products):
                        mm = pe.matmul(to[:, P * b:P * (b + 1)], lhs, rhs, start=(m == 0), stop=(m == len(products) - 1))
                mm.then_inc(h_step, 1)

            for what, n in SCHEDULE:
                project(n) if what == "group" else step(n)

            def scores(a):
                h, n = divmod(a, 8)
                b0 = HD * (h % 2)
                if a >= 2:
                    pe.wait_ge(att_m, a - 1)
                w = (n + 1) * P
                for at in range(0, w, 512):
                    end = min(w, at + 512)
                    mm = pe.matmul(pair(a % 2)[:, at:end], QA[b0:b0 + HD, h // 2, n * P:(n + 1) * P], KA[b0:b0 + HD, h // 2, at:end],
                                   start=True, stop=True)
                mm.then_inc(qk_done, 1)

            def transposes(a):
                pe.wait_ge(att_n, a + 1)
                if a >= 1:
                    pe.wait_ge(att_pt, a)
                for b in range(a % 8 + 1):
                    mm = pe.transpose(pair(2)[:, P * b:P * (b + 1)], SC[a % 3][:, P * b:P * (b + 1)], ident[:, :])
                mm.then_inc(tr_done, 1)

            def values(a):
                h, n = divmod(a, 8)
                b0 = HD * (h % 2)
                quad = a // 4
                pe.wait_ge(att_pt, a + 1)
                if a % 4 == 0 and quad >= 2:
                    pe.wait_ge(att_o, quad - 1)
                for b in range(n + 1):
                    mm = pe.matmul(PS[b0:b0 + HD, 6 + quad % 2, P * (a % 4):P * (a % 4 + 1)], VA[:, b, HD * h:HD * (h + 1)],
                                   PT[a % 2][:, P * b:P * (b + 1)], start=(b == 0), stop=(b == n))
                mm.then_inc(pv_done, 1)

            pe.wait_ge(proj_out, GROUPS)
            pe.wait_ge(h_act_out, 2 * GH_N)
            pe.wait_ge(h_dve_out, 10 * GH_N)
            scores(0)
            scores(1)
            for a in range(ITEMS_A):
                if a + 2 < ITEMS_A:
                    scores(a + 2)
                transposes(a)
                if a >= 1:
                    values(a - 1)
            values(ITEMS_A - 1)

            pe.wait_ge(att_o, ITEMS_A // 4)
            pe.wait_ge(wout_in, 32)

            def out_rows(t):
                if t >= 2:
                    pe.wait_ge(h_done, t - 1)
                for half in range(2):
                    for k in range(KD):
                        mix = QA if k < 4 else QH
                        mm = pe.matmul(pair(t % 2)[:, 512 * half:512 * (half + 1)], mix[:, k % 4, t * P:(t + 1) * P],
                                       wout[k // 4][:, k % 4, 512 * half:512 * (half + 1)], start=(k == 0), stop=(k == KD - 1))
                mm.then_inc(op_done, 1)

            def route(t):
                pe.wait_ge(xn2_ready, t + 1)
                if t >= 1:
                    pe.wait_ge(xn2T_ready, t)
                for k in range(KD):
                    mm = pe.transpose(pair(2)[:, P * k:P * (k + 1)], xn2[t % 2][:, P * k:P * (k + 1)], ident[:, :])
                mm.then_inc(xn2T_mm, 1)

            def logits(t):
                pe.wait_ge(xn2T_ready, t + 1)
                for k in range(KD):
                    mm = pe.matmul(PS[:, 6, NEXP * t:NEXP * (t + 1)], xn2T[t % 2][:, P * k:P * (k + 1)], rw[:, k, :],
                                   start=(k == 0), stop=(k == KD - 1))
                mm.then_inc(lg_done, 1)

            for t in range(TT + 2):
                if t < TT:
                    out_rows(t)
                if t >= 2:
                    logits(t - 2)
                if 1 <= t <= TT:
                    route(t - 1)
            pe.wait_ge(ones_set, 1)
            pe.wait_ge(mask_ready, 1)
            for t in range(TT):
                to = PS[:, 7, NEXP * t:NEXP * (t + 1)]
                pe.matmul(to, before[:, :], mask[:, t, :], start=True, stop=(t == 0))
                if t:
                    pe.matmul(to, ones[:, :], macc[:, t - 1, :], start=False, stop=True)
            pe.matmul(PS[:, 7, TT * NEXP:TT * NEXP + NEXP], ones[:, :], macc[:, TT - 1, :], start=True, stop=True).then_inc(rank_done, 1)
            pe.wait_ge(icol_ready, 1)
            for c in range(3):
                mm = pe.matmul(PS[0:1, 7, P * c:P * (c + 1)], icol[:, c:c + 1], ident[:, :], start=True, stop=True)
            mm.then_inc(items_mm, 1)

            def turn_x(r):
                to = turned(r)
                for k in range(2):
                    at = P * (2 * r + k)
                    for m in range(2):
                        pe.transpose(to[:, m, k, 0:P], xgh[:, m, at:at + P], ident16[:, :])
                        mm = pe.transpose(to[:, m, k, P:CAP], xgh2[:, m, at:at + P], ident16[0:32, 0:32])
                mm.then_inc(t_done, 1)

            def three(to, w, cols, moving, tiles=range(KD)):
                for k in tiles:
                    for m, (a, b) in enumerate(((0, 0), (0, 1), (1, 0))):
                        mm = pe.matmul(to, w[:, a, k, cols:cols + P], moving[:, b, k, :],
                                       start=(k == 0 and m == 0), stop=(k == KD - 1 and m == 2))
                return mm

            pe.wait_ge(items_ready, 3)
            pe.wait_ge(xg_in, 32)
            pe.wait_ge(ones_set, 3)
            for r in range(4):
                turn_x(r)
            n = pe.value_load(items[0:1, 2, 0:1], min_val=NEXP, max_val=MAX_ITEMS)
            with pe.Fori(0, n) as i:
                for c in range(4):
                    pe.wait_ge(hi_done, 24 * i + 4 * c + 4)
                    pe.wait_ge(lo_done, 24 * i + 4 * c + 4)
                    if c == 0:
                        pe.wait_ge(x_act, 2 * i + 2)
                        pe.wait_ge(x_dve, 2 * i + 2)
                    if c == 1:
                        pe.wait_ge(o_rows, 4 * i + 1)
                    for b in range(2):
                        if c >= 2:
                            pe.wait_ge(gu_free, 8 * i + 2 * c + b - 3)
                        for f in range(2):
                            mm = three(PS[:, 2 * (c % 2) + b, CAP * f:CAP * (f + 1)], halved[c % 3], P * (2 * b + f), xT)
                        if b == 0:
                            mm.then_inc(gu_done, 1)
                    mm.then_inc(gu_done, 1)
                pe.wait_ge(xg_in, 32 * i + 64)
                pe.wait_ge(gu_free, 8 * i + 6)
                for r in range(4):
                    turn_x(r)
                def down(q, f, parts=range(4)):
                    for part in parts:
                        mm = three(PS[:, 4 + q % 2, CAP * f:CAP * (f + 1)], halved[1 + q // 2], P * (2 * (q % 2) + f), actT,
                                   (2 * part, 2 * part + 1))
                    return mm

                pe.wait_ge(hi_done, 24 * i + 20)
                pe.wait_ge(lo_done, 24 * i + 20)
                pe.wait_ge(act_lo, 4 * i + 3)
                for q in range(2):
                    down(q, 0, range(3))
                pe.wait_ge(act_lo, 4 * i + 4)
                for q in range(2):
                    down(q, 0, (3,))
                for q in range(2):
                    down(q, 1).then_inc(dn_done, 1)
                pe.wait_ge(hi_done, 24 * i + 24)
                pe.wait_ge(lo_done, 24 * i + 24)
                for q in range(2, 4):
                    pe.wait_ge(dn_free, 8 * i + 2 * q - 1)
                    down(q, 0)
                    down(q, 1).then_inc(dn_done, 1)
                for g in range(2):
                    pe.wait_ge(dn_free, 8 * i + 4 * g + 5)
                    pe.wait_ge(*((x_act, 2 * i + 3) if g == 0 else (gu_free, 8 * i + 8)))
                    for k in range(4):
                        mm = pe.transpose(PS[:, 6 - 4 * g, P * k:P * (k + 1)], oT[:, 4 * g + k, 0:P], ident[:, :])
                    mm.then_inc(t_done, 1)
                    if g == 0:
                        pe.wait_ge(x_dve, 2 * i + 3)
                    for k in range(4):
                        mm = pe.transpose(PS[0:32, 7 - 4 * g, P * k:P * (k + 1)], oT[:, 4 * g + k, P:CAP], ident[:, :])
                    mm.then_inc(t_done, 1)


_INS = ["x", "norm_mix_w", "w_in", "rel_bias", "hgrn_lb_logits", "hgrn_norm_w", "w_out", "norm_ffn_w", "router_w",
        "router_b", "w_gate_up", "b_gate_up", "w_down", "b_down", "final_norm_w"]


def kernel(**inputs):
    import numpy as _np
    import concourse.bacc as _bacc
    from concourse import mybir as _mybir
    from concourse.bass_utils import run_bass_kernel_spmd as _run

    nc = _bacc.Bacc("TRN2", target_bir_lowering=False, num_devices=1)
    arrays, args = {}, {}
    both = [(name, inputs[name]) for name in _INS] + list(constant_arrays().items())
    for name, a in both:
        a = _np.ascontiguousarray(a)
        arrays[f"in_{name}"] = a
        args[name] = nc.dram_tensor(f"in_{name}", a.shape, _mybir.dt.from_np(a.dtype), kind="ExternalInput").ap()
    out = nc.dram_tensor("out_0", (1, S, D), F32, kind="ExternalOutput").ap()
    build(nc, out=out, **args)
    r = _run(nc, [arrays], core_ids=[0])
    return r.results[0]["out_0"]
```
